# Optimizing a Trainium2 kernel written in Bass

```python
import math
import jax, jax.numpy as jnp
from jax import lax
import numpy as np

D_MODEL = 1024
BATCH = 1
SEQ = 512
DEPTH = 2

HEAD_DIM = 64
BLOCK = 128
EPS = 1e-6
NEG = -1e30
A_HEADS = 4
A_QK_DIM = 2 * HEAD_DIM
A_V_DIM = 2 * HEAD_DIM
B_HEADS = 8
B_KV_HEADS = 2
B_HALF_WINDOW = 128
C_PATTERNS = ((128, 1), (512, 4), (2048, 16))
C_HEADS_PER_GROUP = 4
C_HEADS = C_HEADS_PER_GROUP * len(C_PATTERNS)
D_HEADS = 12
D_Q_LORA = 384
D_KV_LORA = 256
D_NOPE = 64
D_ROPE = 32
D_V = 64
ROPE_THETA = 10000.0
NUM_BUCKETS = 32
MAX_DISTANCE = 1024
N_BIAS_HEADS = A_HEADS + B_HEADS
D_FF = -(-8 * D_MODEL // (3 * 256)) * 256
AB_IN = A_HEADS * (2 * A_QK_DIM + A_V_DIM) + (B_HEADS + 2 * B_KV_HEADS) * HEAD_DIM
AB_OUT = A_HEADS * A_V_DIM + B_HEADS * HEAD_DIM
CD_IN = 3 * C_HEADS * HEAD_DIM + D_Q_LORA + D_KV_LORA + D_ROPE
CD_OUT = C_HEADS_PER_GROUP * HEAD_DIM + D_HEADS * D_V

kernel_name = 'hybrid_diff_swa_dilated_mla_encoder'

def rmsnorm(x, g):
    xf = x.astype(jnp.float32)
    y = xf * lax.rsqrt(jnp.mean(xf * xf, axis=-1, keepdims=True) + EPS)
    return (y * g.astype(jnp.float32)).astype(x.dtype)

def t5_bucket(rel):
    nb = NUM_BUCKETS // 2
    max_exact = nb // 2
    ret = jnp.where(rel > 0, nb, 0)
    n = jnp.abs(rel)
    nf = jnp.maximum(n, 1).astype(jnp.float32)
    large = max_exact + (jnp.log(nf / max_exact) / math.log(MAX_DISTANCE / max_exact)
                         * (nb - max_exact)).astype(jnp.int32)
    large = jnp.minimum(large, nb - 1)
    return ret + jnp.where(n < max_exact, n, large)

def heads(t, n):
    B, S, _ = t.shape
    return t.reshape(B, S, n, -1).transpose(0, 2, 1, 3)

def merge_heads(t):
    B, n, S, d = t.shape
    return t.transpose(0, 2, 1, 3).reshape(B, S, n * d)

def rope(t, pos):
    half = D_ROPE // 2
    inv = ROPE_THETA ** (-jnp.arange(half, dtype=jnp.float32) / half)
    ang = pos.astype(jnp.float32)[:, None] * inv[None, :]
    cos, sin = jnp.cos(ang)[:, None, :], jnp.sin(ang)[:, None, :]
    tf = t.astype(jnp.float32)
    t1, t2 = tf[..., :half], tf[..., half:]
    return jnp.concatenate([t1 * cos - t2 * sin, t2 * cos + t1 * sin], axis=-1).astype(t.dtype)

def diff_attention(q1, q2, k1, k2, v, lam, bias_tab):
    B, H, S, d = q1.shape
    scale = d ** -0.5
    kpos = jnp.arange(S)

    def block(b):
        qs = b * BLOCK
        q1b = lax.dynamic_slice_in_dim(q1, qs, BLOCK, axis=2)
        q2b = lax.dynamic_slice_in_dim(q2, qs, BLOCK, axis=2)
        qpos = qs + jnp.arange(BLOCK)
        bias = bias_tab[t5_bucket(kpos[None, :] - qpos[:, None])]
        bias = bias.transpose(2, 0, 1).astype(jnp.float32)
        s1 = jnp.einsum('bhqd,bhkd->bhqk', q1b, k1).astype(jnp.float32) * scale + bias
        s2 = jnp.einsum('bhqd,bhkd->bhqk', q2b, k2).astype(jnp.float32) * scale + bias
        p = jax.nn.softmax(s1, axis=-1) - lam * jax.nn.softmax(s2, axis=-1)
        return jnp.einsum('bhqk,bhkd->bhqd', p.astype(v.dtype), v)

    out = lax.map(block, jnp.arange(S // BLOCK))
    return out.transpose(1, 2, 0, 3, 4).reshape(B, H, S, v.shape[-1])

def dense_attention(q, k, v, scale):
    B, H, S, _ = q.shape

    def block(b):
        qb = lax.dynamic_slice_in_dim(q, b * BLOCK, BLOCK, axis=2)
        s = jnp.einsum('bhqd,bhkd->bhqk', qb, k).astype(jnp.float32) * scale
        p = jax.nn.softmax(s, axis=-1).astype(v.dtype)
        return jnp.einsum('bhqk,bhkd->bhqd', p, v)

    out = lax.map(block, jnp.arange(S // BLOCK))
    return out.transpose(1, 2, 0, 3, 4).reshape(B, H, S, v.shape[-1])

def banded_attention(q, k, v, half_window, bias_tab, dilation, sink=None):
    B, H, L, dq = q.shape
    G = k.shape[1]
    rep = H // G
    dv = v.shape[-1]
    W = half_window
    nb = -(-L // BLOCK)
    Lp = nb * BLOCK
    span = BLOCK + 2 * W
    qp = jnp.pad(q, ((0, 0), (0, 0), (0, Lp - L), (0, 0)))
    kp = jnp.pad(k, ((0, 0), (0, 0), (W, Lp - L + W), (0, 0)))
    vp = jnp.pad(v, ((0, 0), (0, 0), (W, Lp - L + W), (0, 0)))
    idx = jnp.arange(nb)[:, None] * BLOCK + jnp.arange(span)[None, :]
    kb = kp[:, :, idx]
    vb = vp[:, :, idx]
    qb = qp.reshape(B, G, rep, nb, BLOCK, dq)
    s = jnp.einsum('bgrnqd,bgnkd->bgrnqk', qb, kb).astype(jnp.float32) * dq ** -0.5
    rel = jnp.arange(span)[None, :] - W - jnp.arange(BLOCK)[:, None]
    bias = bias_tab[t5_bucket(rel * dilation)].astype(jnp.float32)
    bias = bias.transpose(2, 0, 1).reshape(G, rep, 1, BLOCK, span)
    kpos = idx - W
    valid = ((jnp.abs(rel) <= W)[None]
             & (kpos >= 0)[:, None, :] & (kpos < L)[:, None, :])
    s = jnp.where(valid, s + bias, NEG)
    m = jnp.max(s, axis=-1, keepdims=True)
    if sink is not None:
        sk = sink.astype(jnp.float32).reshape(G, rep, 1, 1, 1)
        m = jnp.maximum(m, sk)
    e = jnp.exp(s - m)
    denom = jnp.sum(e, axis=-1, keepdims=True)
    if sink is not None:
        denom = denom + jnp.exp(sk - m)
    o = jnp.einsum('bgrnqk,bgnkd->bgrnqd', (e / denom).astype(v.dtype), vb)
    lse = (m + jnp.log(denom))[..., 0]
    o = o.reshape(B, H, Lp, dv)[:, :, :L]
    lse = lse.reshape(B, H, Lp)[:, :, :L]
    return o, lse

def dilated_group(q, k, v, window, dilation, bias_tab):
    B, H, S, d = q.shape
    L = S // dilation

    def to_strided(t):
        return t.reshape(B, H, L, dilation, d).transpose(0, 3, 1, 2, 4).reshape(B * dilation, H, L, d)

    o, lse = banded_attention(to_strided(q), to_strided(k), to_strided(v),
                              window // (2 * dilation), bias_tab, dilation)
    o = o.reshape(B, dilation, H, L, d).transpose(0, 2, 3, 1, 4).reshape(B, H, S, d)
    lse = lse.reshape(B, dilation, H, L).transpose(0, 2, 3, 1).reshape(B, H, S)
    return o, lse

def mixer_ab(h, w_in, lam_q1, lam_k1, lam_q2, lam_k2, subln, sink, w_o, bias_table, lambda_init):
    proj = h @ w_in
    o1 = A_HEADS * A_QK_DIM
    o2 = o1 + A_HEADS * A_QK_DIM
    o3 = o2 + A_HEADS * A_V_DIM
    o4 = o3 + B_HEADS * HEAD_DIM
    o5 = o4 + B_KV_HEADS * HEAD_DIM
    qa = heads(proj[..., :o1], A_HEADS)
    ka = heads(proj[..., o1:o2], A_HEADS)
    va = heads(proj[..., o2:o3], A_HEADS)
    lam = (jnp.exp(jnp.sum(lam_q1.astype(jnp.float32) * lam_k1.astype(jnp.float32)))
           - jnp.exp(jnp.sum(lam_q2.astype(jnp.float32) * lam_k2.astype(jnp.float32)))
           + lambda_init)
    oa = diff_attention(qa[..., :HEAD_DIM], qa[..., HEAD_DIM:], ka[..., :HEAD_DIM], ka[..., HEAD_DIM:],
                        va, lam, bias_table[:, :A_HEADS])
    oa = rmsnorm(oa, subln) * (1.0 - lambda_init)
    qb = heads(proj[..., o3:o4], B_HEADS)
    kb = heads(proj[..., o4:o5], B_KV_HEADS)
    vb = heads(proj[..., o5:], B_KV_HEADS)
    ob, _ = banded_attention(qb, kb, vb, B_HALF_WINDOW, bias_table[:, A_HEADS:A_HEADS + B_HEADS], 1, sink)
    return jnp.concatenate([merge_heads(oa), merge_heads(ob)], axis=-1) @ w_o

def mixer_cd(h, w_in, q_norm, w_q_b, kv_norm, w_kv_b, w_o, bias_table, pos):
    B, S, _ = h.shape
    proj = h @ w_in
    cw = C_HEADS * HEAD_DIM
    o1, o2, o3 = cw, 2 * cw, 3 * cw
    o4 = o3 + D_Q_LORA
    o5 = o4 + D_KV_LORA
    qc = heads(proj[..., :o1], C_HEADS)
    kc = heads(proj[..., o1:o2], C_HEADS)
    vc = heads(proj[..., o2:o3], C_HEADS)
    outs, lses = [], []
    for g, (window, dilation) in enumerate(C_PATTERNS):
        sl = slice(g * C_HEADS_PER_GROUP, (g + 1) * C_HEADS_PER_GROUP)
        o_g, lse_g = dilated_group(qc[:, sl], kc[:, sl], vc[:, sl], window, dilation, bias_table[:, sl])
        outs.append(o_g)
        lses.append(lse_g)
    wts = jax.nn.softmax(jnp.stack(lses, axis=0), axis=0)
    oc = jnp.sum(wts[..., None] * jnp.stack(outs, axis=0).astype(jnp.float32), axis=0).astype(h.dtype)
    cq = rmsnorm(proj[..., o3:o4], q_norm)
    q = (cq @ w_q_b).reshape(B, S, D_HEADS, D_NOPE + D_ROPE)
    q_pe = rope(q[..., D_NOPE:], pos)
    ckv = rmsnorm(proj[..., o4:o5], kv_norm)
    kv = (ckv @ w_kv_b).reshape(B, S, D_HEADS, D_NOPE + D_V)
    k_pe = rope(proj[..., o5:].reshape(B, S, 1, D_ROPE), pos)
    qd = jnp.concatenate([q[..., :D_NOPE], q_pe], axis=-1).transpose(0, 2, 1, 3)
    kd = jnp.concatenate([kv[..., :D_NOPE], jnp.broadcast_to(k_pe, (B, S, D_HEADS, D_ROPE))],
                         axis=-1).transpose(0, 2, 1, 3)
    vd = kv[..., D_NOPE:].transpose(0, 2, 1, 3)
    od = dense_attention(qd, kd, vd, (D_NOPE + D_ROPE) ** -0.5)
    return jnp.concatenate([merge_heads(oc), merge_heads(od)], axis=-1) @ w_o

def swiglu(h, w_gate, w_up, w_down):
    return (jax.nn.silu(h @ w_gate) * (h @ w_up)) @ w_down

def setup_inputs(seed: int = 0) -> dict:
    key = jax.random.key(seed)
    ks = jax.random.split(key, 24)
    f = jnp.float32
    ne = (DEPTH + 1) // 2
    no = DEPTH // 2

    def w(k, shape, fan_in):
        return jax.random.normal(k, shape, f) * fan_in ** -0.5

    def gain(k, shape):
        return 1.0 + 0.05 * jax.random.normal(k, shape, f)

    return {
        'x': jax.random.normal(ks[0], (BATCH, SEQ, D_MODEL), f),
        'bias_table': 0.3 * jax.random.normal(ks[1], (NUM_BUCKETS, N_BIAS_HEADS), f),
        'attn_norm': gain(ks[2], (DEPTH, D_MODEL)),
        'ffn_norm': gain(ks[3], (DEPTH, D_MODEL)),
        'final_norm': gain(ks[4], (D_MODEL,)),
        'ab_w_in': w(ks[5], (ne, D_MODEL, AB_IN), D_MODEL),
        'ab_lambda_q1': 0.1 * jax.random.normal(ks[6], (ne, HEAD_DIM), f),
        'ab_lambda_k1': 0.1 * jax.random.normal(ks[7], (ne, HEAD_DIM), f),
        'ab_lambda_q2': 0.1 * jax.random.normal(ks[8], (ne, HEAD_DIM), f),
        'ab_lambda_k2': 0.1 * jax.random.normal(ks[9], (ne, HEAD_DIM), f),
        'ab_subln': gain(ks[10], (ne, A_V_DIM)),
        'ab_sink': 0.5 * jax.random.normal(ks[11], (ne, B_HEADS), f),
        'ab_w_o': w(ks[12], (ne, AB_OUT, D_MODEL), AB_OUT),
        'cd_w_in': w(ks[13], (no, D_MODEL, CD_IN), D_MODEL),
        'cd_q_norm': gain(ks[14], (no, D_Q_LORA)),
        'cd_w_q_b': w(ks[15], (no, D_Q_LORA, D_HEADS * (D_NOPE + D_ROPE)), D_Q_LORA),
        'cd_kv_norm': gain(ks[16], (no, D_KV_LORA)),
        'cd_w_kv_b': w(ks[17], (no, D_KV_LORA, D_HEADS * (D_NOPE + D_V)), D_KV_LORA),
        'cd_w_o': w(ks[18], (no, CD_OUT, D_MODEL), CD_OUT),
        'ffn_w_gate': w(ks[19], (DEPTH, D_MODEL, D_FF), D_MODEL),
        'ffn_w_up': w(ks[20], (DEPTH, D_MODEL, D_FF), D_MODEL),
        'ffn_w_down': w(ks[21], (DEPTH, D_FF, D_MODEL), D_FF),
    }

def reference(x, bias_table, attn_norm, ffn_norm, final_norm, ab_w_in, ab_lambda_q1, ab_lambda_k1,
              ab_lambda_q2, ab_lambda_k2, ab_subln, ab_sink, ab_w_o, cd_w_in, cd_q_norm, cd_w_q_b,
              cd_kv_norm, cd_w_kv_b, cd_w_o, ffn_w_gate, ffn_w_up, ffn_w_down):
    pos = jnp.arange(x.shape[1])
    h = x
    for layer in range(DEPTH):
        j = layer // 2
        hn = rmsnorm(h, attn_norm[layer])
        if layer % 2 == 0:
            lambda_init = 0.8 - 0.6 * math.exp(-0.3 * layer)
            mix = mixer_ab(hn, ab_w_in[j], ab_lambda_q1[j], ab_lambda_k1[j], ab_lambda_q2[j],
                           ab_lambda_k2[j], ab_subln[j], ab_sink[j], ab_w_o[j], bias_table, lambda_init)
        else:
            mix = mixer_cd(hn, cd_w_in[j], cd_q_norm[j], cd_w_q_b[j], cd_kv_norm[j], cd_w_kv_b[j],
                           cd_w_o[j], bias_table, pos)
        h = h + mix
        h = h + swiglu(rmsnorm(h, ffn_norm[layer]), ffn_w_gate[layer], ffn_w_up[layer], ffn_w_down[layer])
    return rmsnorm(h, final_norm)


_drawn_inputs = setup_inputs


def setup_inputs(seed=0):
    import zlib

    import numpy as np

    out = dict(_drawn_inputs(seed))
    spreads = {}
    factors = {'ab_lambda_q1': 3.417,
     'ab_lambda_k2': 8.0,
     'ab_sink': 8.0,
     'cd_q_norm': 8.0,
     'cd_kv_norm': 6.124}
    for name, (base, spread) in spreads.items():
        noise = np.random.default_rng([zlib.crc32(name.encode()), seed]).standard_normal(out[name].shape)
        drawn = base * np.exp(spread * noise) if base else spread * noise
        out[name] = __import__('jax').numpy.asarray(drawn.astype(out[name].dtype))
    for name, factor in factors.items():
        out[name] = (out[name] * factor).astype(out[name].dtype)
    return out
```

```python
import math
from contextlib import ExitStack

import numpy as np
import concourse.bass as bass
from concourse import mybir

F32 = mybir.dt.float32
F32R = mybir.dt.float32r
ALU = mybir.AluOpType
ACT = mybir.ActivationFunctionType
AX = mybir.AxisListType

P = 128
T = 512
DM = 1024
KC = DM // P
TB = T // P
D_FF = 2816
FC = D_FF // P
DOWN_HALF = FC // 2
HD = 64
EPS = 1e-6
NEG = -1e30
BIG = 3.0e38
NB = 32
NH_BIAS = 12
MAX_DISTANCE = 1024
A_HEADS, B_HEADS = 4, 8
D_HEADS, D_NOPE, D_ROPE = 12, 64, 32
QC, KVC = 3, 2
D_TILES = QC + KVC
LAMBDA_INIT = 0.8 - 0.6 * math.exp(-0.3 * 0)

A_UNITS = 3 * A_HEADS
U_KB, U_VB, U_QB = A_UNITS, A_UNITS + 1, A_UNITS + 2
N_AB = A_UNITS + 2 + 4
U_WO0 = N_AB
U_GU0 = U_WO0 + KC
U_DN0 = U_GU0 + 2 * FC
U_C = U_DN0 + 2 * KC
N_C = 18
U_LAT = U_C + N_C
N_LAT = QC + KVC + 2
U_D = U_LAT + N_LAT
U_WO1 = U_D + D_HEADS
U_GU1 = U_WO1 + KC
U_DN1 = U_GU1 + 2 * FC
U_END = U_DN1 + 2 * KC

VECS = ((1024, 1, 1 << 20, 0, 4), (512, 1, 128, 4, 8), (384, 1, 64, 0, 4), (256, 4, 64, 4, 4), (256, 4, 127, 8, 4))
VEC_CENTRE = (511, 255, 191, 127, 127)
VEC_AT = [sum(v[0] for v in VECS[:n]) for n in range(len(VECS))]
VEC_LEN = sum(v[0] for v in VECS)
REP_AT = [sum(P * v[0] * v[4] for v in VECS[:n]) for n in range(len(VECS))]
REP_LEN = sum(P * v[0] * v[4] for v in VECS)

G_ATTN0, G_FFN0, G_ATTN1, G_FFN1, G_FINAL, G_QN, G_KVN, G_SUB = 0, 8, 16, 24, 32, 40, 43, 45
G_COLS = 46

def build_program(nc, io):
    with ExitStack() as ctx:
        def sb(name, shape, dt=F32):
            return ctx.enter_context(nc.sbuf_tensor(name, shape, dt))

        def pb(name):
            return ctx.enter_context(nc.psum_tensor(name, [P, T], F32))

        def sem(name):
            return ctx.enter_context(nc.semaphore(name))

        vec_dram = nc.dram_tensor("bias_vectors", [NH_BIAS, VEC_LEN], F32, kind="Internal").ap()
        rep_dram = nc.dram_tensor("bias_rows", [REP_LEN], F32, kind="Internal").ap()

        xT = sb("xT", [P, KC, T])
        xg = sb("xg", [P, 2, KC, T], F32R)
        big = sb("big", [P, 2 * FC * T], F32R)
        raw = sb("raw", [P, 2, DOWN_HALF * P])
        w_hi = sb("w_hi", [P, 2, DOWN_HALF * P], F32R)
        w_lo = sb("w_lo", [P, 2, DOWN_HALF * P], F32R)
        rstd = sb("rstd", [P, T])
        sc = sb("sc", [P, 4, T])
        pn = sb("pn", [P, 2, T])
        tq = sb("tq", [P, 2, T + P])
        bias = sb("bias", [P, 2, 1024])
        og = sb("og", [P, 3, T])
        ident = sb("ident", [P, P])
        ones = sb("ones", [P, P])
        gains = sb("gains", [P, G_COLS])
        sub_gain = sb("sub_gain", [P, 1])
        tab = sb("tab", [NB + 1, NH_BIAS])
        sink = sb("sink", [P, B_HEADS])
        neg_sink = sb("neg_sink", [P, B_HEADS])
        lam = sb("lam", [P, 8])
        neg_half = sb("neg_half", [P, 4])
        mean_sq = sb("mean_sq", [P, 4])
        inv_rms = sb("inv_rms", [P, 4])
        neg_max = sb("neg_max", [P, 32])
        row_sum = sb("row_sum", [P, 32])
        inv_sum = sb("inv_sum", [P, 8])
        sink_exp = sb("sink_exp", [P, 8])
        masks = sb("masks", [P, TB])
        stats = sb("stats", [P, 96])
        nat = sb("nat", [P, 48])
        picked = sb("picked", [P, P])
        least = sb("least", [P, 16])
        comb_w = sb("comb_w", [P, 24])
        r_sq = sb("r_sq", [P, TB])
        mix = sb("mix", [P, T])

        oc = big[:, 0:2 * KC * T].rearrange("p (s c t) -> p s c t", s=2, c=KC)
        hid = big[:, :].rearrange("p (s c t) -> p s c t", s=2, c=FC)

        def region(at, *dims):
            n = math.prod(dims)
            names = "abcde"[:len(dims)]
            pattern = f"p ({' '.join(names)}) -> p {' '.join(names)}"
            return big[:, at:at + n].rearrange(pattern, **dict(zip(names, dims)))

        R0 = 2 * KC * T
        q_ab = region(R0, 2, 2, T)
        k_ab = region(R0 + 2048, 2, 2, T)
        v_ab = region(R0 + 4096, 2, 2, TB, P)
        pt_ab = region(R0 + 6144, 2, 2, TB, T)

        g_bank = [pb("g0"), pb("g1")]
        s_bank = [pb("s0"), pb("s1")]
        t_bank = [pb("t0"), pb("t1")]
        o_bank = pb("o_bank")
        m_bank = pb("m_bank")

        raw_loaded = [sem("raw_loaded0"), sem("raw_loaded1")]
        w_hi_done = sem("w_hi_done")
        w_lo_done = sem("w_lo_done")
        unit_done = sem("unit_done")
        x_loaded = [sem(f"x_loaded{n}") for n in range(4)]
        consts_loaded = sem("consts_loaded")
        ident_made = sem("ident_made")
        vec_mm = sem("vec_mm")
        vec_copied = sem("vec_copied")
        vec_stored = sem("vec_stored")
        rows_stored = [sem(f"rows_stored{n}") for n in range(len(VECS))]
        bias_loaded = [sem("bias_loaded0"), sem("bias_loaded1")]
        lam_step = sem("lam_step")
        lam_exp = sem("lam_exp")
        x_added = sem("x_added")
        xg_hi_done = sem("xg_hi_done")
        xg_lo_done = sem("xg_lo_done")
        sq_done = sem("sq_done")
        acc_added = sem("acc_added")
        stat_ready = sem("stat_ready")
        ms_ready = sem("ms_ready")
        inv_ready = sem("inv_ready")
        diag_ready = sem("diag_ready")
        bc_ready = sem("bc_ready")
        bc_used = sem("bc_used")
        proj_t = sem("proj_t")
        qk_hi = sem("qk_hi")
        qk_lo = sem("qk_lo")
        s_ready = sem("s_ready")
        scored = sem("scored")
        shift_ready = sem("shift_ready")
        exp_done = sem("exp_done")
        recip_done = sem("recip_done")
        part_done = sem("part_done")
        p_ready = sem("p_ready")
        t_ready = sem("t_ready")
        pt_hi = sem("pt_hi")
        t_free = sem("t_free")
        pv_done = sem("pv_done")
        o_copied = sem("o_copied")
        oc_hi = sem("oc_hi")
        oc_lo = sem("oc_lo")
        silu_done = sem("silu_done")
        silu_in = sem("silu_in")
        up_scaled = sem("up_scaled")
        h_ready = sem("h_ready")
        h_hi = sem("h_hi")
        h_lo = sem("h_lo")
        final_ready = sem("final_ready")
        select_loaded = sem("select_loaded")
        rotary_loaded = sem("rotary_loaded")
        edges_closed = sem("edges_closed")
        k_pads_zeroed = sem("k_pads_zeroed")
        comb_mm = sem("comb_mm")
        comb_step = sem("comb_step")
        comb_diff = sem("comb_diff")
        comb_exp = sem("comb_exp")
        comb_diag = sem("comb_diag")
        comb_bc = sem("comb_bc")
        mix_part = sem("mix_part")
        mix_done = sem("mix_done")
        lat_sq = sem("lat_sq")
        lat_add = sem("lat_add")
        lat_acc = sem("lat_acc")
        lat_mean = sem("lat_mean")
        kr_part = sem("kr_part")
        kpe_ready = sem("kpe_ready")
        q_done = sem("q_done")
        stored = sem("stored")

        block = ctx.enter_context(nc.Block())

        def unit_source(u):
            for name, first, last in (("w_ab", 0, U_WO0), ("w_o0", U_WO0, U_GU0), ("w_gu0", U_GU0, U_DN0),
                                      ("w_dn0", U_DN0, U_C), ("w_c", U_C, U_D), ("w_d", U_D, U_WO1),
                                      ("w_o1", U_WO1, U_GU1), ("w_gu1", U_GU1, U_DN1), ("w_dn1", U_DN1, U_END)):
                if first <= u < last:
                    return io[name], first

        def load_unit(sp, u, slot, name=None, first=None, j=None):
            if name is None:
                src, first = unit_source(u)
                at = src[u - first]
                static = True
            else:
                src = io[name]
                at = src[bass.ds(j, 1)].rearrange("a p n -> (a p) n")
                static = False
            if not static or u >= 2:
                sp.wait_ge(w_lo_done, u - 1)
            sp.dma_start(raw[:, slot, 0:src.shape[2]], at).then_inc(raw_loaded[slot], 16)

        def prep_hi(act, u, slot, tiles, half=None):
            half = u // 2 if half is None else half
            act.wait_ge(raw_loaded[slot], 16 * half + 16)
            if not isinstance(u, int) or u >= 2:
                act.wait_ge(unit_done, u - 1)
            n = tiles * P
            act.activation(w_hi[:, slot, 0:n], raw[:, slot, 0:n], ACT.Copy).then_inc(w_hi_done, 1)

        def prep_lo(pool, u, slot, tiles):
            pool.wait_ge(w_hi_done, u + 1)
            n = tiles * P
            pool.tensor_tensor(w_lo[:, slot, 0:n], raw[:, slot, 0:n], w_hi[:, slot, 0:n].bitcast(F32),
                               ALU.subtract).then_inc(w_lo_done, 1)

        def three(pe, out, l_hi, l_lo, r_hi, r_lo, first, last):
            pe.matmul(out, l_hi, r_hi, start=first, stop=False)
            pe.matmul(out, l_lo, r_hi, start=False, stop=False)
            return pe.matmul(out, l_hi, r_lo, start=False, stop=last)

        def wtile(slot, kc):
            return w_hi[:, slot, kc * P:(kc + 1) * P], w_lo[:, slot, kc * P:(kc + 1) * P]

        def pe_stat(pe, n, acc):
            if n >= 1:
                pe.wait_ge(bc_used, n)
            for b in range(TB):
                mm = pe.matmul(m_bank[:, b:b + 1], acc[:, b * P:(b + 1) * P], ones[:, 0:1], start=True, stop=True)
            mm.then_inc(stat_ready, 1)

        def dve_mean(dve, n, count):
            dve.wait_ge(stat_ready, n + 1)
            dve.tensor_scalar(mean_sq[:, :], m_bank[:, 0:TB], 1.0 / count, EPS, ALU.mult, ALU.add).then_inc(ms_ready, 1)

        def pool_root(pool, n):
            pool.wait_ge(ms_ready, n + 1)
            pool.tensor_tensor(inv_rms[:, :], mean_sq[:, :], neg_half[:, :], ALU.pow).then_inc(inv_ready, 1)

        def dve_diag(dve, n, diag):
            dve.wait_ge(inv_ready, n + 1)
            dve.tensor_tensor(diag.rearrange("p (b t) -> p b t", b=TB),
                              ident[:, :].unsqueeze(1).broadcast_to([P, TB, P]),
                              inv_rms[:, :].unsqueeze(2).broadcast_to([P, TB, P]), ALU.mult).then_inc(diag_ready, 1)

        def pe_broadcast(pe, n, diag):
            pe.wait_ge(diag_ready, n + 1)
            pe.matmul(m_bank[:, :], ones[:, :], diag, start=True, stop=True).then_inc(bc_ready, 1)

        def act_chunk(act, k, m, par, gain, with_xg=True, first_two=False):
            act.wait_ge(x_added, 8 * k + m + 1)
            if not isinstance(m, int):
                act.nop(nofuse=True)
            if with_xg:
                g = gains[:, gain + m:gain + m + 1] if isinstance(m, int) else gains[:, bass.ds(m + gain, 1)]
                x_m, hi_m = chunk(xT, m), xg_chunk(0, m)
                act.activation(hi_m, x_m, ACT.Copy, scale=g).then_inc(xg_hi_done, 1)
            if not first_two:
                act.wait_ge(acc_added, 9 * k + m)
                if not isinstance(m, int):
                    act.nop(nofuse=True)
            act.activation(tq[:, par, 0:T], chunk(xT, m), ACT.Square).then_inc(sq_done, 1)

        def chunk(t, m):
            return t[:, m, :] if isinstance(m, int) else t[:, bass.ds(m, 1), :].rearrange("p a t -> p (a t)")

        def xg_chunk(part, m):
            return xg[:, part, m, :] if isinstance(m, int) else xg[:, part, bass.ds(m, 1), :].rearrange("p a t -> p (a t)")

        def dve_chunk_lo(dve, k, m, gain):
            dve.wait_ge(xg_hi_done, 8 * k + m + 1)
            g = gains[:, gain + m:gain + m + 1] if isinstance(m, int) else gains[:, bass.ds(m + gain, 1)]
            dve.scalar_tensor_tensor(xg_chunk(1, m), chunk(xT, m), g, xg_chunk(0, m).bitcast(F32),
                                     ALU.mult, ALU.subtract).then_inc(xg_lo_done, 1)

        def pool_acc_start(pool, k):
            if k >= 1:
                pool.wait_ge(stat_ready, NORM_AT[k - 1] + 1)
            if k in (1, 3):
                pool.wait_ge(p_ready, (AB_TILES, ALL_TILES)[k // 2])
            pool.memset(sc[:, 3, :], 0.0).then_inc(acc_added, 1)

        def pool_acc(pool, k, m, par):
            pool.wait_ge(sq_done, 8 * k + m + 1)
            pool.wait_ge(acc_added, 9 * k + m + 1)
            pool.tensor_tensor(sc[:, 3, :], sc[:, 3, :], tq[:, par, 0:T], ALU.add).then_inc(acc_added, 1)

        NORM_AT = [0, 1 + A_HEADS, 2 + A_HEADS, 5 + A_HEADS, 6 + A_HEADS]

        def kind_ab(u):
            return "qkv"[u % 3] if u < A_UNITS else {U_KB: "k", U_VB: "v"}.get(u, "q")

        def qk_index(u):
            return sum(kind_ab(x) != "v" for x in range(u))

        QK_AB = qk_index(N_AB)

        def slot_ab(u):
            return (u // 3) % 2 if u < A_UNITS else (0 if u < U_QB else (u - U_QB) % 2)

        def b_keys(b):
            return max(0, b - 1), min(TB, b + 2)

        AB_TILES = 4 * A_HEADS + 4 * B_HEADS
        A_SETS = 5 * A_HEADS
        B_TILES = 4 * B_HEADS
        B_STEPS = B_TILES + 4
        N_PROJ = N_AB + N_C + N_LAT + 2 * D_HEADS
        QK_ALL = QK_AB + 12 + QC + KVC + 1 + 2 * D_HEADS
        ALL_TILES = AB_TILES + TB * D_HEADS

        def a_set(h, b):
            return 5 * h + b + 1

        def b_set(n):
            return A_SETS + n + 1

        def sync_program(sp):
            for n in range(4):
                sp.dma_start(xT[:, 2 * n:2 * n + 2, :], io["x_t"][:, 2 * n:2 * n + 2, :]).then_inc(x_loaded[n], 16)
            load_unit(sp, 0, 0)
            load_unit(sp, 1, 1)

            sp.wait_ge(vec_copied, 5)
            n_first = VEC_AT[3]
            sp.dma_start(vec_dram[:, 0:n_first], sc[0:NH_BIAS, :, :].rearrange("p a t -> p (a t)")[:, 0:n_first]).then_inc(vec_stored, 16)
            sp.dma_start(vec_dram[:, n_first:VEC_LEN], pn[0:NH_BIAS, 0, :]).then_inc(vec_stored, 16)
            sp.wait_ge(vec_stored, 32)

            def store_rows(v):
                length, _, _, first, heads = VECS[v]
                src = bass.AP(vec_dram.tensor, first * VEC_LEN + VEC_AT[v], [[VEC_LEN, heads], [0, P], [1, length]])
                dst = bass.AP(rep_dram.tensor, REP_AT[v], [[P * length, heads], [length, P], [1, length]])
                sp.dma_start(dst, src).then_inc(rows_stored[v], 16)

            def load_bias(v, head, slot, width, dst=None):
                length, _, _, first, _ = VECS[v]
                src = bass.AP(rep_dram.tensor, REP_AT[v] + (head - first) * P * length + P - 1,
                              [[length - 1, P], [1, width]])
                sp.dma_start(bias[:, slot, 0:width] if dst is None else dst, src).then_inc(bias_loaded[slot], 16)

            store_rows(0)
            sp.wait_ge(rows_stored[0], 16)
            load_bias(0, 0, 0, 896)
            load_bias(0, 1, 1, 896)
            load_unit(sp, 2, 0)
            load_unit(sp, 3, 1)
            store_rows(1)
            for v in (2, 3, 4):
                store_rows(v)
            for h in range(A_HEADS):
                for u in range(3 * h + 4, 3 * h + 7):
                    load_unit(sp, u, u % 2)
                if h == 0:
                    sp.wait_ge(rows_stored[1], 16)
                sp.wait_ge(scored, 8 * (h + 1))
                if h + 2 < A_HEADS:
                    load_bias(0, h + 2, h % 2, 896)
                else:
                    e = h + 2 - A_HEADS
                    load_bias(1, b_head(e), e % 2, 384)
            for e in range(B_HEADS):
                for u in {0: (U_QB + 2, U_QB + 3), 2: (U_WO0,), 4: (U_WO0 + 1,)}.get(e, ()):
                    load_unit(sp, u, u % 2)
                if e + 2 < B_HEADS:
                    sp.wait_ge(scored, 8 * A_HEADS + 4 * (e + 1))
                    load_bias(1, b_head(e + 2), e % 2, 384)
            for v in (2, 3, 4):
                sp.wait_ge(rows_stored[v], 16)
            for e in range(2):
                sp_bias_c(sp, load_bias, e)
            stream_loop(sp, "w_o0", U_WO0, U_WO0 + 2, U_GU0)
            stream_loop(sp, "w_gu0", U_GU0, U_GU0, U_DN0)
            stream_loop(sp, "w_dn0", U_DN0, U_DN0, U_C)
            sp_layer1(sp, load_bias)
            sp_store(sp)

        def stream_loop(sp, name, first, u0, u1):
            assert (u1 - u0) % 2 == 0
            with sp.Fori(0, (u1 - u0) // 2) as i:
                for s in range(2):
                    load_unit(sp, i * 2 + (u0 + s), (u0 + s) % 2, name, first, i * 2 + (u0 - first + s))

        def b_head(e):
            return A_HEADS + e // 2 + 4 * (e % 2)

        def sp_store(sp):
            for m in range(KC):
                sp.wait_ge(final_ready, m + 1)
                sp.dma_start(io["out"][:, m, :], xT[:, m, :]).then_inc(stored, 16)
            sp.wait_ge(stored, 16 * KC)

        def gpsimd_program(pool):
            pool.memset(ident[:, :], 0.0).then_inc(ident_made, 1)
            pool.memset(ones[:, :], 1.0)
            pool.memset(neg_half[:, :], -0.5)
            pool.wait_ge(ident_made, 1)
            pool.affine_select(out=ident[:, :], in_=ident[:, :], compare_op=ALU.not_equal, fill=1.0,
                               base=0, pattern=[[-1, P]], channel_multiplier=1).then_inc(ident_made, 1)
            pool.wait_ge(vec_stored, 32)
            pool_acc_start(pool, 0)
            prep_lo(pool, 0, 0, KC)
            for m in range(KC):
                pool_acc(pool, 0, m, m % 2)
                if m == 1:
                    prep_lo(pool, 1, 1, KC)
            pool_ab(pool)
            pool_wo(pool, 0)
            pool_ffn(pool, 0)
            pool_layer1(pool)

        def pool_qk_lo(pool, i, u, dst):
            pool.wait_ge(qk_hi, i + 1)
            pool.tensor_tensor(dst[1], tq[:, u % 2, 0:T], dst[0].bitcast(F32), ALU.subtract).then_inc(qk_lo, 1)

        def qk_dst(u):
            store = q_ab if kind_ab(u) == "q" else k_ab
            return store[:, slot_ab(u), 0, :], store[:, slot_ab(u), 1, :]

        def pool_evac_ab(pool, u):
            prep_lo(pool, u + 2, u % 2, KC)
            if kind_ab(u) != "v":
                pool_qk_lo(pool, qk_index(u), u, qk_dst(u))

        def pool_oc_lo(pool, c, src, before=0):
            pool.wait_ge(oc_hi, before + c + 1)
            pool.tensor_tensor(oc[:, 1, c, :], src, oc[:, 0, c, :].bitcast(F32), ALU.subtract).then_inc(oc_lo, 1)

        def pool_ab(pool):
            pool_root(pool, 0)
            pool_evac_ab(pool, 0)
            pool_evac_ab(pool, 1)
            pool_evac_ab(pool, 2)
            for h in range(A_HEADS):
                for b in range(TB):
                    if b >= 1:
                        pool_evac_ab(pool, 3 * (h + 1) + b - 1)
                    if h >= 1 and b == 1:
                        pool_root(pool, h)
                    if h >= 1 and b == 3:
                        pool_oc_lo(pool, h - 1, og[:, 1, :])
            for n in range(B_STEPS):
                if n == 0:
                    pool_evac_ab(pool, U_QB + 1)
                if n == 1:
                    pool_root(pool, A_HEADS)
                if n == 3:
                    pool_oc_lo(pool, A_HEADS - 1, og[:, 1, :])
                if n in (12, 20):
                    pool_evac_ab(pool, U_QB + 1 + n // 8)
                if n >= 11 and n % 8 == 3:
                    pool_oc_lo(pool, A_HEADS + (n - 11) // 8, og[:, 0, :])

        def pool_wo(pool, layer):
            k = (1, 3)[layer]
            u0 = (U_WO0, U_WO1)[layer]
            pool_acc_start(pool, k)
            with pool.Fori(0, KC // 2) as i:
                for s in range(2):
                    prep_lo(pool, i * 2 + (u0 + s + 2), (u0 + s) % 2, KC)
                    pool_acc(pool, k, i * 2 + s, s)
            pool_root_slot(pool, layer, 0)

        def pool_root_slot(pool, layer, which):
            pool_root(pool, NORM_AT[(1, 3)[layer] + which])

        def pool_ffn(pool, layer):
            u0, u1 = ((U_GU0, U_DN0), (U_GU1, U_DN1))[layer]
            k = (2, 4)[layer]
            f0 = FC * layer

            def hidden_lo(f, par):
                pool.wait_ge(h_hi, f + f0 + 1)
                pool.tensor_tensor(hid_chunk(1, f), pn[:, par, :], hid_chunk(0, f).bitcast(F32),
                                   ALU.subtract).then_inc(h_lo, 1)

            with pool.Fori(0, FC // 2 - 1) as i:
                for par in range(2):
                    f = i * 2 + par
                    prep_lo(pool, f * 2 + (u0 + 2), u0 % 2, KC)
                    prep_lo(pool, f * 2 + (u0 + 3), (u0 + 1) % 2, KC)
                    hidden_lo(f, par)
            for par in range(2):
                f = FC - 2 + par
                tiles = KC if par == 0 else DOWN_HALF
                prep_lo(pool, u0 + 2 * f + 2, u0 % 2, tiles)
                prep_lo(pool, u0 + 2 * f + 3, (u0 + 1) % 2, tiles)
                hidden_lo(f, par)
            pool_acc_start(pool, k)
            with pool.Fori(0, KC // 2 - 1) as i:
                for par in range(2):
                    m = i * 2 + par
                    for s in range(2):
                        prep_lo(pool, m * 2 + (u1 + s + 2), (u1 + s) % 2, DOWN_HALF)
                    pool_acc(pool, k, m, par)
            for par in range(2):
                m = KC - 2 + par
                for s in range(2):
                    if par == 0:
                        prep_lo(pool, u1 + 2 * m + s + 2, (u1 + s) % 2, DOWN_HALF)
                    elif layer == 0:
                        prep_lo(pool, u1 + 2 * m + s + 2, (u1 + s) % 2, KC)
                pool_acc(pool, k, m, par)

        def hid_chunk(part, f):
            return hid[:, part, f, :] if isinstance(f, int) else hid[:, part, bass.ds(f, 1), :].rearrange("p a t -> p (a t)")

        def scalar_program(act):
            act.dma_start(tab[0:NB, :], io["bias_table"]).then_inc(consts_loaded, 16)
            act.dma_start(bias[0:NB + 1, :, :].rearrange("p a t -> p (a t)")[:, 0:VEC_AT[3]],
                          io["one_hot"][:, 0:VEC_AT[3]]).then_inc(consts_loaded, 16)
            act.dma_start(og[0:NB + 1, 0, :], io["one_hot"][:, VEC_AT[3]:VEC_LEN]).then_inc(consts_loaded, 16)
            act.dma_start(gains[:, :], io["gains"]).then_inc(consts_loaded, 16)
            act.dma_start(sink[:, :], bass.AP(io["sink"].tensor, 0, [[0, P], [1, B_HEADS]])).then_inc(consts_loaded, 16)
            act.dma_start(og[:, 1, 0:4 * HD], bass.AP(io["lambdas"].tensor, 0, [[0, P], [1, 4 * HD]])).then_inc(consts_loaded, 16)
            act.dma_start(masks[:, :], io["comb_masks"]).then_inc(consts_loaded, 16)
            act.wait_ge(consts_loaded, 16 * 7)
            act.wait_ge(lam_step, 2)
            act.activation(lam[:, 2:4], lam[:, 0:2], ACT.Exp).then_inc(lam_exp, 1)
            for m in range(KC):
                act_chunk(act, 0, m, m % 2, G_ATTN0, first_two=m < 2)
                if m in (0, 1):
                    prep_hi(act, m, m, KC)
            act_ab(act)
            act_wo(act, 0)
            act_ffn(act, 0)
            act_layer1(act)

        def act_evac_ab(act, u):
            prep_hi(act, u + 2, u % 2, KC)
            if kind_ab(u) != "v":
                act.wait_ge(proj_t, u + 1)
                act.activation(qk_dst(u)[0], tq[:, u % 2, 0:T], ACT.Copy).then_inc(qk_hi, 1)

        def act_exp(act, s, bias_col=None):
            act.activation(sc[:, s % 4, :], sc[:, s % 4, :], ACT.Exp, scale=-1.0, bias=neg_max[:, s % 8:s % 8 + 1],
                           accum_out=row_sum[:, s % 8:s % 8 + 1]).then_inc(exp_done, 1)

        def act_set(act, n, dst, src):
            act.wait_ge(t_ready, n + 1)
            act.activation(dst, src, ACT.Copy).then_inc(pt_hi, 1)

        def bank3(bank, blocks, width=P):
            return bank[:, 0:blocks * width].rearrange("p (a t) -> p a t", a=blocks)

        def act_ab(act):
            act_evac_ab(act, 0)
            act_evac_ab(act, 1)
            act_evac_ab(act, 2)
            for h in range(A_HEADS):
                for b in range(TB):
                    n = 4 * h + b
                    for s in (2 * n, 2 * n + 1):
                        act.wait_ge(scored, s + 1)
                        act_exp(act, s)
                    if h >= 1 and b == 0:
                        act_o_norm(act, h - 1)
                    if b == 0:
                        act_set(act, a_set(h, -1), v_ab[:, h % 2, 0, :, :], bank3(t_bank[a_set(h, -1) % 2], TB))
                    if b >= 1:
                        act_evac_ab(act, 3 * (h + 1) + b - 1)
                    if h >= 2 and b == 0:
                        act.wait_ge(pv_done, h - 1)
                    act_set(act, a_set(h, b), pt_ab[:, h % 2, 0, :, b * P:(b + 1) * P], bank3(t_bank[a_set(h, b) % 2], TB))
                    if h >= 1 and b == 3:
                        act_oc_a(act, h - 1)
            for n in range(B_STEPS):
                if n == 0:
                    act_set(act, b_set(-1), v_ab[:, 0, 0, :, :], bank3(t_bank[b_set(-1) % 2], TB))
                    act_evac_ab(act, U_QB + 1)
                if 2 <= n < B_TILES + 2:
                    m = n - 2
                    b = m % 4
                    ks, ke = b_keys(b)
                    if b == 0:
                        act.wait_ge(pv_done, A_HEADS - 1 + m // 4)
                    act_set(act, b_set(m), pt_ab[:, (m // 4) % 2, 0, ks:ke, b * P:(b + 1) * P],
                            bank3(t_bank[b_set(m) % 2], ke - ks))
                if n < B_TILES:
                    s = 8 * A_HEADS + n
                    j, hd, b = n // 8, (n // 4) % 2, n % 4
                    ks, ke = b_keys(b)
                    w = (ke - ks) * P
                    head = j + 4 * hd
                    act.wait_ge(shift_ready, n + 1)
                    act.activation(sc[:, s % 4, 0:w], sc[:, s % 4, 0:w], ACT.Exp, scale=-1.0,
                                   bias=neg_max[:, s % 8:s % 8 + 1], accum_out=row_sum[:, s % 8:s % 8 + 1])
                    act.activation(sink_exp[:, s % 8:s % 8 + 1], neg_max[:, s % 8:s % 8 + 1], ACT.Exp,
                                   bias=sink[:, head:head + 1]).then_inc(exp_done, 1)
                if n == 0:
                    act_o_norm(act, A_HEADS - 1)
                if n >= 7 and n % 4 == 3:
                    act_o_b(act, (n - 7) // 4)
                if n == 3:
                    act_oc_a(act, A_HEADS - 1)
                if n in (12, 20):
                    act_evac_ab(act, U_QB + 1 + n // 8)

        def act_o_norm(act, h):
            act.wait_ge(pv_done, h + 1)
            if h >= 1:
                act.wait_ge(oc_lo, h)
            act.activation(og[:, 1, :], o_bank[:, :], ACT.Square)
            act.activation(og[:, 0, :], o_bank[:, :], ACT.Copy).then_inc(o_copied, 1)

        def act_oc_a(act, h):
            act.wait_ge(bc_used, 2 + h)
            act.activation(oc[:, 0, h, :], og[:, 1, :], ACT.Copy).then_inc(oc_hi, 1)

        def act_o_b(act, e):
            act.wait_ge(pv_done, A_HEADS + e + 1)
            if e % 2 == 0:
                act.wait_ge(oc_lo, A_HEADS + e // 2)
            half = e % 2
            act.activation(og[half * HD:(half + 1) * HD, 0, :], o_bank[0:HD, :], ACT.Copy).then_inc(o_copied, 1)
            if half:
                act.wait_ge(o_copied, A_HEADS + e + 1)
                act.activation(oc[:, 0, A_HEADS + e // 2, :], og[:, 0, :], ACT.Copy).then_inc(oc_hi, 1)

        def act_wo(act, layer):
            k = (1, 3)[layer]
            u0 = (U_WO0, U_WO1)[layer]
            gain = (G_FFN0, G_FFN1)[layer]
            act.wait_ge(qk_lo, (QK_AB, QK_ALL)[layer])

            def panel(m, s):
                prep_hi(act, m + (u0 + 2), (u0 + s) % 2, KC, half_of(m, u0 + 2, s))
                act_chunk(act, k, m, s, gain, first_two=isinstance(m, int) and m < 2)

            for m in range(2):
                panel(m, m)
            with act.Fori(1, KC // 2) as i:
                for s in range(2):
                    prep_hi(act, i * 2 + (u0 + 2 + s), (u0 + s) % 2, KC, i + (u0 + 2 + s) // 2)
                    act_chunk(act, k, i * 2 + s, s, gain)

        def half_of(m, base, s):
            return (m + base) // 2

        def act_ffn(act, layer):
            u0, u1 = ((U_GU0, U_DN0), (U_GU1, U_DN1))[layer]
            k = (2, 4)[layer]
            f0 = FC * layer
            gain = (G_ATTN1, G_FINAL)[layer]

            def hidden(f, par, u, tiles, half=None):
                prep_hi(act, u, u0 % 2, tiles, half and half[0])
                act.wait_ge(silu_in, f + f0 + 1)
                act.activation(sc[:, par, :], tq[:, 0, 0:T], ACT.Silu).then_inc(silu_done, 1)
                prep_hi(act, u + 1, (u0 + 1) % 2, tiles, half and half[1])
                act.wait_ge(h_ready, f + f0 + 1)
                if not isinstance(f, int):
                    act.nop(nofuse=True)
                act.activation(hid_chunk(0, f), pn[:, par, :], ACT.Copy).then_inc(h_hi, 1)

            act.preload_act_table(ACT.Silu)
            with act.Fori(0, FC // 2 - 1) as i:
                for par in range(2):
                    f = i * 2 + par
                    base = u0 + 2 * par + 2
                    hidden(f, par, i * 4 + base, KC, [i * 2 + (base + s) // 2 for s in range(2)])
            for par in range(2):
                f = FC - 2 + par
                tiles = KC if par == 0 else DOWN_HALF
                hidden(f, par, u0 + 2 * f + 2, tiles)

            def down(m, par, u, tiles, half=None):
                for s in range(2):
                    if tiles:
                        prep_hi(act, u + s, (u1 + s) % 2, tiles, None if half is None else half[s])
                act_chunk(act, k, m, par, gain, with_xg=layer == 0, first_two=isinstance(m, int) and m < 2)

            for m in range(2):
                down(m, m, u1 + 2 * m + 2, DOWN_HALF)
            with act.Fori(1, KC // 2 - 1) as i:
                for par in range(2):
                    base = u1 + 2 * par + 2
                    down(i * 2 + par, par, i * 4 + base, DOWN_HALF, [i * 2 + (base + s) // 2 for s in range(2)])
            for m in (KC - 2, KC - 1):
                tiles = DOWN_HALF if m == KC - 2 else (KC if layer == 0 else 0)
                down(m, m % 2, u1 + 2 * m + 2, tiles)

        def vector_program(dve):
            dve.memset(tab[NB:NB + 1, :], NEG).then_inc(lam_step, 1)
            dve.wait_ge(consts_loaded, 16 * 7)
            for n in range(2):
                ins = dve.tensor_tensor_reduce(out=og[:, 2, n * HD:(n + 1) * HD], in0=og[:, 1, 2 * n * HD:(2 * n + 1) * HD],
                                               in1=og[:, 1, (2 * n + 1) * HD:(2 * n + 2) * HD], scale=1.0, scalar=0.0,
                                               op0=ALU.mult, op1=ALU.add, accum_out=lam[:, n:n + 1])
            ins.then_inc(lam_step, 1)
            dve.tensor_scalar(neg_sink[:, :], sink[:, :], -1.0, None, ALU.mult)
            dve.tensor_scalar(sub_gain[:, :], gains[:, G_SUB:G_SUB + 1], 1.0 - LAMBDA_INIT, None, ALU.mult)
            dve.wait_ge(lam_exp, 1)
            dve.scalar_tensor_tensor(lam[:, 4:5], lam[:, 3:4], LAMBDA_INIT, lam[:, 2:3], ALU.subtract, ALU.subtract).then_inc(lam_step, 1)
            dve.wait_ge(lam_step, 3)
            for n in range(5):
                dve.wait_ge(vec_mm, n + 1)
                w = 512 if n < 3 else (384 if n == 3 else 512)
                dst = sc[0:NH_BIAS, n, 0:w] if n < 4 else pn[0:NH_BIAS, 0, :]
                src = (t_bank + s_bank + [o_bank])[n]
                dve.tensor_copy(dst, src[0:NH_BIAS, 0:w]).then_inc(vec_copied, 1)
            for m in range(KC):
                if m % 2 == 0:
                    dve.wait_ge(x_loaded[m // 2], 16)
                dve.sem_inc(x_added, 1)
                dve_chunk_lo(dve, 0, m, G_ATTN0)
            dve_mean(dve, 0, DM)
            dve_diag(dve, 0, sc[:, 2, :])
            dve.wait_ge(bc_ready, 1)
            dve.tensor_copy(rstd[:, :], m_bank[:, :]).then_inc(bc_used, 1)
            dve.wait_ge(bc_used, 1)
            dve_ab(dve)
            dve_wo(dve, 0)
            dve_ffn(dve, 0)
            dve_layer1(dve)

        def dve_evac_ab(dve, u):
            dve.wait_ge(unit_done, u + 1)
            if u >= 2 and kind_ab(u - 2) != "v":
                dve.wait_ge(qk_lo, qk_index(u - 2) + 1)
            scale = HD ** -0.5 if kind_ab(u) == "q" else 1.0
            dve.scalar_tensor_tensor(tq[:, u % 2, 0:T], g_bank[u % 2][:, :], scale, rstd[:, :],
                                     ALU.mult, ALU.mult).then_inc(proj_t, 1)

        def dve_set(dve, n, dst_lo, src, dst_hi):
            dve.wait_ge(pt_hi, n + 1)
            dve.tensor_tensor(dst_lo, src, dst_hi.bitcast(F32), ALU.subtract).then_inc(t_free, 1)

        def score(dve, s, width, bank, bias_ap):
            dve.wait_ge(s_ready, s + 1)
            dve.tensor_tensor_reduce(out=sc[:, s % 4, 0:width], in0=bank[:, 0:width], in1=bias_ap, scale=-1.0, scalar=BIG,
                                     op0=ALU.add, op1=ALU.min, accum_out=neg_max[:, s % 8:s % 8 + 1]).then_inc(scored, 1)

        def dve_ab(dve):
            for u in range(3):
                dve_evac_ab(dve, u)
            for h in range(A_HEADS):
                dve.wait_ge(bias_loaded[h % 2], 16 * (h // 2 + 1))
                for b in range(TB):
                    n = 4 * h + b
                    for s in (2 * n, 2 * n + 1):
                        score(dve, s, T, s_bank[s % 2], bias[:, h % 2, 384 - b * P:384 - b * P + T])
                    c = (2 * n) % 8
                    dve.wait_ge(exp_done, 2 * n + 2)
                    dve.reciprocal(inv_sum[:, c:c + 2], row_sum[:, c:c + 2]).then_inc(recip_done, 1)
                    dve.wait_ge(recip_done, n + 1)
                    s1 = (2 * n + 1) % 4
                    dve.tensor_scalar(sc[:, s1, :], sc[:, s1, :], inv_sum[:, c + 1:c + 2], lam[:, 4:5], ALU.mult,
                                      ALU.mult).then_inc(part_done, 1)
                    dve.wait_ge(part_done, n + 1)
                    dve.scalar_tensor_tensor(pn[:, n % 2, :], sc[:, s1 - 1, :], inv_sum[:, c:c + 1], sc[:, s1, :],
                                             ALU.mult, ALU.add).then_inc(p_ready, 1)
                    if b == 0:
                        k = a_set(h, -1)
                        dve_set(dve, k, v_ab[:, h % 2, 1, :, :], bank3(t_bank[k % 2], TB), v_ab[:, h % 2, 0, :, :])
                    if b >= 1:
                        dve_evac_ab(dve, 3 * (h + 1) + b - 1)
                    if h >= 1 and b == 1:
                        dve_mean(dve, h, P)
                    if h >= 1 and b == 2:
                        dve_diag(dve, h, og[:, 2, :])
                    if h >= 1 and b == 3:
                        dve_o_norm(dve, h - 1)
                    k = a_set(h, b)
                    cols = slice(b * P, (b + 1) * P)
                    dve_set(dve, k, pt_ab[:, h % 2, 1, :, cols], bank3(t_bank[k % 2], TB), pt_ab[:, h % 2, 0, :, cols])
            for n in range(B_STEPS):
                if n == 0:
                    k = b_set(-1)
                    dve_set(dve, k, v_ab[:, 0, 1, :, :], bank3(t_bank[k % 2], TB), v_ab[:, 0, 0, :, :])
                    dve_evac_ab(dve, U_QB + 1)
                if 1 <= n <= B_TILES:
                    dve_norm_b(dve, n - 1)
                if n < B_TILES:
                    e, b = n // 4, n % 4
                    s = 8 * A_HEADS + n
                    ks, ke = b_keys(b)
                    w = (ke - ks) * P
                    head = e // 2 + 4 * (e % 2)
                    c = s % 8
                    if b == 0:
                        dve.wait_ge(bias_loaded[e % 2], 16 * ((A_HEADS + e) // 2 + 1))
                    j0 = (ks - b + 1) * P
                    score(dve, s, w, s_bank[s % 2], bias[:, e % 2, j0:j0 + w])
                    dve.wait_ge(scored, s + 1)
                    dve.tensor_scalar(neg_max[:, c:c + 1], neg_max[:, c:c + 1], neg_sink[:, head:head + 1], None,
                                      ALU.min).then_inc(shift_ready, 1)
                if n == 1:
                    dve_mean(dve, A_HEADS, P)
                if n == 2:
                    dve_diag(dve, A_HEADS, og[:, 2, :])
                if n == 3:
                    dve_o_norm(dve, A_HEADS - 1)
                if 2 <= n < B_TILES + 2:
                    m = n - 2
                    b = m % 4
                    ks, ke = b_keys(b)
                    k = b_set(m)
                    cols = slice(b * P, (b + 1) * P)
                    dve_set(dve, k, pt_ab[:, (m // 4) % 2, 1, ks:ke, cols], bank3(t_bank[k % 2], ke - ks),
                            pt_ab[:, (m // 4) % 2, 0, ks:ke, cols])
                if n in (12, 20):
                    dve_evac_ab(dve, U_QB + 1 + n // 8)

        def dve_norm_b(dve, n):
            s = 8 * A_HEADS + n
            ks, ke = b_keys(n % 4)
            w = (ke - ks) * P
            c = s % 8
            dve.wait_ge(exp_done, s + 1)
            dve.tensor_tensor(row_sum[:, c:c + 1], row_sum[:, c:c + 1], sink_exp[:, c:c + 1], ALU.add).then_inc(part_done, 1)
            dve.wait_ge(part_done, 4 * A_HEADS + n + 1)
            dve.reciprocal(inv_sum[:, c:c + 1], row_sum[:, c:c + 1]).then_inc(recip_done, 1)
            dve.wait_ge(recip_done, 4 * A_HEADS + n + 1)
            dve.tensor_scalar(pn[:, n % 2, 0:w], sc[:, s % 4, 0:w], inv_sum[:, c:c + 1], None, ALU.mult).then_inc(p_ready, 1)

        def dve_o_norm(dve, h):
            dve.wait_ge(bc_ready, 2 + h)
            dve.scalar_tensor_tensor(og[:, 1, :], og[:, 0, :], sub_gain[:, 0:1], m_bank[:, :], ALU.mult,
                                     ALU.mult).then_inc(bc_used, 1)

        def dve_panel(dve, k, m, u_last, bank, gain, with_xg=True):
            dve.wait_ge(unit_done, u_last + 1)
            dve.tensor_tensor(chunk(xT, m), bank[:, :], chunk(xT, m), ALU.add).then_inc(x_added, 1)
            dve.wait_ge(x_added, 8 * k + m + 1)
            if with_xg:
                dve_chunk_lo(dve, k, m, gain)

        def dve_wo(dve, layer):
            k = (1, 3)[layer]
            u0 = (U_WO0, U_WO1)[layer]
            gain = (G_FFN0, G_FFN1)[layer]
            with dve.Fori(0, KC // 2) as i:
                for s in range(2):
                    dve_panel(dve, k, i * 2 + s, i * 2 + (u0 + s), g_bank[s], gain)

        def dve_rstd(dve, n):
            dve_mean(dve, n, DM)
            dve_diag(dve, n, sc[:, 2, :])
            dve.wait_ge(bc_ready, n + 1)
            dve.tensor_copy(rstd[:, :], m_bank[:, :]).then_inc(bc_used, 1)
            dve.wait_ge(bc_used, n + 1)

        def dve_ffn(dve, layer):
            u0, u1 = ((U_GU0, U_DN0), (U_GU1, U_DN1))[layer]
            k = (2, 4)[layer]
            f0 = FC * layer
            gain = (G_ATTN1, G_FINAL)[layer]
            dve_rstd(dve, NORM_AT[(1, 3)[layer]])

            def hidden(f, par, u, first=False):
                dve.wait_ge(unit_done, u + 1)
                if not first:
                    dve.wait_ge(silu_done, f + f0)
                dve.tensor_tensor(tq[:, 0, 0:T], g_bank[0][:, :], rstd[:, :], ALU.mult).then_inc(silu_in, 1)
                dve.wait_ge(unit_done, u + 2)
                if not first:
                    dve.wait_ge(h_ready, f + f0)
                dve.tensor_tensor(tq[:, 1, 0:T], g_bank[1][:, :], rstd[:, :], ALU.mult).then_inc(up_scaled, 1)
                dve.wait_ge(up_scaled, f + f0 + 1)
                dve.wait_ge(silu_done, f + f0 + 1)
                if not isinstance(f, int) or f + f0 > 1:
                    dve.wait_ge(h_lo, f + f0 - 1)
                dve.tensor_tensor(pn[:, par, :], sc[:, par, :], tq[:, 1, 0:T], ALU.mult).then_inc(h_ready, 1)

            for f in range(2):
                hidden(f, f, u0 + 2 * f, first=f == 0 and layer == 0)
            with dve.Fori(1, FC // 2) as i:
                for par in range(2):
                    hidden(i * 2 + par, par, i * 4 + (u0 + 2 * par))
            with dve.Fori(0, KC // 2) as i:
                for par in range(2):
                    dve_panel(dve, k, i * 2 + par, i * 4 + (u1 + 2 * par + 1), g_bank[par], gain, with_xg=layer == 0)

        def tensor_program(pe):
            pe.wait_ge(ident_made, 2)
            pe.wait_ge(consts_loaded, 16 * 7)
            pe.wait_ge(lam_step, 1)
            flat = bias[0:NB + 1, :, :].rearrange("p a t -> p (a t)")
            for n in range(5):
                w = 512 if n != 3 else 384
                src = flat[:, n * 512:n * 512 + w] if n < 4 else og[0:NB + 1, 0, :]
                dst = (t_bank + s_bank + [o_bank])[n]
                pe.matmul(dst[0:NH_BIAS, 0:w], tab[:, :], src, start=True, stop=True).then_inc(vec_mm, 1)
            pe_ab(pe)
            pe_wo(pe, 0)
            pe_ffn(pe, 0)
            pe_layer1(pe)

        def unit_step(pe, u, kc, tiles, bank, rhs, slot, free=None, chunks=None):
            if kc == 0:
                pe.wait_ge(w_lo_done, u + 1)
                if free is not None:
                    pe.wait_ge(*free)
            if chunks is not None:
                pe.wait_ge(xg_lo_done, chunks + kc + 1)
            w_h, w_l = wtile(slot, kc)
            mm = three(pe, bank[:, :], w_h, w_l, rhs[0][:, kc, :], rhs[1][:, kc, :], kc == 0, kc == tiles - 1)
            if kc == tiles - 1:
                mm.then_inc(unit_done, 1)

        xg_parts = (xg[:, 0], xg[:, 1])
        oc_parts = (oc[:, 0], oc[:, 1])

        def ab_step(pe, u, kc):
            unit_step(pe, u, kc, KC, g_bank[u % 2], xg_parts, u % 2,
                      free=(proj_t, u - 1) if u >= 2 else None, chunks=0 if u == 0 else None)

        def pe_set(pe, n, src, blocks, identity=None):
            if n >= 2:
                pe.wait_ge(t_free, n - 1)
            bank = t_bank[n % 2]
            for c in range(blocks):
                mm = pe.transpose(bank[:, c * P:(c + 1) * P], src(c), ident[:, :])
            mm.then_inc(t_ready, 1)

        def pe_ab(pe):
            for u in range(3):
                for kc in range(KC):
                    ab_step(pe, u, kc)
                if u == 0:
                    pe.wait_ge(acc_added, 9)
                    pe_stat(pe, 0, sc[:, 3, :])
                if u == 1:
                    pe_broadcast(pe, 0, sc[:, 2, :])
            pe.wait_ge(vec_copied, 5)
            for h in range(A_HEADS):
                pe.wait_ge(qk_lo, 2 * h + 2)
                for b in range(TB):
                    n = 4 * h + b
                    for m in range(2):
                        s = 2 * n + m
                        if s >= 2:
                            pe.wait_ge(scored, s - 1)
                        rows = slice(m * HD, (m + 1) * HD)
                        cols = slice(b * P, (b + 1) * P)
                        q, k = q_ab[rows, h % 2], k_ab[rows, h % 2]
                        three(pe, s_bank[s % 2][:, :], q[:, 0, cols], q[:, 1, cols], k[:, 0, :], k[:, 1, :],
                              True, True).then_inc(s_ready, 1)
                    for step in range(6 * b, 6 * b + 6):
                        ab_step(pe, 3 * (h + 1) + step // KC, step % KC)
                    if b == 0:
                        if h >= 1:
                            pe_pv_a(pe, h - 1)
                        u = 3 * h + 2
                        pe.wait_ge(proj_t, u + 1)
                        pe_set(pe, a_set(h, -1), lambda c: tq[:, u % 2, c * P:(c + 1) * P], TB)
                    if h >= 1 and b == 1:
                        pe.wait_ge(o_copied, h)
                        pe_stat(pe, h, og[:, 1, :])
                    if h >= 1 and b == 2:
                        pe_broadcast(pe, h, og[:, 2, :])
                    pe.wait_ge(p_ready, n + 1)
                    pe_set(pe, a_set(h, b), lambda c: pn[:, n % 2, c * P:(c + 1) * P], TB)
            for n in range(B_STEPS):
                if n == 0:
                    pe.wait_ge(proj_t, U_VB + 1)
                    pe_set(pe, b_set(-1), lambda c: tq[:, U_VB % 2, c * P:(c + 1) * P], TB)
                    for kc in range(KC):
                        ab_step(pe, U_QB + 1, kc)
                    pe_pv_a(pe, A_HEADS - 1)
                if n < B_TILES:
                    e, b = n // 4, n % 4
                    j, hd = e // 2, e % 2
                    s = 8 * A_HEADS + n
                    ks, ke = b_keys(b)
                    if n % 8 == 0:
                        pe.wait_ge(qk_lo, 10 + j)
                    pe.wait_ge(scored, s - 1)
                    rows, cols, keys = slice(hd * HD, (hd + 1) * HD), slice(b * P, (b + 1) * P), slice(ks * P, ke * P)
                    q, k = q_ab[rows, j % 2], k_ab[rows, 0]
                    three(pe, s_bank[s % 2][:, 0:(ke - ks) * P], q[:, 0, cols], q[:, 1, cols], k[:, 0, keys], k[:, 1, keys],
                          True, True).then_inc(s_ready, 1)
                    if j in (1, 2) and n % 8 < 4:
                        for kc in (2 * (n % 4), 2 * (n % 4) + 1):
                            ab_step(pe, U_QB + 1 + j, kc)
                for m, kc in wo_ahead_b(n):
                    wo_tile(pe, 0, m, m, kc)
                if n == 1:
                    pe.wait_ge(o_copied, A_HEADS)
                    pe_stat(pe, A_HEADS, og[:, 1, :])
                if n == 2:
                    pe_broadcast(pe, A_HEADS, og[:, 2, :])
                if n >= 6 and n % 4 == 2:
                    pe_pv_b(pe, (n - 6) // 4)
                if 1 <= n <= B_TILES:
                    m = n - 1
                    ks, ke = b_keys(m % 4)
                    pe.wait_ge(p_ready, 4 * A_HEADS + m + 1)
                    pe_set(pe, b_set(m), lambda c: pn[:, m % 2, c * P:(c + 1) * P], ke - ks)

        AHEAD = [(m, kc) for kcs in (range(KC - 2), (KC - 2,)) for m in range(2) for kc in kcs]

        def wo_ahead_b(n):
            first = B_TILES - 8
            if n < first or n > B_TILES + 2:
                return []
            if n < B_TILES:
                return AHEAD[n - first:n - first + 1]
            return AHEAD[8 + 2 * (n - B_TILES):8 + 2 * (n - B_TILES) + 2]

        def wo_tile(pe, layer, m, s, kc):
            u0 = (U_WO0, U_WO1)[layer]
            k = (1, 3)[layer]
            ahead = isinstance(m, int)
            if ahead and kc == 0:
                pe.wait_ge(proj_t, (N_AB, N_PROJ)[layer] - 1 + m)
            if ahead:
                pe.wait_ge(oc_lo, 8 * layer + kc + 1)
            unit_step(pe, m + u0, kc, KC, g_bank[s], oc_parts, (u0 + s) % 2,
                      free=None if ahead else (x_added, m + (8 * k - 1)))

        def pe_pv_a(pe, h):
            pe.wait_ge(t_free, a_set(h, 3) + 1)
            if h >= 1:
                pe.wait_ge(o_copied, h)
            for kc in range(TB):
                mm = three(pe, o_bank[:, :], v_ab[:, h % 2, 0, kc, :], v_ab[:, h % 2, 1, kc, :],
                           pt_ab[:, h % 2, 0, kc, :], pt_ab[:, h % 2, 1, kc, :], kc == 0, kc == TB - 1)
            mm.then_inc(pv_done, 1)

        def pe_pv_b(pe, e):
            pe.wait_ge(t_free, b_set(4 * e + 3) + 1)
            pe.wait_ge(o_copied, A_HEADS + e)
            cols = slice((e % 2) * HD, (e % 2 + 1) * HD)
            for kc in (0, 3, 1, 2):
                qs, qe = b_keys(kc)
                mm = three(pe, o_bank[0:HD, qs * P:qe * P], v_ab[:, 0, 0, kc, cols], v_ab[:, 0, 1, kc, cols],
                           pt_ab[:, e % 2, 0, kc, qs * P:qe * P], pt_ab[:, e % 2, 1, kc, qs * P:qe * P], kc == 0, kc == 2)
            mm.then_inc(pv_done, 1)

        def pe_wo(pe, layer):
            for m in range(2):
                wo_tile(pe, layer, m, m, KC - 1)
            with pe.Fori(1, KC // 2) as i:
                for s in range(2):
                    for kc in range(KC):
                        wo_tile(pe, layer, i * 2 + s, s, kc)

        def pe_ffn(pe, layer):
            u0, u1 = ((U_GU0, U_DN0), (U_GU1, U_DN1))[layer]
            n = NORM_AT[(1, 3)[layer]]
            k = (1, 3)[layer]
            for s in range(2):
                for kc in range(KC):
                    unit_step(pe, u0 + s, kc, KC, g_bank[s], xg_parts, (u0 + s) % 2,
                              free=(x_added, 8 * k + 7 + s), chunks=8 * k if s == 0 else None)
                if s == 0:
                    pe.wait_ge(acc_added, 9 * (k + 1))
                    pe_stat(pe, n, sc[:, 3, :])
                else:
                    pe_broadcast(pe, n, sc[:, 2, :])
            with pe.Fori(1, FC) as i:
                for s in range(2):
                    for kc in range(KC):
                        unit_step(pe, i * 2 + (u0 + s), kc, KC, g_bank[s], xg_parts, (u0 + s) % 2,
                                  free=((silu_in, up_scaled)[s], i + FC * layer))

            hid_parts = (hid[:, 0], hid[:, 1])

            def down(u, s, par, free, panel0=False):
                slot = (u1 + s) % 2
                pe.wait_ge(w_lo_done, u + 1)
                if s == 0:
                    pe.wait_ge(*free)
                for kc in range(DOWN_HALF):
                    c = s * DOWN_HALF + kc
                    if panel0:
                        pe.wait_ge(h_lo, FC * layer + c + 1)
                    w_h, w_l = wtile(slot, kc)
                    mm = three(pe, g_bank[par][:, :], w_h, w_l, hid_parts[0][:, c, :], hid_parts[1][:, c, :],
                               c == 0, c == FC - 1)
                mm.then_inc(unit_done, 1)

            for s in range(2):
                down(u1 + s, s, 0, (silu_in, FC * (layer + 1)), panel0=True)
            for s in range(2):
                down(u1 + 2 + s, s, 1, (up_scaled, FC * (layer + 1)))
            with pe.Fori(1, KC // 2) as i:
                for par in range(2):
                    for s in range(2):
                        down(i * 4 + (u1 + 2 * par + s), s, par, (x_added, i * 2 + (8 * (k + 1) + par - 1)))

        def c_tiles(c):
            return 4 if c % 3 == 0 else 2

        C_TILE_AT = [sum(c_tiles(x) for x in range(c)) for c in range(7)]
        C_TILE_LIST = [(c, ti) for c in range(6) for ti in range(c_tiles(c))]
        S_C = 8 * A_HEADS + B_TILES
        S_D = S_C + len(C_TILE_LIST)
        SET_C = A_SETS + B_TILES + 1
        c_sets, at = {}, SET_C
        for t_, (c_, ti_) in enumerate(C_TILE_LIST):
            if ti_ == 0:
                for k_ in range(2 if c_ % 3 == 0 else 1):
                    c_sets["v", c_, k_] = at
                    at += 1
            c_sets["t", t_] = at
            at += 1
        SET_D = at
        T_AB = N_AB
        QK_C = QK_AB
        QK_LAT = QK_C + 12
        QK_D = QK_LAT + QC + KVC + 1
        PV_C = A_HEADS + B_HEADS
        PV_D = PV_C + len(C_TILE_LIST)
        BIAS_C = (A_HEADS + B_HEADS) // 2

        def c_tile(t):
            c, ti = C_TILE_LIST[t]
            g = c % 3
            if g == 0:
                return c, g, ti // 2, [2 * (ti % 2), 2 * (ti % 2) + 1]
            return c, g, ti, list(range(TB))

        def c_last_tile(e):
            return max(t for t in range(len(C_TILE_LIST)) if 2 * c_tile(t)[0] + c_tile(t)[2] == e)

        def c_bias_count(e):
            return BIAS_C + e // 2 + 1

        def c_steps(t):
            c, ti = C_TILE_LIST[t]
            n = 3 * KC // c_tiles(c)
            return range(ti * n, (ti + 1) * n) if c < 5 else range(0)

        def c_done_units(t):
            return [U_C + 3 * (C_TILE_LIST[t][0] + 1) + s // KC for s in c_steps(t) if s % KC == KC - 1]

        def kind_c(u):
            return "qkv"[(u - U_C) % 3]

        def qk_index_c(u):
            return QK_C + 2 * ((u - U_C) // 3) + (u - U_C) % 3

        def strided(ap, b):
            return ap.rearrange("p (l s) -> p s l", s=4)[:, b, :]

        q_c = region(R0, 2, 2, T)
        k_c = region(R0 + 2048, 2, 2, T + P)
        v_c = region(R0 + 4608, 2, 2, TB + 1, P)
        lat = region(R0 + 7168, 2, QC + KVC, T)
        pt_c = [[oc[:, part, 2 + slot, :] for part in range(2)] for slot in range(2)]
        k_d = region(R0 + 2048, 2, 2, T)
        v_d = region(R0 + 4096, 2, 2, TB, HD)
        q_d = q_c
        pt_d = xg[:, :, :, :].rearrange("p s (c k) t -> p s c k t", c=2)
        stats_v = stats[:, :].rearrange("p (r s g h b) -> p r s g h b", r=2, s=2, g=3, h=2)
        nat_v = nat[:, :].rearrange("p (s g x) -> p s g x", s=2, g=3)
        tq_c = [tq[:, par, HD:HD + T] for par in range(2)]

        def tiles_of(u):
            return D_TILES if U_D <= u < U_WO1 else DOWN_HALF if U_DN0 <= u < U_C or u >= U_DN1 else KC

        def sp_bias_c(sp, load_bias, e):
            c, hd = e // 2, e % 2
            p, g = c // 3, c % 3
            head, slot = 4 * g + 2 * p + hd, e % 2
            if e >= 2:
                sp.wait_ge(scored, S_C + c_last_tile(e - 2) + 1)
            else:
                sp.wait_ge(scored, S_C)
            if g == 0:
                length = VECS[2][0]
                src = bass.AP(rep_dram.tensor, REP_AT[2] + head * P * length + P - 1, [[length - 1, P], [0, TB], [1, 2 * P]])
                sp.dma_start(bias[:, slot, :].rearrange("p (b j) -> p b j", b=TB), src).then_inc(bias_loaded[slot], 16)
            else:
                load_bias(2 + g, head, slot, P)

        def sp_layer1(sp, load_bias):
            sp.wait_ge(h_lo, FC)
            sp.dma_start(pn[:, 0, :], io["comb_select"]).then_inc(select_loaded, 16)
            for u in range(U_C, U_C + 4):
                load_unit(sp, u, u % 2)
            for c in range(6):
                for u in range(U_C + 3 * c + 4, U_C + 3 * c + 7):
                    load_unit(sp, u, u % 2)
                for e in (2 * c + 2, 2 * c + 3):
                    if e < 12:
                        sp_bias_c(sp, load_bias, e)
            sp.wait_ge(scored, S_D)
            sp.dma_start(bias[:, :, :].rearrange("p a t -> p (a t)")[:, 0:3 * T],
                         io["rotary"].rearrange("p a t -> p (a t)")).then_inc(rotary_loaded, 16)
            for u in range(U_C + 22, U_D):
                load_unit(sp, u, u % 2)
            stream_loop(sp, "w_d", U_D, U_D, U_WO1)
            stream_loop(sp, "w_o1", U_WO1, U_WO1, U_GU1)
            stream_loop(sp, "w_gu1", U_GU1, U_GU1, U_DN1)
            stream_loop(sp, "w_dn1", U_DN1, U_DN1, U_END)

        def c_step(pe, u, kc):
            j = u - U_C
            free = (proj_t, T_AB + j - 1) if j >= 2 else (x_added, 8 * 2 + 7 + j)
            unit_step(pe, u, kc, KC, g_bank[j % 2], xg_parts, u % 2, free=free, chunks=16 if j == 0 else None)

        def pe_layer1(pe):
            for j in range(3):
                for kc in range(KC):
                    c_step(pe, U_C + j, kc)
                if j == 0:
                    pe.wait_ge(acc_added, 27)
                    pe_stat(pe, NORM_AT[2], sc[:, 3, :])
                if j == 1:
                    pe_broadcast(pe, NORM_AT[2], sc[:, 2, :])
            pe.wait_ge(k_pads_zeroed, 1)
            for t in range(len(C_TILE_LIST)):
                c, g, hd, blocks = c_tile(t)
                s = S_C + t
                rows = slice(hd * HD, (hd + 1) * HD)
                if C_TILE_LIST[t][1] == 0:
                    pe.wait_ge(qk_lo, QK_C + 2 * c + 2)
                pe.wait_ge(scored, s - 1)
                q, k = q_c[rows, c % 2], k_c[rows, c % 2]
                for i, b in enumerate(blocks):
                    if g == 0:
                        args = [q[:, x, b * P:(b + 1) * P] for x in range(2)] + [k[:, x, b * P:b * P + 2 * P] for x in range(2)]
                        out = s_bank[s % 2][:, 2 * P * i:2 * P * (i + 1)]
                    else:
                        args = [strided(q[:, x, :], b) for x in range(2)] + [strided(k[:, x, HD:HD + T], b) for x in range(2)]
                        out = s_bank[s % 2][:, P * i:P * (i + 1)]
                    mm = three(pe, out, *args, True, True)
                mm.then_inc(s_ready, 1)
                for step in c_steps(t):
                    c_step(pe, U_C + 3 * (c + 1) + step // KC, step % KC)
                if t >= 1:
                    pe_pv_c(pe, t - 1)
                if C_TILE_LIST[t][1] == 0:
                    u = U_C + 3 * c + 2
                    pe.wait_ge(proj_t, T_AB + 3 * c + 3)
                    src = tq[:, (u - U_C) % 2, :]
                    if g == 0:
                        pe_set(pe, c_sets["v", c, 0], lambda x: src[:, x * P:(x + 1) * P], TB)
                        pe_set(pe, c_sets["v", c, 1], lambda x: src[:, TB * P:(TB + 1) * P], 1)
                    else:
                        pe_set(pe, c_sets["v", c, 0], lambda x: strided(src[:, HD:HD + T], x), TB)
                pe.wait_ge(exp_done, s + 1)
                pe_set(pe, c_sets["t", t], lambda x: sc[:, t % 2, x * P:(x + 1) * P], TB)
                if C_TILE_AT[3] <= t < C_TILE_AT[4]:
                    pe_comb(pe, 0, t - C_TILE_AT[3])
            pe_pv_c(pe, len(C_TILE_LIST) - 1)

            for c in range(N_LAT):
                u = U_LAT + c
                for kc in range(KC):
                    if kc == 0 and c >= 2:
                        pe.wait_ge(lat_sq, min(c - 1, QC + KVC))
                    unit_step(pe, u, kc, KC, g_bank[(u - U_C) % 2], xg_parts, u % 2, free=(proj_t, T_AB + u - U_C - 1))
                if c < 4:
                    pe_comb(pe, 1, c)
                if c == 4:
                    pe.wait_ge(mix_done, 6)
                    pe.wait_ge(lat_acc, 1)
                    pe_stat(pe, 7, sc[:, 1, :])
                if c == 5:
                    pe_broadcast(pe, 7, sc[:, 2, :])
                if c == 6:
                    pe.wait_ge(lat_acc, 2)
                    pe_stat(pe, 8, sc[:, 0, :])
            pe_broadcast(pe, 8, sc[:, 2, :])

            for kc in range(D_TILES):
                d_step(pe, 0, kc)
            pe.wait_ge(proj_t, PROJ_D + 2)
            pe_set(pe, SET_D, lambda x: tq[:, 1, x * P:(x + 1) * P], TB)
            pe_head_d(pe, 0, 0)
            pe_head_d(pe, 1, 1)
            with pe.Fori(1, D_HEADS // 2 - 2) as i:
                for par in range(2):
                    pe_head_d(pe, i * 2 + par, par)
            for h in range(D_HEADS - 4, D_HEADS):
                pe_head_d(pe, h, h % 2)
            last = D_HEADS - 1
            for m, kc in AHEAD[7:9]:
                wo_tile(pe, 1, m, m, kc)
            d_tile_set(pe, last, 1, 3)
            for m, kc in AHEAD[9:]:
                wo_tile(pe, 1, m, m, kc)
            pe_pv_d(pe, last, 1)
            pe_wo(pe, 1)
            pe_ffn(pe, 1)
            pe.wait_ge(acc_added, 45)
            pe_stat(pe, NORM_AT[4], sc[:, 3, :])
            pe_broadcast(pe, NORM_AT[4], sc[:, 2, :])

        PROJ_D = T_AB + N_C + N_LAT

        def pe_pv_c(pe, t):
            c, g, hd, blocks = c_tile(t)
            pe.wait_ge(t_free, c_sets["t", t] + 1)
            pe.wait_ge(o_copied, PV_C + t)
            cols = slice(hd * HD, (hd + 1) * HD)
            v, pt = v_c[:, c % 2], pt_c[t % 2]
            for i, b in enumerate(blocks):
                out = o_bank[0:HD, b * P:(b + 1) * P]
                for x in range(2 if g == 0 else 1):
                    j = (2 * i + x) if g == 0 else i
                    mm = three(pe, out, v[:, 0, b + x, cols], v[:, 1, b + x, cols],
                               pt[0][:, j * P:(j + 1) * P], pt[1][:, j * P:(j + 1) * P], x == 0, g != 0 or x == 1)
            mm.then_inc(pv_done, 1)

        def pe_comb(pe, p, step):
            if step == 0:
                pe.wait_ge(select_loaded, 16)
                pe.wait_ge(exp_done, S_C + C_TILE_AT[3 * (p + 1)])
                if p == 0:
                    pe.wait_ge(bc_used, NORM_AT[2] + 1)
                else:
                    pe.wait_ge(mix_done, 3)
                for g in (1, 2):
                    for b in range(TB):
                        i = (g - 1) * TB + b
                        mm = pe.matmul(m_bank[:, i * 16:(i + 1) * 16], pn[:, 0, b * P:(b + 1) * P],
                                       stats_v[:, p, :, g, :, :], start=True, stop=True)
                mm.then_inc(comb_mm, 1)
            if step < 3:
                for hd in range(2):
                    pe.wait_ge(comb_diag, 6 * p + 2 * step + hd + 1)
                    mm = pe.matmul(m_bank[hd * HD:(hd + 1) * HD, :], ones[:, 0:HD], sc[:, 2 + hd, :], start=True, stop=True)
                mm.then_inc(comb_bc, 1)

        def d_step(pe, h, kc):
            u = h + U_D
            slot = (U_D + (h if isinstance(h, int) else 0)) % 2
            return d_step_at(pe, h, kc, slot)

        def d_step_at(pe, h, kc, slot):
            u = h + U_D
            if kc == 0:
                pe.wait_ge(w_lo_done, u + 1)
                pe.wait_ge(qk_lo, QK_LAT + QC + KVC)
                pe.wait_ge(proj_t, h * 2 + PROJ_D)
            w_h, w_l = wtile(slot, kc)
            q = kc < QC
            mm = three(pe, g_bank[0 if q else 1][:, :], w_h, w_l, lat[:, 0, kc, :], lat[:, 1, kc, :],
                       kc in (0, QC), kc in (QC - 1, D_TILES - 1))
            if kc == QC - 1:
                mm.then_inc(q_done, 1)
            if kc == D_TILES - 1:
                mm.then_inc(unit_done, 1)

        def set_d(h, b):
            if isinstance(h, int) and h == D_HEADS - 1 and b >= 2:
                return SET_D + 5 * h + b + 1
            return h * 5 + (SET_D + {0: 1, 1: 2, -1: 3, 2: 4, 3: 5}[b])

        def set_d_par(h_par, b, last=False):
            return (SET_D + h_par + ({0: 1, 1: 2, -1: 3, 2: 4, 3: 5}[b] - (1 if last and b >= 2 else 0))) % 2

        def is_last(h):
            return isinstance(h, int) and h == D_HEADS - 1

        def pe_set_at(pe, n, bank, src, blocks):
            pe.wait_ge(t_free, n - 1)
            for c in range(blocks):
                mm = pe.transpose(bank[:, c * P:(c + 1) * P], src(c), ident[:, :])
            mm.then_inc(t_ready, 1)

        def d_tile_set(pe, h, par, b):
            pe.wait_ge(p_ready, h * 4 + (AB_TILES + b + 1))
            pe_set_at(pe, set_d(h, b), t_bank[set_d_par(par, b, is_last(h))], lambda x: pn[:, b % 2, x * P:(x + 1) * P], TB)

        def pe_pv_d(pe, h, par):
            pe.wait_ge(t_free, set_d(h, 3) + 1)
            pe.wait_ge(o_copied, h + PV_D)
            for kc in range(TB):
                mm = three(pe, o_bank[0:HD, :], v_d[:, par, 0, kc, :], v_d[:, par, 1, kc, :],
                           pt_d[:, par, 0, kc, :], pt_d[:, par, 1, kc, :], kc == 0, kc == TB - 1)
            mm.then_inc(pv_done, 1)

        def pe_head_d(pe, h, par):
            first, last = isinstance(h, int) and h == 0, is_last(h)
            nslot = (U_D + par + 1) % 2
            pe.wait_ge(qk_lo, h * 2 + (QK_D + 2))
            for b in range(TB):
                s = h * 4 + (S_D + b)
                bank = s_bank[(S_D + b) % 2]
                pe.wait_ge(exp_done, s - 1)
                cols = slice(b * P, (b + 1) * P)
                three(pe, bank[:, :], q_d[:, par, 0, cols], q_d[:, par, 1, cols], k_d[:, par, 0, :], k_d[:, par, 1, :],
                      True, True).then_inc(s_ready, 1)
                if not last:
                    for kc in (range(QC), range(QC, D_TILES), (), ())[b]:
                        d_step_at(pe, h + 1, kc, nslot)
                else:
                    for m, kc in (AHEAD[0:3], AHEAD[3:5], (), AHEAD[5:7])[b]:
                        wo_tile(pe, 1, m, m, kc)
                if b == 0 and not first:
                    d_tile_set(pe, h - 1, 1 - par, 3)
                if b == 2 and not first:
                    pe_pv_d(pe, h - 1, 1 - par)
                if b == 3 and not last:
                    pe.wait_ge(proj_t, h * 2 + (PROJ_D + 4))
                    pe_set_at(pe, set_d(h, -1), t_bank[set_d_par(par, -1)], lambda x: tq[:, 1, x * P:(x + 1) * P], TB)
                if b >= 1:
                    d_tile_set(pe, h, par, b - 1)

        def act_evac_c(act, u):
            prep_hi(act, u + 2, u % 2, tiles_of(u + 2))
            if kind_c(u) != "v":
                j = u - U_C
                act.wait_ge(proj_t, T_AB + j + 1)
                act.activation(qk_dst_c(u)[0], tq_c[j % 2], ACT.Copy).then_inc(qk_hi, 1)

        def qk_dst_c(u):
            slot = ((u - U_C) // 3) % 2
            if kind_c(u) == "q":
                return q_c[:, slot, 0, :], q_c[:, slot, 1, :]
            return k_c[:, slot, 0, HD:HD + T], k_c[:, slot, 1, HD:HD + T]

        def act_layer1(act):
            for j in range(3):
                act_evac_c(act, U_C + j)
            for t in range(len(C_TILE_LIST)):
                c, g, hd, blocks = c_tile(t)
                act.wait_ge(scored, S_C + t + 1)
                w = (2 if g == 0 else 1) * P
                for i, b in enumerate(blocks):
                    ins = act.activation(sc[:, t % 2, i * w:(i + 1) * w], sc[:, t % 2, i * w:(i + 1) * w], ACT.Exp, scale=-1.0,
                                         bias=stats_v[:, c // 3, 0, g, hd, b:b + 1],
                                         accum_out=stats_v[:, c // 3, 1, g, hd, b:b + 1])
                ins.then_inc(exp_done, 1)
                for u in c_done_units(t):
                    act_evac_c(act, u)
                if t >= 1:
                    act_o_c(act, t - 1)
                if C_TILE_LIST[t][1] == 0:
                    act_set(act, c_sets["v", c, 0], v_c[:, c % 2, 0, 0:TB, :], bank3(t_bank[c_sets["v", c, 0] % 2], TB))
                    if g == 0:
                        act_set(act, c_sets["v", c, 1], v_c[:, c % 2, 0, TB, :], t_bank[c_sets["v", c, 1] % 2][:, 0:P])
                act.wait_ge(pv_done, PV_C + t - 1)
                act_set(act, c_sets["t", t], pt_c[t % 2][0], t_bank[c_sets["t", t] % 2][:, :])
                if t == C_TILE_AT[3]:
                    act_comb_exp(act, 0)
                if t == C_TILE_AT[4] - 1:
                    act_oc_c(act, 0)
            act_o_c(act, len(C_TILE_LIST) - 1)
            for c in range(N_LAT):
                u = U_LAT + c
                prep_hi(act, u + 2, u % 2, tiles_of(u + 2))
                if c < QC + KVC:
                    act.wait_ge(unit_done, u + 1)
                    dst = lat_sq_dst(c)
                    if c == QC:
                        act.wait_ge(mix_done, 6)
                    if c == 2:
                        act.wait_ge(lat_add, 1)
                    act.activation(dst, g_bank[(u - U_C) % 2][:, :], ACT.Square).then_inc(lat_sq, 1)
                    act.wait_ge(proj_t, T_AB + u - U_C + 1)
                    act.activation(lat[:, 0, c, :], tq_c[(u - U_C) % 2], ACT.Copy).then_inc(qk_hi, 1)
                if c == 0:
                    act_comb_exp(act, 1)
                if c == 4:
                    act_oc_c(act, 1)
            act.wait_ge(kpe_ready, 1)
            for slot in range(2):
                ins = act.activation(k_d[:, slot, 0, :], og[:, 1, :], ACT.Copy)
            ins.then_inc(qk_hi, 1)

            act_q_d(act, 0, 0)
            act_kv_d(act, 0, 0)
            prep_hi(act, U_D + 2, (U_D + 2) % 2, D_TILES)
            act_set(act, SET_D, v_d[:, 0, 0, :, :], bank3(t_bank[SET_D % 2], TB)[:, :, HD:P])
            act_head_d(act, 0, 0)
            act_head_d(act, 1, 1)
            with act.Fori(1, D_HEADS // 2 - 2) as i:
                for par in range(2):
                    act_head_d(act, i * 2 + par, par, i)
            for h in range(D_HEADS - 4, D_HEADS):
                act_head_d(act, h, h % 2)
            last = D_HEADS - 1
            act_pt_d(act, last, 1, 2)
            act_pt_d(act, last, 1, 3)
            act_o_d(act, last, 1, D_HEADS // 2 - 1)
            act_wo(act, 1)
            act_ffn(act, 1)

        def lat_sq_dst(c):
            return (sc[:, 1, :], sc[:, 0, :], sc[:, 0, :], og[:, 2, :], og[:, 1, :])[c]

        def act_comb_exp(act, p):
            act.wait_ge(comb_diff, p + 1)
            act.activation(comb_w[:, 0:24], comb_w[:, 0:24], ACT.Exp).then_inc(comb_exp, 1)

        def act_oc_c(act, p):
            act.wait_ge(mix_done, 3 * (p + 1))
            act.activation(oc[:, 0, p, :], mix[:, :], ACT.Copy).then_inc(oc_hi, 1)

        def act_o_c(act, t):
            c, g, hd, blocks = c_tile(t)
            p = c // 3
            act.wait_ge(pv_done, PV_C + t + 1)
            if p == 1:
                act.wait_ge(mix_done, g + 1)
            rows = slice(hd * HD, (hd + 1) * HD)
            if g == 0:
                cols = slice(blocks[0] * P, blocks[0] * P + 2 * P)
                act.activation(og[rows, 0, cols], o_bank[0:HD, cols], ACT.Copy).then_inc(o_copied, 1)
            else:
                act.activation(og[rows, g, :].rearrange("p (l s) -> p s l", s=4),
                               o_bank[0:HD, :].rearrange("p (s l) -> p s l", s=4), ACT.Copy).then_inc(o_copied, 1)

        def act_q_d(act, h, par):
            act.wait_ge(proj_t, h * 2 + (PROJ_D + 1))
            act.activation(q_d[:, par, 0, :], tq[:, 0, 0:T], ACT.Copy).then_inc(qk_hi, 1)

        def act_kv_d(act, h, par):
            act.wait_ge(proj_t, h * 2 + (PROJ_D + 2))
            act.activation(k_d[0:HD, par, 0, :], tq[0:HD, 1, 0:T], ACT.Copy).then_inc(qk_hi, 1)

        def act_pt_d(act, h, par, b):
            n = set_d(h, b)
            bank = t_bank[set_d_par(par, b, is_last(h))]
            act.wait_ge(t_ready, n + 1)
            act.activation(pt_d[:, par, 0, :, b * P:(b + 1) * P], bank3(bank, TB), ACT.Copy).then_inc(pt_hi, 1)

        def act_o_d(act, h, par, i=None):
            act.wait_ge(pv_done, h + (PV_D + 1))
            if par == 0:
                act.wait_ge(oc_lo, (10 + h // 2) if isinstance(h, int) else i + 10)
            act.activation(og[par * HD:(par + 1) * HD, 0, :], o_bank[0:HD, :], ACT.Copy).then_inc(o_copied, 1)
            if par:
                act.wait_ge(o_copied, h + (PV_D + 1))
                if isinstance(i, int):
                    dst = oc[:, 0, 2 + i, :]
                else:
                    act.nop(nofuse=True)
                    dst = oc[:, 0, bass.ds(i + 2, 1), :].rearrange("p a t -> p (a t)")
                act.activation(dst, og[:, 0, :], ACT.Copy).then_inc(oc_hi, 1)

        def act_head_d(act, h, par, i=None):
            first, last = isinstance(h, int) and h == 0, is_last(h)
            for b in range(TB):
                s = h * 4 + (S_D + b)
                c = (S_D + 4 * par + b) % 8
                if b < 2 and not first:
                    act_pt_d(act, h - 1, 1 - par, 2 + b)
                if b >= 2:
                    if b == 2 and not (isinstance(h, int) and h < 2):
                        act.wait_ge(pv_done, h + (PV_D - 1))
                    act_pt_d(act, h, par, b - 2)
                act.wait_ge(scored, s + 1)
                act.activation(sc[:, b, :], s_bank[(S_D + b) % 2][:, :], ACT.Exp, bias=neg_max[:, c:c + 1],
                               accum_out=row_sum[:, c:c + 1]).then_inc(exp_done, 1)
                if b == 1 and not last:
                    act_q_d(act, h + 1, 1 - par)
                if b == 2 and not last:
                    act_kv_d(act, h + 1, 1 - par)
                    u = h + (U_D + 3)
                    static = isinstance(h, int)
                    tiles = KC if static and h + 3 >= D_HEADS else D_TILES
                    prep_hi(act, u, (U_D + par + 3) % 2, tiles, None if static else i + (U_D + par + 3) // 2)
                if b == 3 and not first:
                    j = (h - 1) // 2 if isinstance(h, int) else (i - 1 if par == 0 else i)
                    act_o_d(act, h - 1, 1 - par, j)
                if b == 3 and not last:
                    n = set_d(h, -1)
                    act.wait_ge(t_ready, n + 1)
                    act.activation(v_d[:, 1 - par, 0, :, :], bank3(t_bank[set_d_par(par, -1)], TB)[:, :, HD:P],
                                   ACT.Copy).then_inc(pt_hi, 1)

        def pool_evac_c(pool, u):
            prep_lo(pool, u + 2, u % 2, tiles_of(u + 2))
            if kind_c(u) != "v":
                i = qk_index_c(u)
                pool.wait_ge(qk_hi, i + 1)
                hi, lo = qk_dst_c(u)
                pool.tensor_tensor(lo, tq_c[(u - U_C) % 2], hi.bitcast(F32), ALU.subtract).then_inc(qk_lo, 1)

        def pool_layer1(pool):
            pool_root(pool, NORM_AT[2])
            for j in range(3):
                pool_evac_c(pool, U_C + j)
            for t in range(len(C_TILE_LIST)):
                for u in c_done_units(t):
                    pool_evac_c(pool, u)
                if t == C_TILE_AT[4] - 1:
                    pool_oc_lo_c(pool, 0)
            for c in range(N_LAT):
                u = U_LAT + c
                prep_lo(pool, u + 2, u % 2, tiles_of(u + 2))
                if c in (1, 2):
                    pool.wait_ge(lat_sq, c + 1)
                    if c == 2:
                        pool.wait_ge(lat_add, 1)
                    pool.tensor_tensor(sc[:, 1, :], sc[:, 1, :], sc[:, 0, :], ALU.add).then_inc(lat_add if c == 1 else lat_acc, 1)
                if c == 4:
                    pool.wait_ge(lat_sq, 5)
                    pool.wait_ge(lat_acc, 1)
                    pool.tensor_tensor(sc[:, 0, :], og[:, 2, :], og[:, 1, :], ALU.add).then_inc(lat_acc, 1)
                if c < QC + KVC:
                    pool.wait_ge(qk_hi, QK_LAT + c + 1)
                    pool.tensor_tensor(lat[:, 1, c, :], tq_c[(u - U_C) % 2], lat[:, 0, c, :].bitcast(F32),
                                       ALU.subtract).then_inc(qk_lo, 1)
                if c == 4:
                    pool_oc_lo_c(pool, 1)
                if c == 5:
                    pool_root(pool, 7)
            pool.wait_ge(qk_hi, QK_D)
            for slot in range(2):
                ins = pool.tensor_tensor(k_d[:, slot, 1, :], og[:, 1, :], k_d[:, slot, 0, :].bitcast(F32), ALU.subtract)
            ins.then_inc(qk_lo, 1)
            pool_root(pool, 8)
            pool_qk_d(pool, 0, 0)
            prep_lo(pool, U_D + 2, (U_D + 2) % 2, D_TILES)
            pool_head_d(pool, 0, 0)
            pool_head_d(pool, 1, 1)
            with pool.Fori(1, D_HEADS // 2 - 2) as i:
                for par in range(2):
                    pool_head_d(pool, i * 2 + par, par, i)
            for h in range(D_HEADS - 4, D_HEADS):
                pool_head_d(pool, h, h % 2)
            pool_oc_lo(pool, D_HEADS // 2 + 1, og[:, 0, :], 8)
            pool_wo(pool, 1)
            pool_ffn(pool, 1)
            pool_root(pool, NORM_AT[4])

        def pool_oc_lo_c(pool, p):
            pool_oc_lo(pool, p, mix[:, :], 8)

        def pool_qk_d(pool, h, par):
            pool.wait_ge(qk_hi, h * 2 + (QK_D + 1))
            pool.tensor_tensor(q_d[:, par, 1, :], tq[:, 0, 0:T], q_d[:, par, 0, :].bitcast(F32), ALU.subtract).then_inc(qk_lo, 1)
            pool.wait_ge(qk_hi, h * 2 + (QK_D + 2))
            pool.tensor_tensor(k_d[0:HD, par, 1, :], tq[0:HD, 1, 0:T], k_d[0:HD, par, 0, :].bitcast(F32),
                               ALU.subtract).then_inc(qk_lo, 1)

        def pool_head_d(pool, h, par, i=None):
            static = isinstance(h, int)
            if not is_last(h):
                pool_qk_d(pool, h + 1, 1 - par)
                tiles = KC if static and h + 3 >= D_HEADS else D_TILES
                prep_lo(pool, h + (U_D + 3), (U_D + par + 3) % 2, tiles)
            if par == 0 and not (static and h == 0):
                if static:
                    pool_oc_lo(pool, 1 + h // 2, og[:, 0, :], 8)
                else:
                    pool.wait_ge(oc_hi, i + (8 + 2))
                    dst = oc[:, 1, bass.ds(i + 1, 1), :].rearrange("p a t -> p (a t)")
                    src = oc[:, 0, bass.ds(i + 1, 1), :].rearrange("p a t -> p (a t)")
                    pool.nop(nofuse=True)
                    pool.tensor_tensor(dst, og[:, 0, :], src.bitcast(F32), ALU.subtract).then_inc(oc_lo, 1)

        def dve_evac_c(dve, u):
            j = u - U_C
            dve.wait_ge(unit_done, u + 1)
            if j >= 2 and kind_c(u - 2) != "v":
                dve.wait_ge(qk_lo, qk_index_c(u - 2) + 1)
            scale = HD ** -0.5 if kind_c(u) == "q" else 1.0
            dve.scalar_tensor_tensor(tq_c[j % 2], g_bank[j % 2][:, :], scale, rstd[:, :], ALU.mult, ALU.mult).then_inc(proj_t, 1)

        def dve_comb(dve, p, step):
            if step == 0:
                dve.wait_ge(comb_mm, p + 1)
                if p == 1:
                    dve.wait_ge(mix_done, 3)
                m = m_bank[:, 0:P].rearrange("p (g x b) -> p g x b", g=2, b=TB)
                dve.tensor_tensor(picked[:, :].rearrange("p (g x b) -> p g x b", g=2, b=TB), m,
                                  masks[:, :].unsqueeze(1).unsqueeze(1).broadcast_to([P, 2, 16, TB]),
                                  ALU.mult).then_inc(comb_step, 1)
                dve.wait_ge(comb_step, 7 * p + 1)
                for g in (1, 2):
                    out = nat[:, :].rearrange("p (s g h b) -> p g b s h", s=2, g=3, h=2)[:, g]
                    dve.tensor_reduce(out, picked[:, (g - 1) * HD:g * HD].rearrange("p (c s h b) -> p c s h b", c=TB, s=2, h=2),
                                      AX.X, ALU.add)
                dve.tensor_copy(nat_v[:, :, 0, :], stats[:, :].rearrange("p (r s g x) -> p r s g x", r=2, s=2, g=3)[:, p, :, 0, :]).then_inc(comb_step, 1)
                dve.wait_ge(comb_step, 7 * p + 2)
                dve.tensor_reduce(least[:, 0:8], nat_v[:, 0].rearrange("p g x -> p x g"), AX.X, ALU.min).then_inc(comb_step, 1)
                dve.wait_ge(comb_step, 7 * p + 3)
                w3 = comb_w[:, 0:24].rearrange("p (g x) -> p g x", g=3)
                dve.tensor_tensor(w3, least[:, 0:8].unsqueeze(1).broadcast_to([P, 3, 8]), nat_v[:, 0], ALU.subtract).then_inc(comb_diff, 1)
                dve.wait_ge(comb_exp, p + 1)
                dve.tensor_tensor(nat_v[:, 0], w3, nat_v[:, 1], ALU.mult).then_inc(comb_step, 1)
                dve.wait_ge(comb_step, 7 * p + 4)
                dve.tensor_reduce(least[:, 8:16], nat_v[:, 0].rearrange("p g x -> p x g"), AX.X, ALU.add).then_inc(comb_step, 1)
                dve.wait_ge(comb_step, 7 * p + 5)
                dve.reciprocal(least[:, 0:8], least[:, 8:16]).then_inc(comb_step, 1)
                dve.wait_ge(comb_step, 7 * p + 6)
                dve.tensor_tensor(w3, w3, least[:, 0:8].unsqueeze(1).broadcast_to([P, 3, 8]), ALU.mult).then_inc(comb_step, 1)
                dve.wait_ge(comb_step, 7 * p + 7)
            for hd in range(2):
                if step >= 1:
                    dve.wait_ge(comb_bc, 3 * p + step)
                at = 8 * step + 4 * hd
                dve.tensor_tensor(sc[:, 2 + hd, :].rearrange("p (b t) -> p b t", b=TB),
                                  ident[:, :].unsqueeze(1).broadcast_to([P, TB, P]),
                                  comb_w[:, at:at + 4].unsqueeze(2).broadcast_to([P, TB, P]), ALU.mult).then_inc(comb_diag, 1)
            dve.wait_ge(comb_bc, 3 * p + step + 1)
            dve.wait_ge(o_copied, PV_C + C_TILE_AT[3 * p + 3])
            if step == 0:
                if p == 1:
                    dve.wait_ge(oc_lo, 9)
                dve.tensor_tensor(mix[:, :], og[:, 0, :], m_bank[:, :], ALU.mult).then_inc(mix_done, 1)
            else:
                dve.tensor_tensor(og[:, step, :], og[:, step, :], m_bank[:, :], ALU.mult).then_inc(mix_part, 1)
                dve.wait_ge(mix_part, 2 * p + step)
                dve.wait_ge(mix_done, 3 * p + step)
                dve.tensor_tensor(mix[:, :], mix[:, :], og[:, step, :], ALU.add).then_inc(mix_done, 1)

        def dve_bias_c(dve, e):
            g, slot = (e // 2) % 3, e % 2
            dve.wait_ge(bias_loaded[slot], 16 * c_bias_count(e))
            if g == 0:
                dve.memset(bias[:, slot, 0:HD], NEG)
                dve.memset(bias[:, slot, 1024 - HD:1024], NEG).then_inc(edges_closed, 1)
                dve.wait_ge(edges_closed, {0: 1, 1: 2, 6: 3, 7: 4}[e])

        def dve_layer1(dve):
            dve_rstd(dve, NORM_AT[2])
            dve.tensor_tensor(r_sq[:, :], inv_rms[:, :], inv_rms[:, :], ALU.mult)
            for par in range(2):
                dve.memset(tq[:, par, 0:HD], 0.0)
                dve.memset(tq[:, par, HD + T:P + T], 0.0)
                for x in range(2):
                    dve.memset(k_c[:, par, x, 0:HD].bitcast(F32), 0.0)
                    ins = dve.memset(k_c[:, par, x, HD + T:P + T].bitcast(F32), 0.0)
            ins.then_inc(k_pads_zeroed, 1)
            for j in range(3):
                dve_evac_c(dve, U_C + j)
            for t in range(len(C_TILE_LIST)):
                c, g, hd, blocks = c_tile(t)
                e = 2 * c + hd
                if blocks[0] == 0:
                    dve_bias_c(dve, e)
                dve.wait_ge(s_ready, S_C + t + 1)
                w = (2 if g == 0 else 1) * P
                for i, b in enumerate(blocks):
                    table = bias[:, e % 2, b * w:(b + 1) * w] if g == 0 else bias[:, e % 2, 0:P]
                    ins = dve.tensor_tensor_reduce(out=sc[:, t % 2, i * w:(i + 1) * w], in0=s_bank[(S_C + t) % 2][:, i * w:(i + 1) * w],
                                                   in1=table, scale=-1.0, scalar=BIG, op0=ALU.add, op1=ALU.min,
                                                   accum_out=stats_v[:, c // 3, 0, g, hd, b:b + 1])
                ins.then_inc(scored, 1)
                for u in c_done_units(t):
                    dve_evac_c(dve, u)
                if C_TILE_LIST[t][1] == 0:
                    k = c_sets["v", c, 0]
                    dve_set(dve, k, v_c[:, c % 2, 1, 0:TB, :], bank3(t_bank[k % 2], TB), v_c[:, c % 2, 0, 0:TB, :])
                    if g == 0:
                        k = c_sets["v", c, 1]
                        dve_set(dve, k, v_c[:, c % 2, 1, TB, :], t_bank[k % 2][:, 0:P], v_c[:, c % 2, 0, TB, :])
                k = c_sets["t", t]
                dve_set(dve, k, pt_c[t % 2][1], t_bank[k % 2][:, :], pt_c[t % 2][0])
                if C_TILE_AT[3] <= t < C_TILE_AT[3] + 3:
                    dve_comb(dve, 0, t - C_TILE_AT[3])
            for c in range(N_LAT):
                u = U_LAT + c
                j = u - U_C
                bank = g_bank[j % 2]
                dve.wait_ge(unit_done, u + 1)
                if c < QC + KVC:
                    dve.wait_ge(lat_sq, c + 1)
                    if c >= 2:
                        dve.wait_ge(qk_lo, QK_LAT + c - 1)
                    elif kind_c(u - 2) != "v":
                        dve.wait_ge(qk_lo, qk_index_c(u - 2) + 1)
                    dve.scalar_tensor_tensor(tq_c[j % 2], bank[:, :], gains[:, G_QN + c:G_QN + c + 1], rstd[:, :],
                                             ALU.mult, ALU.mult).then_inc(proj_t, 1)
                else:
                    dve.wait_ge(qk_lo, QK_LAT + c - 1)
                    dve.tensor_tensor(tq_c[j % 2], bank[:, :], rstd[:, :], ALU.mult).then_inc(proj_t, 1)
                    dve.wait_ge(rotary_loaded, 16)
                    dve.wait_ge(proj_t, T_AB + j + 1)
                    table = bias[:, 0, T:2 * T] if c == 5 else bias[:, 1, 0:T]
                    dve.tensor_tensor(tq_c[j % 2], tq_c[j % 2], table, ALU.mult).then_inc(kr_part, 1)
                if c < 3:
                    dve_comb(dve, 1, c)
                if c == 5:
                    dve_lat_mean(dve, 0, QC * P)
                    dve_diag(dve, 7, sc[:, 2, :])
                    dve.wait_ge(bc_ready, 8)
                    dve.tensor_tensor(bias[:, 0, 0:T], bias[:, 0, 0:T], m_bank[:, :], ALU.mult).then_inc(bc_used, 1)
            dve.wait_ge(kr_part, 2)
            dve.tensor_tensor(og[:, 1, :], tq_c[0], tq_c[1], ALU.add).then_inc(kpe_ready, 1)
            dve_lat_mean(dve, 1, KVC * P)
            dve_diag(dve, 8, sc[:, 2, :])
            dve.wait_ge(bc_ready, 9)
            dve.tensor_copy(rstd[:, :], m_bank[:, :]).then_inc(bc_used, 1)
            dve.wait_ge(bc_used, 9)
            dve_q_d(dve, 0)
            dve_kv_d(dve, 0)
            dve.wait_ge(pt_hi, SET_D + 1)
            dve.tensor_tensor(v_d[:, 0, 1, :, :], bank3(t_bank[SET_D % 2], TB)[:, :, HD:P], v_d[:, 0, 0, :, :].bitcast(F32),
                              ALU.subtract).then_inc(t_free, 1)
            dve_head_d(dve, 0, 0)
            dve_head_d(dve, 1, 1)
            with dve.Fori(1, D_HEADS // 2 - 2) as i:
                for par in range(2):
                    dve_head_d(dve, i * 2 + par, par)
            for h in range(D_HEADS - 4, D_HEADS):
                dve_head_d(dve, h, h % 2)
            last = D_HEADS - 1
            dve_norm_d(dve, last, 1, 3)
            dve_pt_d(dve, last, 1, 2)
            dve_pt_d(dve, last, 1, 3)
            dve_wo(dve, 1)
            dve_ffn(dve, 1)
            n = NORM_AT[4]
            dve_mean(dve, n, DM)
            dve_diag(dve, n, sc[:, 2, :])
            dve.wait_ge(bc_ready, n + 1)
            for m in range(KC):
                dve.scalar_tensor_tensor(xT[:, m, :], xT[:, m, :], gains[:, G_FINAL + m:G_FINAL + m + 1], m_bank[:, :],
                                         ALU.mult, ALU.mult).then_inc(final_ready, 1)

        def dve_lat_mean(dve, i, count):
            n = 7 + i
            dve.wait_ge(stat_ready, n + 1)
            dve.scalar_tensor_tensor(mean_sq[:, :], m_bank[:, 0:TB], 1.0 / count, r_sq[:, :], ALU.mult, ALU.mult).then_inc(lat_mean, 1)
            dve.wait_ge(lat_mean, i + 1)
            dve.tensor_scalar(mean_sq[:, :], mean_sq[:, :], EPS, None, ALU.add).then_inc(ms_ready, 1)

        def dve_q_d(dve, h):
            dve.wait_ge(q_done, h + 1)
            dve.wait_ge(qk_lo, h * 2 + (QK_D - 1))
            dve.tensor_tensor(tq[:, 0, 0:T], g_bank[0][:, :], bias[:, 0, 0:T], ALU.mult).then_inc(proj_t, 1)

        def dve_kv_d(dve, h):
            dve.wait_ge(unit_done, h + (U_D + 1))
            dve.wait_ge(qk_lo, h * 2 + QK_D)
            dve.tensor_tensor(tq[:, 1, 0:T], g_bank[1][:, :], rstd[:, :], ALU.mult).then_inc(proj_t, 1)

        def dve_pt_d(dve, h, par, b):
            n = set_d(h, b)
            bank = t_bank[set_d_par(par, b, is_last(h))]
            cols = slice(b * P, (b + 1) * P)
            dve.wait_ge(pt_hi, n + 1)
            dve.tensor_tensor(pt_d[:, par, 1, :, cols], bank3(bank, TB), pt_d[:, par, 0, :, cols].bitcast(F32),
                              ALU.subtract).then_inc(t_free, 1)

        def dve_norm_d(dve, h, par, b):
            s = h * 4 + (S_D + b)
            n = h * 4 + (AB_TILES + b)
            c = (S_D + 4 * par + b) % 8
            dve.wait_ge(exp_done, s + 1)
            dve.reciprocal(inv_sum[:, c:c + 1], row_sum[:, c:c + 1]).then_inc(recip_done, 1)
            dve.wait_ge(recip_done, n + 1)
            dve.tensor_scalar(pn[:, b % 2, :], sc[:, b, :], inv_sum[:, c:c + 1], None, ALU.mult).then_inc(p_ready, 1)

        def dve_head_d(dve, h, par):
            first, last = isinstance(h, int) and h == 0, is_last(h)
            for b in range(TB):
                s = h * 4 + (S_D + b)
                c = (S_D + 4 * par + b) % 8
                if b >= 1:
                    dve_norm_d(dve, h, par, b - 1)
                elif not first:
                    dve_norm_d(dve, h - 1, 1 - par, 3)
                dve.wait_ge(s_ready, s + 1)
                dve.tensor_reduce(neg_max[:, c:c + 1], s_bank[(S_D + b) % 2][:, :], AX.X, ALU.max, negate=True).then_inc(scored, 1)
                if b < 2 and not first:
                    dve_pt_d(dve, h - 1, 1 - par, 2 + b)
                if b >= 2:
                    dve_pt_d(dve, h, par, b - 2)
                if b == 1 and not last:
                    dve_q_d(dve, h + 1)
                if b == 2 and not last:
                    dve_kv_d(dve, h + 1)
                if b == 3 and not last:
                    k = set_d(h, -1)
                    dve.wait_ge(pt_hi, k + 1)
                    dve.tensor_tensor(v_d[:, 1 - par, 1, :, :], bank3(t_bank[set_d_par(par, -1)], TB)[:, :, HD:P],
                                      v_d[:, 1 - par, 0, :, :].bitcast(F32), ALU.subtract).then_inc(t_free, 1)

        @block.sync
        def _(sp):
            sync_program(sp)

        @block.gpsimd
        def _(pool):
            gpsimd_program(pool)

        @block.scalar
        def _(act):
            scalar_program(act)

        @block.vector
        def _(dve):
            vector_program(dve)

        @block.tensor
        def _(pe):
            tensor_program(pe)

def t5_bucket(rel):
    nb = NB // 2
    max_exact = nb // 2
    n = np.abs(rel)
    nf = np.maximum(n, 1).astype(np.float32)
    large = max_exact + (np.log(nf / np.float32(max_exact)) / np.float32(math.log(MAX_DISTANCE / max_exact))
                         * np.float32(nb - max_exact)).astype(np.int32)
    large = np.minimum(large, nb - 1)
    return np.where(rel > 0, nb, 0) + np.where(n < max_exact, n, large)

def one_hot_table():
    table = np.zeros((NB + 1, VEC_LEN), np.float32)
    for (length, dilation, widest, _, _), at, centre in zip(VECS, VEC_AT, VEC_CENTRE):
        rel = np.arange(length) - centre
        row = np.where(np.abs(rel) <= widest, t5_bucket(rel * dilation), NB)
        if at == VEC_AT[4]:
            row = np.where(rel % 4 == 0, row, NB)
        table[row, at + np.arange(length)] = 1.0
    return table

def rotary_tables():
    half = D_ROPE // 2
    inv = np.float32(10000.0) ** (-np.arange(half, dtype=np.float32) / np.float32(half))
    angle = np.arange(T, dtype=np.float32)[:, None] * inv[None, :]
    cos, sin = np.cos(angle).T, np.sin(angle).T
    cos2, sin2 = np.concatenate([cos, cos]), np.concatenate([-sin, sin])
    scale = np.float32((D_NOPE + D_ROPE) ** -0.5)
    q_mult = np.concatenate([np.ones((D_NOPE, T), np.float32), cos2, sin2]) * scale
    k_cos = np.concatenate([cos2] * 4)
    k_sin = np.concatenate([sin2] * 4)
    return np.ascontiguousarray(np.stack([q_mult, k_cos, k_sin], axis=1).astype(np.float32))

def comb_select():
    select = np.zeros((P, TB, P), np.float32)
    masks = np.zeros((P, TB), np.float32)
    p = np.arange(P)
    for b in range(TB):
        select[(P * b + p) // 4, b, p] = 1.0
    masks[p, p % 4] = 1.0
    return select.reshape(P, TB * P), masks

def panels(w, cols=None):
    if cols is not None:
        w = w[:, cols]
    k, m = w.shape
    return np.ascontiguousarray(w.reshape(k // P, P, m // P, P).transpose(2, 1, 0, 3).reshape(m // P, P, k))

def kernel(x, bias_table, attn_norm, ffn_norm, final_norm, ab_w_in, ab_lambda_q1, ab_lambda_k1,
           ab_lambda_q2, ab_lambda_k2, ab_subln, ab_sink, ab_w_o, cd_w_in, cd_q_norm, cd_w_q_b,
           cd_kv_norm, cd_w_kv_b, cd_w_o, ffn_w_gate, ffn_w_up, ffn_w_down):
    import concourse.bacc as bacc
    from concourse.bass_utils import run_bass_kernel_spmd

    (x, bias_table, attn_norm, ffn_norm, final_norm, ab_w_in, ab_subln, ab_sink, ab_w_o, cd_w_in, cd_q_norm, cd_w_q_b,
     cd_kv_norm, cd_w_kv_b, cd_w_o, ffn_w_gate, ffn_w_up, ffn_w_down) = map(np.asarray, (
         x, bias_table, attn_norm, ffn_norm, final_norm, ab_w_in, ab_subln, ab_sink, ab_w_o, cd_w_in, cd_q_norm,
         cd_w_q_b, cd_kv_norm, cd_w_kv_b, cd_w_o, ffn_w_gate, ffn_w_up, ffn_w_down))

    ar = np.arange
    o1, o2, o3 = 512, 1024, 1536
    o4, o5 = o3 + 512, o3 + 512 + 128
    cols = [o + h * P + ar(P) for h in range(A_HEADS) for o in (0, o1, o2)]
    cols += [o4 + ar(P), o5 + ar(P)]
    cols += [o3 + np.concatenate([j * HD + ar(HD), (j + 4) * HD + ar(HD)]) for j in range(4)]
    w_ab = panels(ab_w_in[0], np.concatenate(cols))
    rows = np.concatenate([ar(512)] + [512 + np.concatenate([j * HD + ar(HD), (j + 4) * HD + ar(HD)]) for j in range(4)])
    w_o0 = panels(ab_w_o[0][rows])

    cols = [o + (2 * g + p) * P + ar(P) for p in range(2) for g in range(3) for o in (0, 768, 1536)]
    cols += [2304 + c * P + ar(P) for c in range(QC + KVC)]
    kr = 2304 + (QC + KVC) * P + ar(D_ROPE)
    kr_swapped = np.roll(kr, D_ROPE // 2)
    cols += [np.tile(kr, 4), np.tile(kr_swapped, 4)]
    w_c = panels(cd_w_in[0], np.concatenate(cols))
    per = D_NOPE + D_ROPE
    qcols = np.concatenate([h * per + np.concatenate([ar(per), D_NOPE + np.roll(ar(D_ROPE), D_ROPE // 2)])
                            for h in range(D_HEADS)])
    w_d = np.ascontiguousarray(np.concatenate([panels(cd_w_q_b[0], qcols), panels(cd_w_kv_b[0])], axis=2))
    w_o1 = panels(cd_w_o[0])

    arrays = {
        "x_t": np.ascontiguousarray(x[0].T.reshape(KC, P, T).transpose(1, 0, 2)),
        "bias_table": bias_table,
        "one_hot": one_hot_table(),
        "rotary": rotary_tables(),
        "comb_select": comb_select()[0],
        "comb_masks": comb_select()[1],
        "gains": np.ascontiguousarray(np.concatenate(
            [g.reshape(-1, P).T for g in (attn_norm[0], ffn_norm[0], attn_norm[1], ffn_norm[1], final_norm,
                                          cd_q_norm[0], cd_kv_norm[0], ab_subln[0])], axis=1)),
        "sink": ab_sink[0],
        "lambdas": np.concatenate([np.asarray(a)[0] for a in (ab_lambda_q1, ab_lambda_k1, ab_lambda_q2, ab_lambda_k2)]),
        "w_ab": w_ab, "w_o0": w_o0, "w_c": w_c, "w_d": w_d, "w_o1": w_o1,
    }
    for layer in range(2):
        gate, up = panels(ffn_w_gate[layer]), panels(ffn_w_up[layer])
        arrays[f"w_gu{layer}"] = np.ascontiguousarray(np.stack([gate, up], axis=1).reshape(2 * FC, P, DM))
        down = panels(ffn_w_down[layer])
        arrays[f"w_dn{layer}"] = np.ascontiguousarray(
            down.reshape(KC, P, 2, DOWN_HALF * P).transpose(0, 2, 1, 3).reshape(2 * KC, P, DOWN_HALF * P))

    nc = bacc.Bacc("TRN2", target_bir_lowering=False, num_devices=1)
    arrays = {f"in_{n}": a for n, a in arrays.items()}
    io = {n[3:]: nc.dram_tensor(n, a.shape, mybir.dt.from_np(a.dtype), kind="ExternalInput").ap() for n, a in arrays.items()}
    io["out"] = nc.dram_tensor("out", (P, KC, T), F32, kind="ExternalOutput").ap()
    build_program(nc, io)
    r = run_bass_kernel_spmd(nc, [arrays], core_ids=[0])
    out = np.asarray(r.results[0]["out"])
    return np.ascontiguousarray(out.transpose(1, 0, 2).reshape(DM, T).T)[None]
```

```python
import math
from contextlib import ExitStack

import numpy as np
import concourse.bass as bass
from concourse import mybir

F32 = mybir.dt.float32
F32R = mybir.dt.float32r
ALU = mybir.AluOpType
ACT = mybir.ActivationFunctionType
AX = mybir.AxisListType

P = 128
T = 512
DM = 1024
KC = DM // P
TB = T // P
D_FF = 2816
FC = D_FF // P
DOWN_HALF = FC // 2
HD = 64
EPS = 1e-6
NEG = -1e30
BIG = 3.0e38
NB = 32
NH_BIAS = 12
MAX_DISTANCE = 1024
A_HEADS, B_HEADS = 4, 8
D_HEADS, D_NOPE, D_ROPE = 12, 64, 32
QC, KVC = 3, 2
D_TILES = QC + KVC
LAMBDA_INIT = 0.8 - 0.6 * math.exp(-0.3 * 0)

A_UNITS = 3 * A_HEADS
U_KB, U_VB, U_QB = A_UNITS, A_UNITS + 1, A_UNITS + 2
N_AB = A_UNITS + 2 + 4
U_WO0 = N_AB
U_GU0 = U_WO0 + KC
U_DN0 = U_GU0 + 2 * FC
U_C = U_DN0 + 2 * KC
N_C = 18
U_LAT = U_C + N_C
N_LAT = QC + KVC + 2
U_D = U_LAT + N_LAT
U_WO1 = U_D + D_HEADS
U_GU1 = U_WO1 + KC
U_DN1 = U_GU1 + 2 * FC
U_END = U_DN1 + 2 * KC

VECS = ((1024, 1, 1 << 20, 0, 4), (512, 1, 128, 4, 8), (384, 1, 64, 0, 4), (256, 4, 64, 4, 4), (256, 4, 127, 8, 4))
VEC_CENTRE = (511, 255, 191, 127, 127)
VEC_AT = [sum(v[0] for v in VECS[:n]) for n in range(len(VECS))]
VEC_LEN = sum(v[0] for v in VECS)
REP_AT = [sum(P * v[0] * v[4] for v in VECS[:n]) for n in range(len(VECS))]
REP_LEN = sum(P * v[0] * v[4] for v in VECS)

G_ATTN0, G_FFN0, G_ATTN1, G_FFN1, G_FINAL, G_QN, G_KVN, G_SUB = 0, 8, 16, 24, 32, 40, 43, 45
G_COLS = 46

def build_program(nc, io):
    with ExitStack() as ctx:
        def sb(name, shape, dt=F32):
            return ctx.enter_context(nc.sbuf_tensor(name, shape, dt))

        def pb(name):
            return ctx.enter_context(nc.psum_tensor(name, [P, T], F32))

        def sem(name):
            return ctx.enter_context(nc.semaphore(name))

        vec_dram = nc.dram_tensor("bias_vectors", [NH_BIAS, VEC_LEN], F32, kind="Internal").ap()
        rep_dram = nc.dram_tensor("bias_rows", [REP_LEN], F32, kind="Internal").ap()

        xT = sb("xT", [P, KC, T])
        xg = sb("xg", [P, 2, KC, T], F32R)
        big = sb("big", [P, 2 * FC * T], F32R)
        raw = sb("raw", [P, 2, DOWN_HALF * P])
        w_hi = sb("w_hi", [P, 2, DOWN_HALF * P], F32R)
        w_lo = sb("w_lo", [P, 2, DOWN_HALF * P], F32R)
        rstd = sb("rstd", [P, T])
        sc = sb("sc", [P, 4, T])
        pn = sb("pn", [P, 2, T])
        tq = sb("tq", [P, 2, T + P])
        bias = sb("bias", [P, 2, 1024])
        og = sb("og", [P, 3, T])
        ident = sb("ident", [P, P])
        ones = sb("ones", [P, P])
        gains = sb("gains", [P, G_COLS])
        sub_gain = sb("sub_gain", [P, 1])
        tab = sb("tab", [NB + 1, NH_BIAS])
        sink = sb("sink", [P, B_HEADS])
        neg_sink = sb("neg_sink", [P, B_HEADS])
        lam = sb("lam", [P, 8])
        neg_half = sb("neg_half", [P, 4])
        mean_sq = sb("mean_sq", [P, 4])
        inv_rms = sb("inv_rms", [P, 4])
        neg_max = sb("neg_max", [P, 32])
        row_sum = sb("row_sum", [P, 32])
        inv_sum = sb("inv_sum", [P, 8])
        masks = sb("masks", [P, TB])
        stats = sb("stats", [P, 96])
        nat = sb("nat", [P, 48])
        picked = sb("picked", [P, P])
        least = sb("least", [P, 16])
        comb_w = sb("comb_w", [P, 24])
        r_sq = sb("r_sq", [P, TB])
        mix = sb("mix", [P, T])

        oc = big[:, 0:2 * KC * T].rearrange("p (s c t) -> p s c t", s=2, c=KC)
        hid = big[:, :].rearrange("p (s c t) -> p s c t", s=2, c=FC)

        def region(at, *dims):
            n = math.prod(dims)
            names = "abcde"[:len(dims)]
            pattern = f"p ({' '.join(names)}) -> p {' '.join(names)}"
            return big[:, at:at + n].rearrange(pattern, **dict(zip(names, dims)))

        R0 = 2 * KC * T
        q_ab = region(R0, 2, 2, T)
        k_ab = region(R0 + 2048, 2, 2, T)
        v_ab = region(R0 + 4096, 2, 2, TB, P)
        pt_ab = region(R0 + 6144, 2, 2, TB, T)

        g_bank = [pb("g0"), pb("g1")]
        s_bank = [pb("s0"), pb("s1")]
        t_bank = [pb("t0"), pb("t1")]
        o_bank = pb("o_bank")
        m_bank = pb("m_bank")

        raw_loaded = [sem("raw_loaded0"), sem("raw_loaded1")]
        w_hi_done = sem("w_hi_done")
        w_lo_done = sem("w_lo_done")
        unit_done = sem("unit_done")
        x_loaded = [sem(f"x_loaded{n}") for n in range(4)]
        table_loaded = sem("table_loaded")
        table_closed = sem("table_closed")
        gains_loaded = sem("gains_loaded")
        consts_loaded = sem("consts_loaded")
        ident_made = sem("ident_made")
        vec_mm = sem("vec_mm")
        vec_copied = sem("vec_copied")
        vec_stored = [sem("vec_stored0"), sem("vec_stored1")]
        rows_stored = [sem(f"rows_stored{n}") for n in range(len(VECS))]
        bias_loaded = [sem("bias_loaded0"), sem("bias_loaded1")]
        lam_step = sem("lam_step")
        lam_exp = sem("lam_exp")
        x_added = sem("x_added")
        xg_hi_done = sem("xg_hi_done")
        xg_lo_done = sem("xg_lo_done")
        sq_done = sem("sq_done")
        acc_added = sem("acc_added")
        stat_ready = sem("stat_ready")
        ms_ready = sem("ms_ready")
        inv_ready = sem("inv_ready")
        diag_ready = sem("diag_ready")
        bc_ready = sem("bc_ready")
        bc_used = sem("bc_used")
        proj_t = sem("proj_t")
        qk_hi = sem("qk_hi")
        qk_lo = sem("qk_lo")
        s_ready = sem("s_ready")
        scored = sem("scored")
        exp_done = sem("exp_done")
        recip_done = sem("recip_done")
        part_done = sem("part_done")
        p_ready = sem("p_ready")
        t_ready = sem("t_ready")
        pt_hi = sem("pt_hi")
        t_free = sem("t_free")
        pv_done = sem("pv_done")
        o_copied = sem("o_copied")
        oc_hi = sem("oc_hi")
        oc_lo = sem("oc_lo")
        silu_done = sem("silu_done")
        silu_in = sem("silu_in")
        up_scaled = sem("up_scaled")
        h_ready = sem("h_ready")
        h_hi = sem("h_hi")
        h_lo = sem("h_lo")
        final_ready = sem("final_ready")
        select_loaded = sem("select_loaded")
        rotary_loaded = sem("rotary_loaded")
        edges_closed = sem("edges_closed")
        k_pads_zeroed = sem("k_pads_zeroed")
        comb_mm = sem("comb_mm")
        comb_step = sem("comb_step")
        comb_diff = sem("comb_diff")
        comb_exp = sem("comb_exp")
        comb_diag = sem("comb_diag")
        comb_bc = sem("comb_bc")
        mix_part = sem("mix_part")
        mix_done = sem("mix_done")
        lat_sq = sem("lat_sq")
        lat_add = sem("lat_add")
        lat_acc = sem("lat_acc")
        lat_mean = sem("lat_mean")
        kr_part = sem("kr_part")
        kpe_ready = sem("kpe_ready")
        q_done = sem("q_done")
        stored = sem("stored")

        block = ctx.enter_context(nc.Block())

        def unit_source(u):
            for name, first, last in (("w_ab", 0, U_WO0), ("w_o0", U_WO0, U_GU0), ("w_gu0", U_GU0, U_DN0),
                                      ("w_dn0", U_DN0, U_C), ("w_c", U_C, U_D), ("w_d", U_D, U_WO1),
                                      ("w_o1", U_WO1, U_GU1), ("w_gu1", U_GU1, U_DN1), ("w_dn1", U_DN1, U_END)):
                if first <= u < last:
                    return io[name], first

        def load_unit(sp, u, slot, name=None, first=None, j=None):
            if name is None:
                src, first = unit_source(u)
                at = src[u - first]
                static = True
            else:
                src = io[name]
                at = src[bass.ds(j, 1)].rearrange("a p n -> (a p) n")
                static = False
            if not static or u >= 2:
                sp.wait_ge(w_lo_done, u - 1)
            sp.dma_start(raw[:, slot, 0:src.shape[2]], at).then_inc(raw_loaded[slot], 16)

        def prep_hi(act, u, slot, tiles, half=None):
            half = u // 2 if half is None else half
            act.wait_ge(raw_loaded[slot], 16 * half + 16)
            if not isinstance(u, int) or u >= 2:
                act.wait_ge(unit_done, u - 1)
            n = tiles * P
            act.activation(w_hi[:, slot, 0:n], raw[:, slot, 0:n], ACT.Copy).then_inc(w_hi_done, 1)

        def prep_lo(engine, u, slot, tiles):
            engine.wait_ge(w_hi_done, u + 1)
            n = tiles * P
            engine.tensor_tensor(w_lo[:, slot, 0:n], raw[:, slot, 0:n], w_hi[:, slot, 0:n].bitcast(F32),
                               ALU.subtract).then_inc(w_lo_done, 1)

        def three(pe, out, l_hi, l_lo, r_hi, r_lo, first, last):
            pe.matmul(out, l_hi, r_hi, start=first, stop=False)
            pe.matmul(out, l_lo, r_hi, start=False, stop=False)
            return pe.matmul(out, l_hi, r_lo, start=False, stop=last)

        def wtile(slot, kc):
            return w_hi[:, slot, kc * P:(kc + 1) * P], w_lo[:, slot, kc * P:(kc + 1) * P]

        def pe_stat(pe, n, acc):
            if n >= 1:
                pe.wait_ge(bc_used, n)
            for b in range(TB):
                mm = pe.matmul(m_bank[:, b:b + 1], acc[:, b * P:(b + 1) * P], ones[:, 0:1], start=True, stop=True)
            mm.then_inc(stat_ready, 1)

        def dve_mean(dve, n, count):
            dve.wait_ge(stat_ready, n + 1)
            dve.tensor_scalar(mean_sq[:, :], m_bank[:, 0:TB], 1.0 / count, EPS, ALU.mult, ALU.add).then_inc(ms_ready, 1)

        def pool_root(pool, n):
            pool.wait_ge(ms_ready, n + 1)
            pool.tensor_tensor(inv_rms[:, :], mean_sq[:, :], neg_half[:, :], ALU.pow).then_inc(inv_ready, 1)

        def dve_diag(dve, n, diag):
            dve.wait_ge(inv_ready, n + 1)
            dve.tensor_tensor(diag.rearrange("p (b t) -> p b t", b=TB),
                              ident[:, :].unsqueeze(1).broadcast_to([P, TB, P]),
                              inv_rms[:, :].unsqueeze(2).broadcast_to([P, TB, P]), ALU.mult).then_inc(diag_ready, 1)

        def pe_broadcast(pe, n, diag):
            pe.wait_ge(diag_ready, n + 1)
            pe.matmul(m_bank[:, :], ones[:, :], diag, start=True, stop=True).then_inc(bc_ready, 1)

        def act_chunk(act, k, m, par, gain, with_xg=True, first_two=False):
            if k == 0:
                act.wait_ge(x_loaded[m // 2], 16)
            else:
                act.wait_ge(x_added, 8 * k + m + 1)
            if not isinstance(m, int):
                act.nop(nofuse=True)
            if with_xg:
                g = gains[:, gain + m:gain + m + 1] if isinstance(m, int) else gains[:, bass.ds(m + gain, 1)]
                x_m, hi_m = chunk(xT, m), xg_chunk(0, m)
                act.activation(hi_m, x_m, ACT.Copy, scale=g).then_inc(xg_hi_done, 1)
            if not first_two:
                act.wait_ge(acc_added, 9 * k + m)
                if not isinstance(m, int):
                    act.nop(nofuse=True)
            act.activation(tq[:, par, 0:T], chunk(xT, m), ACT.Square).then_inc(sq_done, 1)

        def chunk(t, m):
            return t[:, m, :] if isinstance(m, int) else t[:, bass.ds(m, 1), :].rearrange("p a t -> p (a t)")

        def xg_chunk(part, m):
            return xg[:, part, m, :] if isinstance(m, int) else xg[:, part, bass.ds(m, 1), :].rearrange("p a t -> p (a t)")

        def dve_chunk_lo(dve, k, m, gain):
            dve.wait_ge(xg_hi_done, 8 * k + m + 1)
            g = gains[:, gain + m:gain + m + 1] if isinstance(m, int) else gains[:, bass.ds(m + gain, 1)]
            dve.scalar_tensor_tensor(xg_chunk(1, m), chunk(xT, m), g, xg_chunk(0, m).bitcast(F32),
                                     ALU.mult, ALU.subtract).then_inc(xg_lo_done, 1)

        def pool_acc_start(pool, k):
            if k >= 1:
                pool.wait_ge(stat_ready, NORM_AT[k - 1] + 1)
            if k in (1, 3):
                pool.wait_ge(p_ready, (AB_TILES, ALL_TILES)[k // 2])
            pool.memset(sc[:, 3, :], 0.0).then_inc(acc_added, 1)

        def pool_acc(pool, k, m, par):
            pool.wait_ge(sq_done, 8 * k + m + 1)
            pool.wait_ge(acc_added, 9 * k + m + 1)
            pool.tensor_tensor(sc[:, 3, :], sc[:, 3, :], tq[:, par, 0:T], ALU.add).then_inc(acc_added, 1)

        BROADCAST_AT = (1, KC - 2)
        NORM_AT = [0, 1 + A_HEADS, 2 + A_HEADS, 5 + A_HEADS, 6 + A_HEADS]

        def kind_ab(u):
            return "qkv"[u % 3] if u < A_UNITS else {U_KB: "k", U_VB: "v"}.get(u, "q")

        def qk_index(u):
            return sum(kind_ab(x) != "v" for x in range(u))

        QK_AB = qk_index(N_AB)

        def slot_ab(u):
            return (u // 3) % 2 if u < A_UNITS else (0 if u < U_QB else (u - U_QB) % 2)

        def b_keys(b):
            return max(0, b - 1), min(TB, b + 2)

        AB_TILES = 4 * A_HEADS + 4 * B_HEADS
        A_SETS = 5 * A_HEADS
        B_TILES = 4 * B_HEADS
        B_STEPS = B_TILES + 4
        N_PROJ = N_AB + N_C + N_LAT + 2 * D_HEADS
        QK_ALL = QK_AB + 12 + QC + KVC + 1 + 2 * D_HEADS
        ALL_TILES = AB_TILES + TB * D_HEADS

        def a_set(h, b):
            return 5 * h + b + 1

        def b_set(n):
            return A_SETS + n + 1

        def sync_program(sp):
            for n in range(4):
                sp.dma_start(xT[:, 2 * n:2 * n + 2, :], io["x_t"][:, 2 * n:2 * n + 2, :]).then_inc(x_loaded[n], 16)
                if n == 0:
                    load_unit(sp, 0, 0)
            load_unit(sp, 1, 1)

            n_first = VECS[0][0]
            sp.wait_ge(vec_copied, 2)
            sp.dma_start(vec_dram[:, 0:n_first], pn[0:NH_BIAS, :, :].rearrange("p a t -> p (a t)")).then_inc(vec_stored[0], 16)

            def store_rows(v):
                length, _, _, first, heads = VECS[v]
                src = bass.AP(vec_dram.tensor, first * VEC_LEN + VEC_AT[v], [[VEC_LEN, heads], [0, P], [1, length]])
                dst = bass.AP(rep_dram.tensor, REP_AT[v], [[P * length, heads], [length, P], [1, length]])
                sp.dma_start(dst, src).then_inc(rows_stored[v], 16)

            def load_bias(v, head, slot, width):
                length, _, _, first, _ = VECS[v]
                src = bass.AP(rep_dram.tensor, REP_AT[v] + (head - first) * P * length + P - 1,
                              [[length - 1, P], [1, width]])
                sp.dma_start(bias[:, slot, 0:width], src).then_inc(bias_loaded[slot], 16)

            sp.wait_ge(vec_stored[0], 16)
            store_rows(0)
            sp.wait_ge(vec_copied, 5)
            for dst, src in ((vec_dram[:, VEC_AT[1]:VEC_AT[2]], mix[0:NH_BIAS, :]),
                             (vec_dram[:, VEC_AT[2]:VEC_AT[3]], rstd[0:NH_BIAS, 0:VECS[2][0]]),
                             (vec_dram[:, VEC_AT[3]:VEC_LEN], og[0:NH_BIAS, 2, :])):
                sp.dma_start(dst, src).then_inc(vec_stored[1], 16)
            sp.wait_ge(rows_stored[0], 16)
            load_bias(0, 0, 0, 896)
            load_unit(sp, 2, 0)
            load_bias(0, 1, 1, 896)
            load_unit(sp, 3, 1)
            sp.wait_ge(vec_stored[1], 48)
            for v in (1, 2, 3, 4):
                store_rows(v)
            for h in range(A_HEADS):
                for u in range(3 * h + 4, 3 * h + 7):
                    load_unit(sp, u, u % 2)
                if h == 0:
                    sp.wait_ge(rows_stored[1], 16)
                sp.wait_ge(scored, 8 * (h + 1))
                if h + 2 < A_HEADS:
                    load_bias(0, h + 2, h % 2, 896)
                else:
                    e = h + 2 - A_HEADS
                    load_bias(1, b_head(e), e % 2, 384)
            for e in range(B_HEADS):
                for u in {0: (U_QB + 2, U_QB + 3), 2: (U_WO0,), 4: (U_WO0 + 1,)}.get(e, ()):
                    load_unit(sp, u, u % 2)
                if e + 2 < B_HEADS:
                    sp.wait_ge(scored, 8 * A_HEADS + 4 * (e + 1))
                    load_bias(1, b_head(e + 2), e % 2, 384)
            for v in (2, 3, 4):
                sp.wait_ge(rows_stored[v], 16)
            for e in range(2):
                sp_bias_c(sp, load_bias, e)
            stream_loop(sp, "w_o0", U_WO0, U_WO0 + 2, U_GU0)
            stream_loop(sp, "w_gu0", U_GU0, U_GU0, U_DN0)
            stream_loop(sp, "w_dn0", U_DN0, U_DN0, U_C)
            sp_layer1(sp, load_bias)
            sp_store(sp)

        def stream_loop(sp, name, first, u0, u1):
            assert (u1 - u0) % 2 == 0
            with sp.Fori(0, (u1 - u0) // 2) as i:
                for s in range(2):
                    load_unit(sp, i * 2 + (u0 + s), (u0 + s) % 2, name, first, i * 2 + (u0 - first + s))

        def b_head(e):
            return A_HEADS + e // 2 + 4 * (e % 2)

        def sp_store(sp):
            for m in range(KC):
                sp.wait_ge(final_ready, m + 1)
                sp.dma_start(io["out"][:, m, :], xT[:, m, :]).then_inc(stored, 16)
            sp.wait_ge(stored, 16 * KC)

        def gpsimd_program(pool):
            pool.memset(ident[:, :], 0.0).then_inc(ident_made, 1)
            pool.memset(ones[:, :], 1.0)
            pool.memset(neg_half[:, :], -0.5)
            pool.wait_ge(ident_made, 1)
            pool.affine_select(out=ident[:, :], in_=ident[:, :], compare_op=ALU.not_equal, fill=1.0,
                               base=0, pattern=[[-1, P]], channel_multiplier=1).then_inc(ident_made, 1)
            prep_lo(pool, 0, 0, KC)
            prep_lo(pool, 1, 1, KC)
            pool_ab(pool)
            pool_wo(pool, 0)
            pool_ffn(pool, 0)
            pool_layer1(pool)

        def pool_qk_lo(pool, i, u, dst):
            pool.wait_ge(qk_hi, i + 1)
            pool.tensor_tensor(dst[1], tq[:, u % 2, 0:T], dst[0].bitcast(F32), ALU.subtract).then_inc(qk_lo, 1)

        def qk_dst(u):
            store = q_ab if kind_ab(u) == "q" else k_ab
            return store[:, slot_ab(u), 0, :], store[:, slot_ab(u), 1, :]

        def pool_evac_ab(pool, u):
            prep_lo(pool, u + 2, u % 2, KC)
            if kind_ab(u) != "v":
                pool_qk_lo(pool, qk_index(u), u, qk_dst(u))

        def pool_oc_lo(pool, c, src, before=0):
            pool.wait_ge(oc_hi, before + c + 1)
            pool.tensor_tensor(oc[:, 1, c, :], src, oc[:, 0, c, :].bitcast(F32), ALU.subtract).then_inc(oc_lo, 1)

        def pool_ab(pool):
            pool_root(pool, 0)
            pool_evac_ab(pool, 0)
            pool_evac_ab(pool, 1)
            pool_evac_ab(pool, 2)
            for h in range(A_HEADS):
                for b in range(TB):
                    if b >= 1:
                        pool_evac_ab(pool, 3 * (h + 1) + b - 1)
                    if h >= 1 and b == 1:
                        pool_root(pool, h)
                    if h >= 1 and b == 3:
                        pool_oc_lo(pool, h - 1, og[:, 1, :])
            for n in range(B_STEPS):
                if n == 0:
                    pool_evac_ab(pool, U_QB + 1)
                if n == 1:
                    pool_root(pool, A_HEADS)
                if n == 3:
                    pool_oc_lo(pool, A_HEADS - 1, og[:, 1, :])
                if n in (12, 20):
                    u = U_QB + 1 + n // 8
                    pool_qk_lo(pool, qk_index(u), u, qk_dst(u))
                if n in (13, 21, 29):
                    pool_oc_lo(pool, A_HEADS + (n - 11) // 8, og[:, 0, :])
                if n in (14, 22):
                    prep_lo(pool, U_QB + 3 + n // 8, (U_QB + 3 + n // 8) % 2, KC)

        def pool_wo(pool, layer):
            k = (1, 3)[layer]
            u0 = (U_WO0, U_WO1)[layer]
            pool_acc_start(pool, k)
            pool_acc(pool, k, 0, 0)
            pool.wait_ge(w_lo_done, u0 + 3)
            prep_lo(pool, u0 + 3, (u0 + 1) % 2, KC)
            pool_acc(pool, k, 1, 1)
            with pool.Fori(1, KC // 2) as i:
                for s in range(2):
                    prep_lo(pool, i * 2 + (u0 + s + 2), (u0 + s) % 2, KC)
                    pool_acc(pool, k, i * 2 + s, s)
            pool_root_slot(pool, layer, 0)

        def pool_root_slot(pool, layer, which):
            pool_root(pool, NORM_AT[(1, 3)[layer] + which])

        def pool_ffn(pool, layer):
            u0, u1 = ((U_GU0, U_DN0), (U_GU1, U_DN1))[layer]
            k = (2, 4)[layer]
            f0 = FC * layer

            def hidden_lo(f, par):
                pool.wait_ge(h_hi, f + f0 + 1)
                pool.tensor_tensor(hid_chunk(1, f), pn[:, par, :], hid_chunk(0, f).bitcast(F32),
                                   ALU.subtract).then_inc(h_lo, 1)

            with pool.Fori(0, FC // 2 - 1) as i:
                for par in range(2):
                    f = i * 2 + par
                    prep_lo(pool, f * 2 + (u0 + 2), u0 % 2, KC)
                    prep_lo(pool, f * 2 + (u0 + 3), (u0 + 1) % 2, KC)
                    hidden_lo(f, par)
            for par in range(2):
                f = FC - 2 + par
                tiles = KC if par == 0 else DOWN_HALF
                prep_lo(pool, u0 + 2 * f + 2, u0 % 2, tiles)
                prep_lo(pool, u0 + 2 * f + 3, (u0 + 1) % 2, tiles)
                hidden_lo(f, par)
            pool_acc_start(pool, k)
            with pool.Fori(0, KC // 2 - 1) as i:
                for par in range(2):
                    m = i * 2 + par
                    for s in range(2):
                        prep_lo(pool, m * 2 + (u1 + s + 2), (u1 + s) % 2, DOWN_HALF)
                    pool_acc(pool, k, m, par)
            for par in range(2):
                m = KC - 2 + par
                for s in range(2):
                    if par == 0:
                        prep_lo(pool, u1 + 2 * m + s + 2, (u1 + s) % 2, DOWN_HALF)
                    elif layer == 0:
                        prep_lo(pool, u1 + 2 * m + s + 2, (u1 + s) % 2, KC)
                if layer == 0 or m < KC - 1:
                    pool_acc(pool, k, m, par)

        def hid_chunk(part, f):
            return hid[:, part, f, :] if isinstance(f, int) else hid[:, part, bass.ds(f, 1), :].rearrange("p a t -> p (a t)")

        def scalar_program(act):
            act.dma_start(tab[0:NB, :], io["bias_table"]).then_inc(table_loaded, 16)
            act.dma_start(bias[0:NB + 1, :, :].rearrange("p a t -> p (a t)")[:, 0:VEC_AT[3]],
                          io["one_hot"][:, 0:VEC_AT[3]]).then_inc(table_loaded, 16)
            act.dma_start(og[0:NB + 1, 0, :], io["one_hot"][:, VEC_AT[3]:VEC_LEN]).then_inc(table_loaded, 16)
            act.dma_start(gains[:, :], io["gains"]).then_inc(gains_loaded, 16)
            act.dma_start(sink[:, :], bass.AP(io["sink"].tensor, 0, [[0, P], [1, B_HEADS]])).then_inc(consts_loaded, 16)
            act.dma_start(og[:, 1, 0:4 * HD], bass.AP(io["lambdas"].tensor, 0, [[0, P], [1, 4 * HD]])).then_inc(consts_loaded, 16)
            act.dma_start(masks[:, :], io["comb_masks"]).then_inc(consts_loaded, 16)
            act.preload_act_table(ACT.Exp)
            act.wait_ge(gains_loaded, 16)
            for m in range(KC):
                act_chunk(act, 0, m, m % 2, G_ATTN0, first_two=m < 2)
                if m in (0, 1):
                    prep_hi(act, m, m, KC)
            act.wait_ge(lam_step, 1)
            act.activation(lam[:, 2:4], lam[:, 0:2], ACT.Exp).then_inc(lam_exp, 1)
            act_ab(act)
            act_wo(act, 0)
            act_ffn(act, 0)
            act_layer1(act)

        def act_evac_ab(act, u):
            prep_hi(act, u + 2, u % 2, KC)
            act_evac_qk(act, u)

        def act_evac_qk(act, u):
            if kind_ab(u) != "v":
                act.wait_ge(proj_t, u + 1)
                act.activation(qk_dst(u)[0], tq[:, u % 2, 0:T], ACT.Copy).then_inc(qk_hi, 1)

        def act_exp(act, s):
            act.activation(sc[:, s % 4, :], sc[:, s % 4, :], ACT.Exp, scale=-1.0, bias=neg_max[:, s % 8:s % 8 + 1],
                           accum_out=row_sum[:, s % 8:s % 8 + 1]).then_inc(exp_done, 1)

        def act_set(act, n, dst, src):
            act.wait_ge(t_ready, n + 1)
            act.activation(dst, src, ACT.Copy).then_inc(pt_hi, 1)

        def bank3(bank, blocks, width=P):
            return bank[:, 0:blocks * width].rearrange("p (a t) -> p a t", a=blocks)

        def act_ab(act):
            for u in range(3):
                act_evac_ab(act, u)
            for h in range(A_HEADS):
                for b in range(TB):
                    n = 4 * h + b
                    for s in (2 * n, 2 * n + 1):
                        act.wait_ge(scored, s + 1)
                        act_exp(act, s)
                    if h >= 1 and b == 0:
                        act_o_norm(act, h - 1)
                    if b == 0:
                        act_set(act, a_set(h, -1), v_ab[:, h % 2, 0, :, :], bank3(t_bank[a_set(h, -1) % 2], TB))
                    if b >= 1:
                        act_evac_ab(act, 3 * (h + 1) + b - 1)
                    if h >= 2 and b == 0:
                        act.wait_ge(pv_done, h - 1)
                    act_set(act, a_set(h, b), pt_ab[:, h % 2, 0, :, b * P:(b + 1) * P], bank3(t_bank[a_set(h, b) % 2], TB))
                    if h >= 1 and b == 3:
                        act_oc_a(act, h - 1)
            for n in range(B_STEPS):
                if n == 0:
                    act_set(act, b_set(-1), v_ab[:, 0, 0, :, :], bank3(t_bank[b_set(-1) % 2], TB))
                    act_evac_ab(act, U_QB + 1)
                if 2 <= n < B_TILES + 2:
                    m = n - 2
                    b = m % 4
                    ks, ke = b_keys(b)
                    if b == 0:
                        act.wait_ge(pv_done, A_HEADS - 1 + m // 4)
                    act_set(act, b_set(m), pt_ab[:, (m // 4) % 2, 0, ks:ke, b * P:(b + 1) * P],
                            bank3(t_bank[b_set(m) % 2], ke - ks))
                if n < B_TILES:
                    s = 8 * A_HEADS + n
                    ks, ke = b_keys(n % 4)
                    w = (ke - ks) * P
                    act.wait_ge(scored, s + 1)
                    act.activation(sc[:, s % 4, 0:w + 1], sc[:, s % 4, 0:w + 1], ACT.Exp, scale=-1.0,
                                   bias=neg_max[:, s % 8:s % 8 + 1],
                                   accum_out=row_sum[:, s % 8:s % 8 + 1]).then_inc(exp_done, 1)
                if n == 0:
                    act_o_norm(act, A_HEADS - 1)
                if n >= 7 and n % 4 == 3:
                    act_o_b(act, (n - 7) // 4)
                if n in (13, 21, 29, B_STEPS - 1):
                    act_oc_b(act, (n - 11) // 8)
                if n == 3:
                    act_oc_a(act, A_HEADS - 1)
                if n in (12, 20):
                    act_evac_qk(act, U_QB + 1 + n // 8)
                if n in (14, 22):
                    prep_hi(act, U_QB + 3 + n // 8, (U_QB + 3 + n // 8) % 2, KC)

        def act_o_norm(act, h):
            act.wait_ge(pv_done, h + 1)
            if h >= 1:
                act.wait_ge(oc_lo, h)
            act.activation(og[:, 1, :], o_bank[:, :], ACT.Square)
            act.activation(og[:, 0, :], o_bank[:, :], ACT.Copy).then_inc(o_copied, 1)

        def act_oc_a(act, h):
            act.wait_ge(bc_used, 2 + h)
            act.activation(oc[:, 0, h, :], og[:, 1, :], ACT.Copy).then_inc(oc_hi, 1)

        def act_o_b(act, e):
            act.wait_ge(pv_done, A_HEADS + e + 1)
            if e % 2 == 0:
                act.wait_ge(oc_lo, A_HEADS + e // 2)
            half = e % 2
            act.activation(og[half * HD:(half + 1) * HD, 0, :], o_bank[0:HD, :], ACT.Copy).then_inc(o_copied, 1)

        def act_oc_b(act, j):
            act.wait_ge(o_copied, A_HEADS + 2 * j + 2)
            act.activation(oc[:, 0, A_HEADS + j, :], og[:, 0, :], ACT.Copy).then_inc(oc_hi, 1)

        def act_wo(act, layer):
            k = (1, 3)[layer]
            u0 = (U_WO0, U_WO1)[layer]
            gain = (G_FFN0, G_FFN1)[layer]
            act.wait_ge(qk_lo, (QK_AB, QK_ALL)[layer])

            def panel(m, s):
                prep_hi(act, m + (u0 + 2), (u0 + s) % 2, KC)
                act_chunk(act, k, m, s, gain, first_two=isinstance(m, int) and m < 2)

            for m in range(2):
                panel(m, m)
            with act.Fori(1, KC // 2) as i:
                for s in range(2):
                    prep_hi(act, i * 2 + (u0 + 2 + s), (u0 + s) % 2, KC, i + (u0 + 2 + s) // 2)
                    act_chunk(act, k, i * 2 + s, s, gain)

        def act_ffn(act, layer):
            u0, u1 = ((U_GU0, U_DN0), (U_GU1, U_DN1))[layer]
            k = (2, 4)[layer]
            f0 = FC * layer
            gain = (G_ATTN1, G_FINAL)[layer]

            def hidden(f, par, u, tiles, half=None):
                prep_hi(act, u, u0 % 2, tiles, half and half[0])
                act.wait_ge(silu_in, f + f0 + 1)
                act.activation(sc[:, par, :], tq[:, 0, 0:T], ACT.Silu).then_inc(silu_done, 1)
                prep_hi(act, u + 1, (u0 + 1) % 2, tiles, half and half[1])
                act.wait_ge(h_ready, f + f0 + 1)
                if not isinstance(f, int):
                    act.nop(nofuse=True)
                act.activation(hid_chunk(0, f), pn[:, par, :], ACT.Copy).then_inc(h_hi, 1)

            act.preload_act_table(ACT.Silu)
            with act.Fori(0, FC // 2 - 1) as i:
                for par in range(2):
                    f = i * 2 + par
                    base = u0 + 2 * par + 2
                    hidden(f, par, i * 4 + base, KC, [i * 2 + (base + s) // 2 for s in range(2)])
            for par in range(2):
                f = FC - 2 + par
                tiles = KC if par == 0 else DOWN_HALF
                hidden(f, par, u0 + 2 * f + 2, tiles)

            def down(m, par, u, tiles, half=None):
                for s in range(2):
                    if tiles:
                        prep_hi(act, u + s, (u1 + s) % 2, tiles, None if half is None else half[s])
                act_chunk(act, k, m, par, gain, with_xg=layer == 0, first_two=isinstance(m, int) and m < 2)

            for m in range(2):
                down(m, m, u1 + 2 * m + 2, DOWN_HALF)
            with act.Fori(1, KC // 2 - 1) as i:
                for par in range(2):
                    base = u1 + 2 * par + 2
                    down(i * 2 + par, par, i * 4 + base, DOWN_HALF, [i * 2 + (base + s) // 2 for s in range(2)])
            for m in (KC - 2, KC - 1):
                tiles = DOWN_HALF if m == KC - 2 else (KC if layer == 0 else 0)
                down(m, m % 2, u1 + 2 * m + 2, tiles)

        def vector_program(dve):
            dve.memset(tab[NB:NB + 1, :], NEG).then_inc(table_closed, 1)
            dve.memset(sc[:, 3, :], 0.0).then_inc(acc_added, 1)

            def copy_vec(n):
                dve.wait_ge(vec_mm, n + 1)
                dst = (pn[0:NH_BIAS, 0, :], pn[0:NH_BIAS, 1, :], mix[0:NH_BIAS, :], rstd[0:NH_BIAS, 0:VECS[2][0]],
                       og[0:NH_BIAS, 2, :])[n]
                src = (t_bank + s_bank + [o_bank])[n]
                dve.tensor_copy(dst, src[0:NH_BIAS, 0:dst.shape[-1]]).then_inc(vec_copied, 1)

            def add_square(m):
                dve.wait_ge(sq_done, m + 1)
                dve.wait_ge(acc_added, m + 1)
                dve.tensor_tensor(sc[:, 3, :], sc[:, 3, :], tq[:, m % 2, 0:T], ALU.add).then_inc(acc_added, 1)

            copy_vec(0)
            copy_vec(1)
            for m in range(KC):
                if m % 2 == 0:
                    dve.wait_ge(x_loaded[m // 2], 16)
                dve.sem_inc(x_added, 1)
                dve_chunk_lo(dve, 0, m, G_ATTN0)
                if m < 3:
                    copy_vec(2 + m)
                if m >= 1:
                    add_square(m - 1)
            add_square(KC - 1)
            dve.wait_ge(consts_loaded, 16 * 3)
            for n in range(2):
                ins = dve.tensor_tensor_reduce(out=picked[:, n * HD:(n + 1) * HD], in0=og[:, 1, 2 * n * HD:(2 * n + 1) * HD],
                                               in1=og[:, 1, (2 * n + 1) * HD:(2 * n + 2) * HD], scale=1.0, scalar=0.0,
                                               op0=ALU.mult, op1=ALU.add, accum_out=lam[:, n:n + 1])
            ins.then_inc(lam_step, 1)
            dve.tensor_scalar(neg_sink[:, :], sink[:, :], -1.0, None, ALU.mult)
            dve.tensor_scalar(sub_gain[:, :], gains[:, G_SUB:G_SUB + 1], 1.0 - LAMBDA_INIT, None, ALU.mult)
            dve_mean(dve, 0, DM)
            dve_diag(dve, 0, sc[:, 2, :])
            dve.wait_ge(lam_exp, 1)
            dve.scalar_tensor_tensor(lam[:, 4:5], lam[:, 3:4], LAMBDA_INIT, lam[:, 2:3], ALU.subtract,
                                     ALU.subtract).then_inc(lam_step, 1)
            dve.wait_ge(lam_step, 2)
            dve.wait_ge(vec_stored[1], 48)
            dve.wait_ge(bc_ready, 1)
            dve.tensor_copy(rstd[:, :], m_bank[:, :]).then_inc(bc_used, 1)
            dve.wait_ge(bc_used, 1)
            dve_ab(dve)
            dve_wo(dve, 0)
            dve_ffn(dve, 0)
            dve_layer1(dve)

        def dve_evac_ab(dve, u):
            dve.wait_ge(unit_done, u + 1)
            if u >= 2 and kind_ab(u - 2) != "v":
                dve.wait_ge(qk_lo, qk_index(u - 2) + 1)
            scale = HD ** -0.5 if kind_ab(u) == "q" else 1.0
            dve.scalar_tensor_tensor(tq[:, u % 2, 0:T], g_bank[u % 2][:, :], scale, rstd[:, :],
                                     ALU.mult, ALU.mult).then_inc(proj_t, 1)

        def dve_set(dve, n, dst_lo, src, dst_hi):
            dve.wait_ge(pt_hi, n + 1)
            dve.tensor_tensor(dst_lo, src, dst_hi.bitcast(F32), ALU.subtract).then_inc(t_free, 1)

        def score(dve, s, width, bank, bias_ap, least=BIG):
            dve.wait_ge(s_ready, s + 1)
            dve.tensor_tensor_reduce(out=sc[:, s % 4, 0:width], in0=bank[:, 0:width], in1=bias_ap, scale=-1.0, scalar=least,
                                     op0=ALU.add, op1=ALU.min, accum_out=neg_max[:, s % 8:s % 8 + 1]).then_inc(scored, 1)

        def dve_ab(dve):
            for u in range(3):
                dve_evac_ab(dve, u)
            for h in range(A_HEADS):
                dve.wait_ge(bias_loaded[h % 2], 16 * (h // 2 + 1))
                for b in range(TB):
                    n = 4 * h + b
                    for s in (2 * n, 2 * n + 1):
                        score(dve, s, T, s_bank[s % 2], bias[:, h % 2, 384 - b * P:384 - b * P + T])
                    c = (2 * n) % 8
                    dve.wait_ge(exp_done, 2 * n + 2)
                    dve.reciprocal(inv_sum[:, c:c + 2], row_sum[:, c:c + 2]).then_inc(recip_done, 1)
                    dve.wait_ge(recip_done, n + 1)
                    s1 = (2 * n + 1) % 4
                    dve.tensor_scalar(sc[:, s1, :], sc[:, s1, :], inv_sum[:, c + 1:c + 2], lam[:, 4:5], ALU.mult,
                                      ALU.mult).then_inc(part_done, 1)
                    dve.wait_ge(part_done, n + 1)
                    dve.scalar_tensor_tensor(pn[:, n % 2, :], sc[:, s1 - 1, :], inv_sum[:, c:c + 1], sc[:, s1, :],
                                             ALU.mult, ALU.add).then_inc(p_ready, 1)
                    if b == 0:
                        k = a_set(h, -1)
                        dve_set(dve, k, v_ab[:, h % 2, 1, :, :], bank3(t_bank[k % 2], TB), v_ab[:, h % 2, 0, :, :])
                    if b >= 1:
                        dve_evac_ab(dve, 3 * (h + 1) + b - 1)
                    if h >= 1 and b == 1:
                        dve_mean(dve, h, P)
                    if h >= 1 and b == 2:
                        dve_diag(dve, h, og[:, 2, :])
                    if h >= 1 and b == 3:
                        dve_o_norm(dve, h - 1)
                    k = a_set(h, b)
                    cols = slice(b * P, (b + 1) * P)
                    dve_set(dve, k, pt_ab[:, h % 2, 1, :, cols], bank3(t_bank[k % 2], TB), pt_ab[:, h % 2, 0, :, cols])
            for n in range(B_STEPS):
                if n == 0:
                    k = b_set(-1)
                    dve_set(dve, k, v_ab[:, 0, 1, :, :], bank3(t_bank[k % 2], TB), v_ab[:, 0, 0, :, :])
                    dve_evac_ab(dve, U_QB + 1)
                if 1 <= n <= B_TILES:
                    dve_norm_b(dve, n - 1)
                if n < B_TILES:
                    e, b = n // 4, n % 4
                    s = 8 * A_HEADS + n
                    ks, ke = b_keys(b)
                    w = (ke - ks) * P
                    head = e // 2 + 4 * (e % 2)
                    c = s % 8
                    if b == 0:
                        dve.wait_ge(bias_loaded[e % 2], 16 * ((A_HEADS + e) // 2 + 1))
                    j0 = (ks - b + 1) * P
                    if n >= 4:
                        dve.wait_ge(p_ready, 4 * A_HEADS + n - 3)
                    dve.tensor_copy(sc[:, s % 4, w:w + 1], neg_sink[:, head:head + 1])
                    score(dve, s, w, s_bank[s % 2], bias[:, e % 2, j0:j0 + w], neg_sink[:, head:head + 1])
                if n == 1:
                    dve_mean(dve, A_HEADS, P)
                if n == 2:
                    dve_diag(dve, A_HEADS, og[:, 2, :])
                if n == 3:
                    dve_o_norm(dve, A_HEADS - 1)
                if 2 <= n < B_TILES + 2:
                    m = n - 2
                    b = m % 4
                    ks, ke = b_keys(b)
                    k = b_set(m)
                    cols = slice(b * P, (b + 1) * P)
                    dve_set(dve, k, pt_ab[:, (m // 4) % 2, 1, ks:ke, cols], bank3(t_bank[k % 2], ke - ks),
                            pt_ab[:, (m // 4) % 2, 0, ks:ke, cols])
                if n in (12, 20):
                    dve_evac_ab(dve, U_QB + 1 + n // 8)

        def dve_norm_b(dve, n):
            s = 8 * A_HEADS + n
            ks, ke = b_keys(n % 4)
            w = (ke - ks) * P
            c = s % 8
            dve.wait_ge(exp_done, s + 1)
            dve.reciprocal(inv_sum[:, c:c + 1], row_sum[:, c:c + 1]).then_inc(recip_done, 1)
            dve.wait_ge(recip_done, 4 * A_HEADS + n + 1)
            dve.tensor_scalar(pn[:, n % 2, 0:w], sc[:, s % 4, 0:w], inv_sum[:, c:c + 1], None, ALU.mult).then_inc(p_ready, 1)

        def dve_o_norm(dve, h):
            dve.wait_ge(bc_ready, 2 + h)
            dve.scalar_tensor_tensor(og[:, 1, :], og[:, 0, :], sub_gain[:, 0:1], m_bank[:, :], ALU.mult,
                                     ALU.mult).then_inc(bc_used, 1)

        def dve_panel(dve, k, m, u_last, bank, gain, with_xg=True):
            dve.wait_ge(unit_done, u_last + 1)
            dve.tensor_tensor(chunk(xT, m), bank[:, :], chunk(xT, m), ALU.add).then_inc(x_added, 1)
            dve.wait_ge(x_added, 8 * k + m + 1)
            if with_xg:
                dve_chunk_lo(dve, k, m, gain)

        def dve_wo(dve, layer):
            k = (1, 3)[layer]
            u0 = (U_WO0, U_WO1)[layer]
            gain = (G_FFN0, G_FFN1)[layer]
            dve.wait_ge(oc_hi, 8 * layer + KC)
            dve.wait_ge(oc_lo, 8 * layer + KC - 1)
            dve.tensor_tensor(oc[:, 1, KC - 1, :], og[:, 0, :], oc[:, 0, KC - 1, :].bitcast(F32), ALU.subtract).then_inc(oc_lo, 1)
            for m in range(2):
                dve.wait_ge(unit_done, u0 + m + 1)
                dve.tensor_tensor(xT[:, m, :], g_bank[m][:, :], xT[:, m, :], ALU.add).then_inc(x_added, 1)
                if m == 0:
                    prep_lo(dve, u0 + 2, u0 % 2, KC)
            for m in range(2):
                dve.wait_ge(x_added, 8 * k + m + 1)
                dve_chunk_lo(dve, k, m, gain)
            with dve.Fori(1, KC // 2) as i:
                for s in range(2):
                    dve_panel(dve, k, i * 2 + s, i * 2 + (u0 + s), g_bank[s], gain)

        def dve_rstd(dve, n):
            dve_mean(dve, n, DM)
            dve_diag(dve, n, sc[:, 2, :])
            dve.wait_ge(bc_ready, n + 1)
            dve.tensor_copy(rstd[:, :], m_bank[:, :]).then_inc(bc_used, 1)
            dve.wait_ge(bc_used, n + 1)

        def dve_ffn(dve, layer):
            u0, u1 = ((U_GU0, U_DN0), (U_GU1, U_DN1))[layer]
            k = (2, 4)[layer]
            f0 = FC * layer
            gain = (G_ATTN1, G_FINAL)[layer]
            dve_rstd(dve, NORM_AT[(1, 3)[layer]])

            def hidden(f, par, u, first=False):
                dve.wait_ge(unit_done, u + 1)
                if not first:
                    dve.wait_ge(silu_done, f + f0)
                dve.tensor_tensor(tq[:, 0, 0:T], g_bank[0][:, :], rstd[:, :], ALU.mult).then_inc(silu_in, 1)
                dve.wait_ge(unit_done, u + 2)
                if not first:
                    dve.wait_ge(h_ready, f + f0)
                dve.tensor_tensor(tq[:, 1, 0:T], g_bank[1][:, :], rstd[:, :], ALU.mult).then_inc(up_scaled, 1)
                dve.wait_ge(up_scaled, f + f0 + 1)
                dve.wait_ge(silu_done, f + f0 + 1)
                if not isinstance(f, int) or f + f0 > 1:
                    dve.wait_ge(h_lo, f + f0 - 1)
                dve.tensor_tensor(pn[:, par, :], sc[:, par, :], tq[:, 1, 0:T], ALU.mult).then_inc(h_ready, 1)

            for f in range(2):
                hidden(f, f, u0 + 2 * f, first=f == 0 and layer == 0)
            with dve.Fori(1, FC // 2) as i:
                for par in range(2):
                    hidden(i * 2 + par, par, i * 4 + (u0 + 2 * par))
            with dve.Fori(0, KC // 2) as i:
                for par in range(2):
                    dve_panel(dve, k, i * 2 + par, i * 4 + (u1 + 2 * par + 1), g_bank[par], gain, with_xg=layer == 0)

        def tensor_program(pe):
            pe.wait_ge(ident_made, 2)
            pe.wait_ge(table_loaded, 16 * 3)
            pe.wait_ge(table_closed, 1)
            flat = bias[0:NB + 1, :, :].rearrange("p a t -> p (a t)")
            for n in range(5):
                w = 512 if n != 3 else 384
                src = flat[:, n * 512:n * 512 + w] if n < 4 else og[0:NB + 1, 0, :]
                dst = (t_bank + s_bank + [o_bank])[n]
                pe.matmul(dst[0:NH_BIAS, 0:w], tab[:, :], src, start=True, stop=True).then_inc(vec_mm, 1)
            pe_ab(pe)
            pe_wo(pe, 0)
            pe_ffn(pe, 0)
            pe_layer1(pe)

        def unit_step(pe, u, kc, tiles, bank, rhs, slot, free=None, chunks=None):
            if kc == 0:
                pe.wait_ge(w_lo_done, u + 1)
                if free is not None:
                    pe.wait_ge(*free)
            if chunks is not None:
                pe.wait_ge(xg_lo_done, chunks + kc + 1)
            w_h, w_l = wtile(slot, kc)
            mm = three(pe, bank[:, :], w_h, w_l, rhs[0][:, kc, :], rhs[1][:, kc, :], kc == 0, kc == tiles - 1)
            if kc == tiles - 1:
                mm.then_inc(unit_done, 1)

        xg_parts = (xg[:, 0], xg[:, 1])
        oc_parts = (oc[:, 0], oc[:, 1])

        def ab_step(pe, u, kc):
            unit_step(pe, u, kc, KC, g_bank[u % 2], xg_parts, u % 2,
                      free=(proj_t, u - 1) if u >= 2 else None, chunks=0 if u == 0 else None)

        def pe_set(pe, n, src, blocks):
            if n >= 2:
                pe.wait_ge(t_free, n - 1)
            bank = t_bank[n % 2]
            for c in range(blocks):
                mm = pe.transpose(bank[:, c * P:(c + 1) * P], src(c), ident[:, :])
            mm.then_inc(t_ready, 1)

        def pe_ab(pe):
            for u in range(3):
                for kc in range(KC):
                    if (u, kc) == BROADCAST_AT:
                        pe_broadcast(pe, 0, sc[:, 2, :])
                    ab_step(pe, u, kc)
                if u == 0:
                    pe.wait_ge(acc_added, 9)
                    pe_stat(pe, 0, sc[:, 3, :])
            pe.wait_ge(vec_copied, 5)
            for h in range(A_HEADS):
                pe.wait_ge(qk_lo, 2 * h + 2)
                for b in range(TB):
                    n = 4 * h + b
                    cols = slice(b * P, (b + 1) * P)
                    if n >= 1:
                        pe.wait_ge(scored, 2 * n)
                    for x, y in ((0, 0), (1, 0), (0, 1)):
                        for m in range(2):
                            rows = slice(m * HD, (m + 1) * HD)
                            mm = pe.matmul(s_bank[m][:, :], q_ab[rows, h % 2, x, cols], k_ab[rows, h % 2, y, :],
                                           start=(x, y) == (0, 0), stop=(x, y) == (0, 1))
                            if (x, y) == (0, 1):
                                mm.then_inc(s_ready, 1)
                    for step in range(6 * b, 6 * b + 6):
                        ab_step(pe, 3 * (h + 1) + step // KC, step % KC)
                    if b == 0:
                        if h >= 1:
                            pe_pv_a(pe, h - 1)
                        u = 3 * h + 2
                        pe.wait_ge(proj_t, u + 1)
                        pe_set(pe, a_set(h, -1), lambda c: tq[:, u % 2, c * P:(c + 1) * P], TB)
                    if h >= 1 and b == 1:
                        pe.wait_ge(o_copied, h)
                        pe_stat(pe, h, og[:, 1, :])
                    pe.wait_ge(p_ready, n + 1)
                    pe_set(pe, a_set(h, b), lambda c: pn[:, n % 2, c * P:(c + 1) * P], TB)
                    if h >= 1 and b == 2:
                        pe_broadcast(pe, h, og[:, 2, :])
            for n in range(B_STEPS):
                if n == 0:
                    pe.wait_ge(proj_t, U_VB + 1)
                    pe_set(pe, b_set(-1), lambda c: tq[:, U_VB % 2, c * P:(c + 1) * P], TB)
                    for kc in range(KC):
                        ab_step(pe, U_QB + 1, kc)
                    pe_pv_a(pe, A_HEADS - 1)
                if n < B_TILES:
                    e, b = n // 4, n % 4
                    j, hd = e // 2, e % 2
                    s = 8 * A_HEADS + n
                    ks, ke = b_keys(b)
                    if n % 8 == 0:
                        pe.wait_ge(qk_lo, 10 + j)
                    pe.wait_ge(scored, s - 1)
                    rows, cols, keys = slice(hd * HD, (hd + 1) * HD), slice(b * P, (b + 1) * P), slice(ks * P, ke * P)
                    q, k = q_ab[rows, j % 2], k_ab[rows, 0]
                    three(pe, s_bank[s % 2][:, 0:(ke - ks) * P], q[:, 0, cols], q[:, 1, cols], k[:, 0, keys], k[:, 1, keys],
                          True, True).then_inc(s_ready, 1)
                    if j in (1, 2) and n % 8 < 4:
                        for kc in (2 * (n % 4), 2 * (n % 4) + 1):
                            ab_step(pe, U_QB + 1 + j, kc)
                for m, kc in wo_ahead_b(n):
                    wo_tile(pe, 0, m, m, kc)
                if n == 1:
                    pe.wait_ge(o_copied, A_HEADS)
                    pe_stat(pe, A_HEADS, og[:, 1, :])
                if n >= 6 and n % 4 == 2:
                    pe_pv_b(pe, (n - 6) // 4)
                if 1 <= n <= B_TILES:
                    m = n - 1
                    ks, ke = b_keys(m % 4)
                    pe.wait_ge(p_ready, 4 * A_HEADS + m + 1)
                    pe_set(pe, b_set(m), lambda c: pn[:, m % 2, c * P:(c + 1) * P], ke - ks)
                if n == 2:
                    pe_broadcast(pe, A_HEADS, og[:, 2, :])

        AHEAD = [(m, kc) for kcs in (range(KC - 2), (KC - 2,)) for m in range(2) for kc in kcs]

        def wo_ahead_b(n):
            first = B_TILES - 8
            if n < first or n > B_TILES + 2:
                return []
            if n < B_TILES:
                return AHEAD[n - first:n - first + 1]
            return AHEAD[8 + 2 * (n - B_TILES):8 + 2 * (n - B_TILES) + 2]

        def wo_tile(pe, layer, m, s, kc):
            u0 = (U_WO0, U_WO1)[layer]
            k = (1, 3)[layer]
            ahead = isinstance(m, int)
            if ahead and kc == 0:
                pe.wait_ge(proj_t, (N_AB, N_PROJ)[layer] - 1 + m)
            if ahead:
                pe.wait_ge(oc_lo, 8 * layer + kc + 1)
            unit_step(pe, m + u0, kc, KC, g_bank[s], oc_parts, (u0 + s) % 2,
                      free=None if ahead else (x_added, m + (8 * k - 1)))

        def pe_pv_a(pe, h):
            pe.wait_ge(t_free, a_set(h, 3) + 1)
            if h >= 1:
                pe.wait_ge(o_copied, h)
            for kc in range(TB):
                mm = three(pe, o_bank[:, :], v_ab[:, h % 2, 0, kc, :], v_ab[:, h % 2, 1, kc, :],
                           pt_ab[:, h % 2, 0, kc, :], pt_ab[:, h % 2, 1, kc, :], kc == 0, kc == TB - 1)
            mm.then_inc(pv_done, 1)

        def pe_pv_b(pe, e):
            pe.wait_ge(t_free, b_set(4 * e + 3) + 1)
            pe.wait_ge(o_copied, A_HEADS + e)
            cols = slice((e % 2) * HD, (e % 2 + 1) * HD)
            for kc in (0, 3, 1, 2):
                qs, qe = b_keys(kc)
                mm = three(pe, o_bank[0:HD, qs * P:qe * P], v_ab[:, 0, 0, kc, cols], v_ab[:, 0, 1, kc, cols],
                           pt_ab[:, e % 2, 0, kc, qs * P:qe * P], pt_ab[:, e % 2, 1, kc, qs * P:qe * P], kc == 0, kc == 2)
            mm.then_inc(pv_done, 1)

        def pe_wo(pe, layer):
            for m in range(2):
                wo_tile(pe, layer, m, m, KC - 1)
            with pe.Fori(1, KC // 2) as i:
                for s in range(2):
                    for kc in range(KC):
                        wo_tile(pe, layer, i * 2 + s, s, kc)

        def pe_ffn(pe, layer):
            u0, u1 = ((U_GU0, U_DN0), (U_GU1, U_DN1))[layer]
            n = NORM_AT[(1, 3)[layer]]
            k = (1, 3)[layer]
            for s in range(2):
                for kc in range(KC):
                    if (s, kc) == BROADCAST_AT:
                        pe_broadcast(pe, n, sc[:, 2, :])
                    unit_step(pe, u0 + s, kc, KC, g_bank[s], xg_parts, (u0 + s) % 2,
                              free=(x_added, 8 * k + 7 + s), chunks=8 * k if s == 0 else None)
                if s == 0:
                    pe.wait_ge(acc_added, 9 * (k + 1))
                    pe_stat(pe, n, sc[:, 3, :])
            with pe.Fori(1, FC) as i:
                for s in range(2):
                    for kc in range(KC):
                        unit_step(pe, i * 2 + (u0 + s), kc, KC, g_bank[s], xg_parts, (u0 + s) % 2,
                                  free=((silu_in, up_scaled)[s], i + FC * layer))

            hid_parts = (hid[:, 0], hid[:, 1])

            def down(u, s, par, free, panel0=False):
                slot = (u1 + s) % 2
                pe.wait_ge(w_lo_done, u + 1)
                if s == 0:
                    pe.wait_ge(*free)
                for kc in range(DOWN_HALF):
                    c = s * DOWN_HALF + kc
                    if panel0:
                        pe.wait_ge(h_lo, FC * layer + c + 1)
                    w_h, w_l = wtile(slot, kc)
                    mm = three(pe, g_bank[par][:, :], w_h, w_l, hid_parts[0][:, c, :], hid_parts[1][:, c, :],
                               c == 0, c == FC - 1)
                mm.then_inc(unit_done, 1)

            for s in range(2):
                down(u1 + s, s, 0, (silu_in, FC * (layer + 1)), panel0=True)
            for s in range(2):
                down(u1 + 2 + s, s, 1, (up_scaled, FC * (layer + 1)))
            with pe.Fori(1, KC // 2) as i:
                for par in range(2):
                    for s in range(2):
                        down(i * 4 + (u1 + 2 * par + s), s, par, (x_added, i * 2 + (8 * (k + 1) + par - 1)))

        def c_tiles(c):
            return 4 if c % 3 == 0 else 2

        C_TILE_AT = [sum(c_tiles(x) for x in range(c)) for c in range(7)]
        C_TILE_LIST = [(c, ti) for c in range(6) for ti in range(c_tiles(c))]
        S_C = 8 * A_HEADS + B_TILES
        S_D = S_C + len(C_TILE_LIST)
        SET_C = A_SETS + B_TILES + 1
        c_sets, at = {}, SET_C
        for t_, (c_, ti_) in enumerate(C_TILE_LIST):
            if ti_ == 0:
                for k_ in range(2 if c_ % 3 == 0 else 1):
                    c_sets["v", c_, k_] = at
                    at += 1
            c_sets["t", t_] = at
            at += 1
        SET_D = at
        T_AB = N_AB
        QK_C = QK_AB
        QK_LAT = QK_C + 12
        QK_D = QK_LAT + QC + KVC + 1
        PV_C = A_HEADS + B_HEADS
        PV_D = PV_C + len(C_TILE_LIST)
        BIAS_C = (A_HEADS + B_HEADS) // 2

        def c_tile(t):
            c, ti = C_TILE_LIST[t]
            g = c % 3
            if g == 0:
                return c, g, ti // 2, [2 * (ti % 2), 2 * (ti % 2) + 1]
            return c, g, ti, list(range(TB))

        def c_last_tile(e):
            return max(t for t in range(len(C_TILE_LIST)) if 2 * c_tile(t)[0] + c_tile(t)[2] == e)

        def c_bias_count(e):
            return BIAS_C + e // 2 + 1

        def c_steps(t):
            c, ti = C_TILE_LIST[t]
            n = 3 * KC // c_tiles(c)
            return range(ti * n, (ti + 1) * n) if c < 5 else range(0)

        def c_done_units(t):
            return [U_C + 3 * (C_TILE_LIST[t][0] + 1) + s // KC for s in c_steps(t) if s % KC == KC - 1]

        def kind_c(u):
            return "qkv"[(u - U_C) % 3]

        def qk_index_c(u):
            return QK_C + 2 * ((u - U_C) // 3) + (u - U_C) % 3

        def strided(ap, b):
            return ap.rearrange("p (l s) -> p s l", s=4)[:, b, :]

        q_c = region(R0, 2, 2, T)
        k_c = region(R0 + 2048, 2, 2, T + P)
        v_c = region(R0 + 4608, 2, 2, TB + 1, P)
        lat = region(R0 + 7168, 2, QC + KVC, T)
        pt_c = [[oc[:, part, 2 + slot, :] for part in range(2)] for slot in range(2)]
        k_d = region(R0 + 2048, 2, 2, T)
        v_d = region(R0 + 4096, 2, 2, TB, HD)
        q_d = q_c
        pt_d = xg[:, :, :, :].rearrange("p s (c k) t -> p s c k t", c=2)
        stats_v = stats[:, :].rearrange("p (r s g h b) -> p r s g h b", r=2, s=2, g=3, h=2)
        nat_v = nat[:, :].rearrange("p (s g x) -> p s g x", s=2, g=3)
        tq_c = [tq[:, par, HD:HD + T] for par in range(2)]

        def tiles_of(u):
            return D_TILES if U_D <= u < U_WO1 else DOWN_HALF if U_DN0 <= u < U_C or u >= U_DN1 else KC

        def sp_bias_c(sp, load_bias, e):
            c, hd = e // 2, e % 2
            p, g = c // 3, c % 3
            head, slot = 4 * g + 2 * p + hd, e % 2
            if e >= 2:
                sp.wait_ge(scored, S_C + c_last_tile(e - 2) + 1)
            else:
                sp.wait_ge(scored, S_C)
            if g == 0:
                length = VECS[2][0]
                src = bass.AP(rep_dram.tensor, REP_AT[2] + head * P * length + P - 1, [[length - 1, P], [0, TB], [1, 2 * P]])
                sp.dma_start(bias[:, slot, :].rearrange("p (b j) -> p b j", b=TB), src).then_inc(bias_loaded[slot], 16)
            else:
                load_bias(2 + g, head, slot, P)

        def sp_layer1(sp, load_bias):
            sp.wait_ge(h_lo, FC)
            sp.dma_start(pn[:, 0, :], io["comb_select"]).then_inc(select_loaded, 16)
            for u in range(U_C, U_C + 4):
                load_unit(sp, u, u % 2)
            for c in range(6):
                for u in range(U_C + 3 * c + 4, U_C + 3 * c + 7):
                    load_unit(sp, u, u % 2)
                for e in (2 * c + 2, 2 * c + 3):
                    if e < 12:
                        sp_bias_c(sp, load_bias, e)
            sp.wait_ge(scored, S_D)
            sp.dma_start(bias[:, :, :].rearrange("p a t -> p (a t)")[:, 0:3 * T],
                         io["rotary"].rearrange("p a t -> p (a t)")).then_inc(rotary_loaded, 16)
            for u in range(U_C + 22, U_D):
                load_unit(sp, u, u % 2)
            stream_loop(sp, "w_d", U_D, U_D, U_WO1)
            stream_loop(sp, "w_o1", U_WO1, U_WO1, U_GU1)
            stream_loop(sp, "w_gu1", U_GU1, U_GU1, U_DN1)
            stream_loop(sp, "w_dn1", U_DN1, U_DN1, U_END)

        def c_step(pe, u, kc):
            j = u - U_C
            free = (proj_t, T_AB + j - 1) if j >= 2 else (x_added, 8 * 2 + 7 + j)
            unit_step(pe, u, kc, KC, g_bank[j % 2], xg_parts, u % 2, free=free, chunks=16 if j == 0 else None)

        def pe_layer1(pe):
            for j in range(3):
                for kc in range(KC):
                    if (j, kc) == BROADCAST_AT:
                        pe_broadcast(pe, NORM_AT[2], sc[:, 2, :])
                    c_step(pe, U_C + j, kc)
                if j == 0:
                    pe.wait_ge(acc_added, 27)
                    pe_stat(pe, NORM_AT[2], sc[:, 3, :])
            pe.wait_ge(k_pads_zeroed, 1)
            for t in range(len(C_TILE_LIST)):
                c, g, hd, blocks = c_tile(t)
                s = S_C + t
                rows = slice(hd * HD, (hd + 1) * HD)
                if C_TILE_LIST[t][1] == 0:
                    pe.wait_ge(qk_lo, QK_C + 2 * c + 2)
                pe.wait_ge(scored, s - 1)
                q, k = q_c[rows, c % 2], k_c[rows, c % 2]
                for i, b in enumerate(blocks):
                    if g == 0:
                        args = [q[:, x, b * P:(b + 1) * P] for x in range(2)] + [k[:, x, b * P:b * P + 2 * P] for x in range(2)]
                        out = s_bank[s % 2][:, 2 * P * i:2 * P * (i + 1)]
                    else:
                        args = [strided(q[:, x, :], b) for x in range(2)] + [strided(k[:, x, HD:HD + T], b) for x in range(2)]
                        out = s_bank[s % 2][:, P * i:P * (i + 1)]
                    mm = three(pe, out, *args, True, True)
                mm.then_inc(s_ready, 1)
                for step in c_steps(t):
                    c_step(pe, U_C + 3 * (c + 1) + step // KC, step % KC)
                for a in range(*LAT_AHEAD[0][t - C_TILE_AT[5]]) if t >= C_TILE_AT[5] else ():
                    lat_step(pe, a // KC, a % KC)
                if C_TILE_AT[3] < t < C_TILE_AT[4]:
                    pe_comb_spread(pe, 0, t - C_TILE_AT[3] - 1)
                if t >= 1:
                    pe_pv_c(pe, t - 1)
                if C_TILE_LIST[t][1] == 0:
                    u = U_C + 3 * c + 2
                    pe.wait_ge(proj_t, T_AB + 3 * c + 3)
                    src = tq[:, (u - U_C) % 2, :]
                    if g == 0:
                        pe_set(pe, c_sets["v", c, 0], lambda x: src[:, x * P:(x + 1) * P], TB)
                        pe_set(pe, c_sets["v", c, 1], lambda x: src[:, TB * P:(TB + 1) * P], 1)
                    else:
                        pe_set(pe, c_sets["v", c, 0], lambda x: strided(src[:, HD:HD + T], x), TB)
                pe.wait_ge(exp_done, s + 1)
                pe_set(pe, c_sets["t", t], lambda x: sc[:, t % 2, x * P:(x + 1) * P], TB)
                if t == C_TILE_AT[3]:
                    pe_comb_pick(pe, 0)

            for c in range(N_LAT):
                for kc in range(KC):
                    if (c, kc) == LAT_AHEAD[2]:
                        pe_pv_c(pe, len(C_TILE_LIST) - 1)
                    if (c, kc) >= LAT_AHEAD[1]:
                        lat_step(pe, c, kc)
                if c == 0:
                    pe_comb_pick(pe, 1)
                if c == 3:
                    pe.wait_ge(mix_done, 6)
                    pe.wait_ge(lat_acc, 1)
                    pe_stat(pe, 7, sc[:, 1, :])
                if c == 4:
                    pe_broadcast(pe, 7, sc[:, 2, :])
                if c == 5:
                    pe.wait_ge(lat_acc, 2)
                    pe_stat(pe, 8, sc[:, 0, :])
            pe_broadcast(pe, 8, sc[:, 2, :])

            for kc in range(D_TILES):
                d_step(pe, 0, kc, U_D % 2)
            pe.wait_ge(proj_t, PROJ_D + 2)
            pe.wait_ge(bc_used, 9)
            pe_set_at(pe, m_bank, lambda x: tq[:, 1, x * P:(x + 1) * P], TB)
            pe_head_d(pe, 0, 0)
            pe_head_d(pe, 1, 1)
            with pe.Fori(1, D_HEADS // 2 - 1) as i:
                for par in range(2):
                    pe_head_d(pe, i * 2 + par, par)
            for h in range(D_HEADS - 2, D_HEADS):
                pe_head_d(pe, h, h % 2)
            last = D_HEADS - 1
            for m, kc in AHEAD[7:9]:
                wo_tile(pe, 1, m, m, kc)
            d_tile_set(pe, last, 3)
            for m, kc in AHEAD[9:]:
                wo_tile(pe, 1, m, m, kc)
            pe_pv_d(pe, last, 1)
            pe_wo(pe, 1)
            pe_ffn(pe, 1)
            pe.wait_ge(acc_added, 9 * 5 - 1)
            pe.wait_ge(bc_used, NORM_AT[4])
            pe.wait_ge(sq_done, 8 * 5)
            for b in range(TB):
                cols = slice(b * P, (b + 1) * P)
                pe.matmul(m_bank[:, b:b + 1], sc[:, 3, cols], ones[:, 0:1], start=True, stop=False)
                mm = pe.matmul(m_bank[:, b:b + 1], tq[:, (KC - 1) % 2, cols], ones[:, 0:1], start=False, stop=True)
            mm.then_inc(stat_ready, 1)
            pe_broadcast(pe, NORM_AT[4], sc[:, 2, :])

        LAT_AHEAD = (((0, 5), (5, 10)), (1, 2), (1, 5))

        def lat_step(pe, c, kc):
            u = U_LAT + c
            if kc == 0 and c >= 2:
                pe.wait_ge(lat_sq, min(c - 1, QC + KVC))
            if (c, kc) in SPREAD_AT:
                pe_comb_spread(pe, 1, SPREAD_AT.index((c, kc)))
            unit_step(pe, u, kc, KC, g_bank[(u - U_C) % 2], xg_parts, u % 2, free=(proj_t, T_AB + u - U_C - 1))

        SPREAD_AT = ((2, 2), (2, 7), (3, 5))

        PROJ_D = T_AB + N_C + N_LAT

        def pe_pv_c(pe, t):
            c, g, hd, blocks = c_tile(t)
            pe.wait_ge(t_free, c_sets["t", t] + 1)
            pe.wait_ge(o_copied, PV_C + t)
            cols = slice(hd * HD, (hd + 1) * HD)
            v, pt = v_c[:, c % 2], pt_c[t % 2]
            for i, b in enumerate(blocks):
                out = o_bank[0:HD, b * P:(b + 1) * P]
                for x in range(2 if g == 0 else 1):
                    j = (2 * i + x) if g == 0 else i
                    mm = three(pe, out, v[:, 0, b + x, cols], v[:, 1, b + x, cols],
                               pt[0][:, j * P:(j + 1) * P], pt[1][:, j * P:(j + 1) * P], x == 0, g != 0 or x == 1)
            mm.then_inc(pv_done, 1)

        def pe_comb_pick(pe, p):
            pe.wait_ge(select_loaded, 16)
            pe.wait_ge(exp_done, S_C + C_TILE_AT[3 * (p + 1)])
            if p == 0:
                pe.wait_ge(bc_used, NORM_AT[2] + 1)
            else:
                pe.wait_ge(mix_done, 3)
            for g in (1, 2):
                for b in range(TB):
                    i = (g - 1) * TB + b
                    mm = pe.matmul(m_bank[:, i * 16:(i + 1) * 16], pn[:, 0, b * P:(b + 1) * P],
                                   stats_v[:, p, :, g, :, :], start=True, stop=True)
            mm.then_inc(comb_mm, 1)

        def pe_comb_spread(pe, p, g):
            if g >= 1:
                pe.wait_ge(mix_done, 3 * p + g)
            for hd in range(2):
                pe.wait_ge(comb_diag, 6 * p + 2 * g + hd + 1)
                mm = pe.matmul(m_bank[hd * HD:(hd + 1) * HD, :], ones[:, 0:HD], sc[:, 2 + hd, :], start=True, stop=True)
            mm.then_inc(comb_bc, 1)

        def d_step(pe, h, kc, slot):
            u = h + U_D
            if kc == 0:
                pe.wait_ge(w_lo_done, u + 1)
                pe.wait_ge(qk_lo, QK_LAT + QC + KVC)
                pe.wait_ge(proj_t, h * 2 + PROJ_D)
            w_h, w_l = wtile(slot, kc)
            q = kc < QC
            mm = three(pe, g_bank[0 if q else 1][:, :], w_h, w_l, lat[:, 0, kc, :], lat[:, 1, kc, :],
                       kc in (0, QC), kc in (QC - 1, D_TILES - 1))
            if kc == QC - 1:
                mm.then_inc(q_done, 1)
            if kc == D_TILES - 1:
                mm.then_inc(unit_done, 1)

        def set_d(h, b):
            if isinstance(h, int) and h == D_HEADS - 1 and b >= 2:
                return SET_D + 5 * h + b + 1
            return h * 5 + (SET_D + {0: 1, 1: 2, -1: 3, 2: 4, 3: 5}[b])

        def is_last(h):
            return isinstance(h, int) and h == D_HEADS - 1

        def pe_set_at(pe, bank, src, blocks):
            for c in range(blocks):
                mm = pe.transpose(bank[:, c * P:(c + 1) * P], src(c), ident[:, :])
            mm.then_inc(t_ready, 1)

        def d_tile_set(pe, h, b):
            pe.wait_ge(p_ready, h * 4 + (AB_TILES + b + 1))
            if b >= 2:
                pe.wait_ge(t_free, set_d(h, b - 2) + 1)
            elif isinstance(h, int) and h == 0:
                pe.wait_ge(t_free, SET_D)
            else:
                pe.wait_ge(t_free, set_d(h - 1, b + 2) + 1)
            pe_set_at(pe, t_bank[b % 2], lambda x: pn[:, b % 2, x * P:(x + 1) * P], TB)

        def d_value_set(pe, h):
            pe.wait_ge(proj_t, h * 2 + (PROJ_D + 4))
            pe.wait_ge(t_free, (SET_D if isinstance(h, int) and h == 0 else set_d(h - 1, -1)) + 1)
            pe_set_at(pe, m_bank, lambda x: tq[:, 1, x * P:(x + 1) * P], TB)

        def pe_pv_d(pe, h, par):
            pe.wait_ge(t_free, set_d(h, 3) + 1)
            pe.wait_ge(o_copied, h + PV_D)
            for kc in range(TB):
                mm = three(pe, o_bank[0:HD, :], v_d[:, par, 0, kc, :], v_d[:, par, 1, kc, :],
                           pt_d[:, par, 0, kc, :], pt_d[:, par, 1, kc, :], kc == 0, kc == TB - 1)
            mm.then_inc(pv_done, 1)

        def pe_head_d(pe, h, par):
            first, last = isinstance(h, int) and h == 0, is_last(h)
            nslot = (U_D + par + 1) % 2
            pe.wait_ge(qk_lo, h * 2 + (QK_D + 2))
            for b in range(TB):
                s = h * 4 + (S_D + b)
                bank = s_bank[(S_D + b) % 2]
                pe.wait_ge(exp_done, s - 1)
                cols = slice(b * P, (b + 1) * P)
                three(pe, bank[:, :], q_d[:, par, 0, cols], q_d[:, par, 1, cols], k_d[:, par, 0, :], k_d[:, par, 1, :],
                      True, True).then_inc(s_ready, 1)
                if not last:
                    for kc in (range(QC), range(QC, D_TILES), (), ())[b]:
                        d_step(pe, h + 1, kc, nslot)
                else:
                    for m, kc in (AHEAD[0:3], AHEAD[3:5], (), AHEAD[5:7])[b]:
                        wo_tile(pe, 1, m, m, kc)
                if b == 0 and not first:
                    d_tile_set(pe, h - 1, 3)
                if b == 2 and not first:
                    pe_pv_d(pe, h - 1, 1 - par)
                if b == 3 and not last:
                    d_value_set(pe, h)
                if b >= 1:
                    d_tile_set(pe, h, b - 1)

        def act_evac_c(act, u):
            prep_hi(act, u + 2, u % 2, tiles_of(u + 2))
            if kind_c(u) != "v":
                j = u - U_C
                act.wait_ge(proj_t, T_AB + j + 1)
                act.activation(qk_dst_c(u)[0], tq_c[j % 2], ACT.Copy).then_inc(qk_hi, 1)

        def qk_dst_c(u):
            slot = ((u - U_C) // 3) % 2
            if kind_c(u) == "q":
                return q_c[:, slot, 0, :], q_c[:, slot, 1, :]
            return k_c[:, slot, 0, HD:HD + T], k_c[:, slot, 1, HD:HD + T]

        def act_layer1(act):
            for j in range(3):
                act_evac_c(act, U_C + j)
            for t in range(len(C_TILE_LIST)):
                c, g, hd, blocks = c_tile(t)
                act.wait_ge(scored, S_C + t + 1)
                w = (2 if g == 0 else 1) * P
                for i, b in enumerate(blocks):
                    ins = act.activation(sc[:, t % 2, i * w:(i + 1) * w], sc[:, t % 2, i * w:(i + 1) * w], ACT.Exp, scale=-1.0,
                                         bias=stats_v[:, c // 3, 0, g, hd, b:b + 1],
                                         accum_out=stats_v[:, c // 3, 1, g, hd, b:b + 1])
                ins.then_inc(exp_done, 1)
                for u in c_done_units(t):
                    act_evac_c(act, u)
                if t >= 1:
                    act_o_c(act, t - 1)
                if C_TILE_LIST[t][1] == 0:
                    act_set(act, c_sets["v", c, 0], v_c[:, c % 2, 0, 0:TB, :], bank3(t_bank[c_sets["v", c, 0] % 2], TB))
                    if g == 0:
                        act_set(act, c_sets["v", c, 1], v_c[:, c % 2, 0, TB, :], t_bank[c_sets["v", c, 1] % 2][:, 0:P])
                act.wait_ge(pv_done, PV_C + t - 1)
                act_set(act, c_sets["t", t], pt_c[t % 2][0], t_bank[c_sets["t", t] % 2][:, :])
                if t == C_TILE_AT[3]:
                    act_comb_exp(act, 0)
                if t == C_TILE_AT[4]:
                    act_oc_c(act, 0)
            act_o_c(act, len(C_TILE_LIST) - 1)
            for c in range(N_LAT):
                u = U_LAT + c
                prep_hi(act, u + 2, u % 2, tiles_of(u + 2))
                if c < QC + KVC:
                    act.wait_ge(unit_done, u + 1)
                    dst = lat_sq_dst(c)
                    if c == QC:
                        act.wait_ge(mix_done, 6)
                    if c == 2:
                        act.wait_ge(lat_add, 1)
                    act.activation(dst, g_bank[(u - U_C) % 2][:, :], ACT.Square).then_inc(lat_sq, 1)
                    act.wait_ge(proj_t, T_AB + u - U_C + 1)
                    act.activation(lat[:, 0, c, :], tq_c[(u - U_C) % 2], ACT.Copy).then_inc(qk_hi, 1)
                if c == 0:
                    act_comb_exp(act, 1)
                if c == 4:
                    act_oc_c(act, 1)
            act.wait_ge(kpe_ready, 1)
            for slot in range(2):
                ins = act.activation(k_d[:, slot, 0, :], og[:, 1, :], ACT.Copy)
            ins.then_inc(qk_hi, 1)

            act_q_d(act, 0, 0)
            act_kv_d(act, 0, 0)
            act_set(act, SET_D, v_d[:, 0, 0, :, :], bank3(m_bank, TB)[:, :, HD:P])
            act_head_d(act, 0, 0)
            act_head_d(act, 1, 1)
            with act.Fori(1, D_HEADS // 2 - 1) as i:
                for par in range(2):
                    act_head_d(act, i * 2 + par, par, i)
            for h in range(D_HEADS - 2, D_HEADS):
                act_head_d(act, h, h % 2)
            last = D_HEADS - 1
            act_pt_d(act, last, 1, 2)
            act_o_d(act, last - 1, 0, D_HEADS // 2 - 1)
            act_pt_d(act, last, 1, 3)
            act_o_d(act, last, 1, D_HEADS // 2 - 1)
            act_wo(act, 1)
            act_ffn(act, 1)

        def lat_sq_dst(c):
            return (sc[:, 1, :], sc[:, 0, :], sc[:, 0, :], og[:, 2, :], og[:, 1, :])[c]

        def act_comb_exp(act, p):
            act.wait_ge(comb_diff, p + 1)
            act.activation(comb_w[:, 0:24], comb_w[:, 0:24], ACT.Exp).then_inc(comb_exp, 1)

        def act_oc_c(act, p):
            act.wait_ge(mix_done, 3 * (p + 1))
            act.activation(oc[:, 0, p, :], mix[:, :], ACT.Copy).then_inc(oc_hi, 1)

        def act_o_c(act, t):
            c, g, hd, blocks = c_tile(t)
            p = c // 3
            act.wait_ge(pv_done, PV_C + t + 1)
            if p == 1:
                act.wait_ge(mix_done, g + 1)
            rows = slice(hd * HD, (hd + 1) * HD)
            if g == 0:
                cols = slice(blocks[0] * P, blocks[0] * P + 2 * P)
                act.activation(og[rows, 0, cols], o_bank[0:HD, cols], ACT.Copy).then_inc(o_copied, 1)
            else:
                act.activation(og[rows, g, :].rearrange("p (l s) -> p s l", s=4),
                               o_bank[0:HD, :].rearrange("p (s l) -> p s l", s=4), ACT.Copy).then_inc(o_copied, 1)

        def act_q_d(act, h, par):
            act.wait_ge(proj_t, h * 2 + (PROJ_D + 1))
            act.activation(q_d[:, par, 0, :], tq[:, 0, 0:T], ACT.Copy).then_inc(qk_hi, 1)

        def act_kv_d(act, h, par):
            act.wait_ge(proj_t, h * 2 + (PROJ_D + 2))
            act.activation(k_d[0:HD, par, 0, :], tq[0:HD, 1, 0:T], ACT.Copy).then_inc(qk_hi, 1)

        def act_pt_d(act, h, par, b):
            n = set_d(h, b)
            bank = t_bank[b % 2]
            act.wait_ge(t_ready, n + 1)
            act.activation(pt_d[:, par, 0, :, b * P:(b + 1) * P], bank3(bank, TB), ACT.Copy).then_inc(pt_hi, 1)

        def act_o_d(act, h, par, i=None):
            act.wait_ge(pv_done, h + (PV_D + 1))
            if par == 0:
                act.wait_ge(oc_lo, (10 + h // 2) if isinstance(h, int) else i + 10)
            act.activation(og[par * HD:(par + 1) * HD, 0, :], o_bank[0:HD, :], ACT.Copy).then_inc(o_copied, 1)
            if par:
                act.wait_ge(o_copied, h + (PV_D + 1))
                if isinstance(i, int):
                    dst = oc[:, 0, 2 + i, :]
                else:
                    act.nop(nofuse=True)
                    dst = oc[:, 0, bass.ds(i + 2, 1), :].rearrange("p a t -> p (a t)")
                act.activation(dst, og[:, 0, :], ACT.Copy).then_inc(oc_hi, 1)

        def act_head_d(act, h, par, i=None):
            static = isinstance(h, int)
            first, last = static and h == 0, is_last(h)
            for b in range(TB):
                s = h * 4 + (S_D + b)
                c = (S_D + 4 * par + b) % 8
                if b < 2 and not first:
                    act_pt_d(act, h - 1, 1 - par, 2 + b)
                if b >= 2:
                    if b == 2 and not (static and h < 2):
                        act.wait_ge(pv_done, h + (PV_D - 1))
                    act_pt_d(act, h, par, b - 2)
                act.wait_ge(scored, s + 1)
                act.activation(sc[:, b, :], s_bank[(S_D + b) % 2][:, :], ACT.Exp, bias=neg_max[:, c:c + 1],
                               accum_out=row_sum[:, c:c + 1]).then_inc(exp_done, 1)
                if b == 0:
                    if not (static and h < 2):
                        act_o_d(act, h - 2, par, h // 2 - 1 if static else i - 1)
                    prep_hi(act, h + (U_D + 2), (U_D + par) % 2, KC if static and h + 2 >= D_HEADS else D_TILES,
                            None if static else i + (U_D + par + 2) // 2)
                if b == 1 and not last:
                    act_q_d(act, h + 1, 1 - par)
                if b == 2 and not last:
                    act_kv_d(act, h + 1, 1 - par)
                if b == 3 and not last:
                    if not first:
                        act.wait_ge(pv_done, h + PV_D)
                    act.wait_ge(t_ready, set_d(h, -1) + 1)
                    act.activation(v_d[:, 1 - par, 0, :, :], bank3(m_bank, TB)[:, :, HD:P], ACT.Copy).then_inc(pt_hi, 1)

        def pool_evac_c(pool, u):
            prep_lo(pool, u + 2, u % 2, tiles_of(u + 2))
            if kind_c(u) != "v":
                i = qk_index_c(u)
                pool.wait_ge(qk_hi, i + 1)
                hi, lo = qk_dst_c(u)
                pool.tensor_tensor(lo, tq_c[(u - U_C) % 2], hi.bitcast(F32), ALU.subtract).then_inc(qk_lo, 1)

        def pool_layer1(pool):
            pool_root(pool, NORM_AT[2])
            for j in range(3):
                pool_evac_c(pool, U_C + j)
            for t in range(len(C_TILE_LIST)):
                for u in c_done_units(t):
                    pool_evac_c(pool, u)
                if t == C_TILE_AT[4]:
                    pool_oc_lo_c(pool, 0)
            for c in range(N_LAT):
                u = U_LAT + c
                prep_lo(pool, u + 2, u % 2, tiles_of(u + 2))
                if c in (1, 2):
                    pool.wait_ge(lat_sq, c + 1)
                    if c == 2:
                        pool.wait_ge(lat_add, 1)
                    pool.tensor_tensor(sc[:, 1, :], sc[:, 1, :], sc[:, 0, :], ALU.add).then_inc(lat_add if c == 1 else lat_acc, 1)
                if c == 4:
                    pool.wait_ge(lat_sq, 5)
                    pool.wait_ge(lat_acc, 1)
                    pool.tensor_tensor(sc[:, 0, :], og[:, 2, :], og[:, 1, :], ALU.add).then_inc(lat_acc, 1)
                if c < QC + KVC:
                    pool.wait_ge(qk_hi, QK_LAT + c + 1)
                    pool.tensor_tensor(lat[:, 1, c, :], tq_c[(u - U_C) % 2], lat[:, 0, c, :].bitcast(F32),
                                       ALU.subtract).then_inc(qk_lo, 1)
                if c == 4:
                    pool_oc_lo_c(pool, 1)
                if c == 3:
                    pool_root(pool, 7)
                if c == 5:
                    pool_root(pool, 8)
            pool.wait_ge(qk_hi, QK_D)
            for slot in range(2):
                ins = pool.tensor_tensor(k_d[:, slot, 1, :], og[:, 1, :], k_d[:, slot, 0, :].bitcast(F32), ALU.subtract)
            ins.then_inc(qk_lo, 1)
            pool_qk_d(pool, 0, 0)
            pool_head_d(pool, 0, 0)
            pool_head_d(pool, 1, 1)
            with pool.Fori(1, D_HEADS // 2 - 1) as i:
                for par in range(2):
                    pool_head_d(pool, i * 2 + par, par, i)
            for h in range(D_HEADS - 2, D_HEADS):
                pool_head_d(pool, h, h % 2)
            pool_wo(pool, 1)
            pool_ffn(pool, 1)
            pool_root(pool, NORM_AT[4])

        def pool_oc_lo_c(pool, p):
            pool_oc_lo(pool, p, mix[:, :], 8)

        def pool_qk_d(pool, h, par):
            pool.wait_ge(qk_hi, h * 2 + (QK_D + 1))
            pool.tensor_tensor(q_d[:, par, 1, :], tq[:, 0, 0:T], q_d[:, par, 0, :].bitcast(F32), ALU.subtract).then_inc(qk_lo, 1)
            pool.wait_ge(qk_hi, h * 2 + (QK_D + 2))
            pool.tensor_tensor(k_d[0:HD, par, 1, :], tq[0:HD, 1, 0:T], k_d[0:HD, par, 0, :].bitcast(F32),
                               ALU.subtract).then_inc(qk_lo, 1)

        def pool_head_d(pool, h, par, i=None):
            static = isinstance(h, int)
            if par == 1 and not (static and h < 2):
                if static:
                    pool_oc_lo(pool, 1 + h // 2, og[:, 0, :], 8)
                else:
                    pool.wait_ge(oc_hi, i + (8 + 2))
                    dst = oc[:, 1, bass.ds(i + 1, 1), :].rearrange("p a t -> p (a t)")
                    src = oc[:, 0, bass.ds(i + 1, 1), :].rearrange("p a t -> p (a t)")
                    pool.nop(nofuse=True)
                    pool.tensor_tensor(dst, og[:, 0, :], src.bitcast(F32), ALU.subtract).then_inc(oc_lo, 1)
            prep_lo(pool, h + (U_D + 2), (U_D + par) % 2, KC if static and h + 2 >= D_HEADS else D_TILES)
            if not is_last(h):
                pool_qk_d(pool, h + 1, 1 - par)

        def dve_evac_c(dve, u):
            j = u - U_C
            dve.wait_ge(unit_done, u + 1)
            if j >= 2 and kind_c(u - 2) != "v":
                dve.wait_ge(qk_lo, qk_index_c(u - 2) + 1)
            scale = HD ** -0.5 if kind_c(u) == "q" else 1.0
            dve.scalar_tensor_tensor(tq_c[j % 2], g_bank[j % 2][:, :], scale, rstd[:, :], ALU.mult, ALU.mult).then_inc(proj_t, 1)

        def dve_comb(dve, p, step):
            if step >= 1:
                dve_mix(dve, p, step - 1)
            if step == 0:
                dve.wait_ge(comb_mm, p + 1)
                if p == 1:
                    dve.wait_ge(mix_done, 3)
                m = m_bank[:, 0:P].rearrange("p (g x b) -> p g x b", g=2, b=TB)
                dve.tensor_tensor(picked[:, :].rearrange("p (g x b) -> p g x b", g=2, b=TB), m,
                                  masks[:, :].unsqueeze(1).unsqueeze(1).broadcast_to([P, 2, 16, TB]),
                                  ALU.mult).then_inc(comb_step, 1)
                dve.wait_ge(comb_step, 7 * p + 1)
                for g in (1, 2):
                    out = nat[:, :].rearrange("p (s g h b) -> p g b s h", s=2, g=3, h=2)[:, g]
                    dve.tensor_reduce(out, picked[:, (g - 1) * HD:g * HD].rearrange("p (c s h b) -> p c s h b", c=TB, s=2, h=2),
                                      AX.X, ALU.add)
                own = stats[:, :].rearrange("p (r s g x) -> p r s g x", r=2, s=2, g=3)[:, p, :, 0, :]
                dve.tensor_copy(nat_v[:, :, 0, :], own).then_inc(comb_step, 1)
                dve.wait_ge(comb_step, 7 * p + 2)
                dve.tensor_reduce(least[:, 0:8], nat_v[:, 0].rearrange("p g x -> p x g"), AX.X, ALU.min).then_inc(comb_step, 1)
                dve.wait_ge(comb_step, 7 * p + 3)
                w3 = comb_w[:, 0:24].rearrange("p (g x) -> p g x", g=3)
                dve.tensor_tensor(w3, least[:, 0:8].unsqueeze(1).broadcast_to([P, 3, 8]), nat_v[:, 0],
                                  ALU.subtract).then_inc(comb_diff, 1)
                dve.wait_ge(comb_exp, p + 1)
                dve.tensor_tensor(nat_v[:, 0], w3, nat_v[:, 1], ALU.mult).then_inc(comb_step, 1)
                dve.wait_ge(comb_step, 7 * p + 4)
                dve.tensor_reduce(least[:, 8:16], nat_v[:, 0].rearrange("p g x -> p x g"), AX.X, ALU.add).then_inc(comb_step, 1)
                dve.wait_ge(comb_step, 7 * p + 5)
                dve.reciprocal(least[:, 0:8], least[:, 8:16]).then_inc(comb_step, 1)
                dve.wait_ge(comb_step, 7 * p + 6)
                dve.tensor_tensor(w3, w3, least[:, 0:8].unsqueeze(1).broadcast_to([P, 3, 8]), ALU.mult).then_inc(comb_step, 1)
                dve.wait_ge(comb_step, 7 * p + 7)
            for hd in range(2 if step < 3 else 0):
                at = 8 * step + 4 * hd
                dve.tensor_tensor(sc[:, 2 + hd, :].rearrange("p (b t) -> p b t", b=TB),
                                  ident[:, :].unsqueeze(1).broadcast_to([P, TB, P]),
                                  comb_w[:, at:at + 4].unsqueeze(2).broadcast_to([P, TB, P]), ALU.mult).then_inc(comb_diag, 1)

        def dve_mix(dve, p, g):
            dve.wait_ge(comb_bc, 3 * p + g + 1)
            dve.wait_ge(o_copied, PV_C + C_TILE_AT[3 * p + 3])
            if g == 0:
                if p == 1:
                    dve.wait_ge(oc_lo, 9)
                dve.tensor_tensor(mix[:, :], og[:, 0, :], m_bank[:, :], ALU.mult).then_inc(mix_done, 1)
            else:
                dve.tensor_tensor(og[:, g, :], og[:, g, :], m_bank[:, :], ALU.mult).then_inc(mix_part, 1)
                dve.wait_ge(mix_part, 2 * p + g)
                dve.wait_ge(mix_done, 3 * p + g)
                dve.tensor_tensor(mix[:, :], mix[:, :], og[:, g, :], ALU.add).then_inc(mix_done, 1)

        def dve_bias_c(dve, e):
            g, slot = (e // 2) % 3, e % 2
            dve.wait_ge(bias_loaded[slot], 16 * c_bias_count(e))
            if g == 0:
                dve.memset(bias[:, slot, 0:HD], NEG)
                dve.memset(bias[:, slot, 1024 - HD:1024], NEG).then_inc(edges_closed, 1)
                dve.wait_ge(edges_closed, {0: 1, 1: 2, 6: 3, 7: 4}[e])

        def dve_layer1(dve):
            dve_rstd(dve, NORM_AT[2])
            dve.tensor_tensor(r_sq[:, :], inv_rms[:, :], inv_rms[:, :], ALU.mult)
            for par in range(2):
                dve.memset(tq[:, par, 0:HD], 0.0)
                dve.memset(tq[:, par, HD + T:P + T], 0.0)
                for x in range(2):
                    dve.memset(k_c[:, par, x, 0:HD].bitcast(F32), 0.0)
                    ins = dve.memset(k_c[:, par, x, HD + T:P + T].bitcast(F32), 0.0)
            ins.then_inc(k_pads_zeroed, 1)
            for j in range(3):
                dve_evac_c(dve, U_C + j)
            for t in range(len(C_TILE_LIST)):
                c, g, hd, blocks = c_tile(t)
                e = 2 * c + hd
                if blocks[0] == 0:
                    dve_bias_c(dve, e)
                dve.wait_ge(s_ready, S_C + t + 1)
                w = (2 if g == 0 else 1) * P
                for i, b in enumerate(blocks):
                    table = bias[:, e % 2, b * w:(b + 1) * w] if g == 0 else bias[:, e % 2, 0:P]
                    ins = dve.tensor_tensor_reduce(out=sc[:, t % 2, i * w:(i + 1) * w],
                                                   in0=s_bank[(S_C + t) % 2][:, i * w:(i + 1) * w],
                                                   in1=table, scale=-1.0, scalar=BIG, op0=ALU.add, op1=ALU.min,
                                                   accum_out=stats_v[:, c // 3, 0, g, hd, b:b + 1])
                ins.then_inc(scored, 1)
                for u in c_done_units(t):
                    dve_evac_c(dve, u)
                if C_TILE_AT[3] < t < C_TILE_AT[4]:
                    dve_comb(dve, 0, t - C_TILE_AT[3])
                if C_TILE_LIST[t][1] == 0:
                    k = c_sets["v", c, 0]
                    dve_set(dve, k, v_c[:, c % 2, 1, 0:TB, :], bank3(t_bank[k % 2], TB), v_c[:, c % 2, 0, 0:TB, :])
                    if g == 0:
                        k = c_sets["v", c, 1]
                        dve_set(dve, k, v_c[:, c % 2, 1, TB, :], t_bank[k % 2][:, 0:P], v_c[:, c % 2, 0, TB, :])
                k = c_sets["t", t]
                dve_set(dve, k, pt_c[t % 2][1], t_bank[k % 2][:, :], pt_c[t % 2][0])
                if t == C_TILE_AT[3]:
                    dve_comb(dve, 0, 0)
            for c in range(N_LAT):
                u = U_LAT + c
                j = u - U_C
                bank = g_bank[j % 2]
                if c == 3:
                    dve_comb(dve, 1, 3)
                if c in (4, 6):
                    dve_diag(dve, 7 + (c - 4) // 2, sc[:, 2, :])
                if c == 5:
                    dve.wait_ge(rotary_loaded, 16)
                    dve.wait_ge(bc_ready, 8)
                    dve.tensor_tensor(bias[:, 0, 0:T], bias[:, 0, 0:T], m_bank[:, :], ALU.mult).then_inc(bc_used, 1)
                dve.wait_ge(unit_done, u + 1)
                if c < QC + KVC:
                    dve.wait_ge(lat_sq, c + 1)
                    if c >= 2:
                        dve.wait_ge(qk_lo, QK_LAT + c - 1)
                    elif kind_c(u - 2) != "v":
                        dve.wait_ge(qk_lo, qk_index_c(u - 2) + 1)
                    dve.scalar_tensor_tensor(tq_c[j % 2], bank[:, :], gains[:, G_QN + c:G_QN + c + 1], rstd[:, :],
                                             ALU.mult, ALU.mult).then_inc(proj_t, 1)
                else:
                    dve.wait_ge(qk_lo, QK_LAT + c - 1)
                    dve.tensor_tensor(tq_c[j % 2], bank[:, :], rstd[:, :], ALU.mult).then_inc(proj_t, 1)
                    dve.wait_ge(rotary_loaded, 16)
                    dve.wait_ge(proj_t, T_AB + j + 1)
                    table = bias[:, 0, T:2 * T] if c == 5 else bias[:, 1, 0:T]
                    dve.tensor_tensor(tq_c[j % 2], tq_c[j % 2], table, ALU.mult).then_inc(kr_part, 1)
                if c < 3:
                    dve_comb(dve, 1, c)
                if c == 3:
                    dve_lat_mean(dve, 0, QC * P)
                if c == 5:
                    dve_lat_mean(dve, 1, KVC * P)
            dve.wait_ge(kr_part, 2)
            dve.tensor_tensor(og[:, 1, :], tq_c[0], tq_c[1], ALU.add).then_inc(kpe_ready, 1)
            dve.wait_ge(bc_ready, 9)
            dve.tensor_copy(rstd[:, :], m_bank[:, :]).then_inc(bc_used, 1)
            dve.wait_ge(bc_used, 9)
            dve_q_d(dve, 0)
            dve_kv_d(dve, 0)
            dve.wait_ge(pt_hi, SET_D + 1)
            dve.tensor_tensor(v_d[:, 0, 1, :, :], bank3(m_bank, TB)[:, :, HD:P], v_d[:, 0, 0, :, :].bitcast(F32),
                              ALU.subtract).then_inc(t_free, 1)
            dve_head_d(dve, 0, 0)
            dve_head_d(dve, 1, 1)
            with dve.Fori(1, D_HEADS // 2 - 1) as i:
                for par in range(2):
                    dve_head_d(dve, i * 2 + par, par)
            for h in range(D_HEADS - 2, D_HEADS):
                dve_head_d(dve, h, h % 2)
            last = D_HEADS - 1
            dve_norm_d(dve, last, 1, 3)
            dve_pt_d(dve, last, 1, 2)
            dve_pt_d(dve, last, 1, 3)
            dve_wo(dve, 1)
            dve_ffn(dve, 1)
            n = NORM_AT[4]
            dve_mean(dve, n, DM)
            dve_diag(dve, n, sc[:, 2, :])
            dve.wait_ge(bc_ready, n + 1)
            for m in range(KC):
                dve.scalar_tensor_tensor(xT[:, m, :], xT[:, m, :], gains[:, G_FINAL + m:G_FINAL + m + 1], m_bank[:, :],
                                         ALU.mult, ALU.mult).then_inc(final_ready, 1)

        def dve_lat_mean(dve, i, count):
            n = 7 + i
            dve.wait_ge(stat_ready, n + 1)
            dve.scalar_tensor_tensor(mean_sq[:, :], m_bank[:, 0:TB], 1.0 / count, r_sq[:, :], ALU.mult,
                                     ALU.mult).then_inc(lat_mean, 1)
            dve.wait_ge(lat_mean, i + 1)
            dve.tensor_scalar(mean_sq[:, :], mean_sq[:, :], EPS, None, ALU.add).then_inc(ms_ready, 1)

        def dve_q_d(dve, h):
            dve.wait_ge(q_done, h + 1)
            dve.wait_ge(qk_lo, h * 2 + (QK_D - 1))
            dve.tensor_tensor(tq[:, 0, 0:T], g_bank[0][:, :], bias[:, 0, 0:T], ALU.mult).then_inc(proj_t, 1)

        def dve_kv_d(dve, h):
            dve.wait_ge(unit_done, h + (U_D + 1))
            dve.wait_ge(qk_lo, h * 2 + QK_D)
            dve.tensor_tensor(tq[:, 1, 0:T], g_bank[1][:, :], rstd[:, :], ALU.mult).then_inc(proj_t, 1)

        def dve_pt_d(dve, h, par, b):
            n = set_d(h, b)
            bank = t_bank[b % 2]
            cols = slice(b * P, (b + 1) * P)
            dve.wait_ge(pt_hi, n + 1)
            dve.tensor_tensor(pt_d[:, par, 1, :, cols], bank3(bank, TB), pt_d[:, par, 0, :, cols].bitcast(F32),
                              ALU.subtract).then_inc(t_free, 1)

        def dve_norm_d(dve, h, par, b):
            s = h * 4 + (S_D + b)
            n = h * 4 + (AB_TILES + b)
            c = (S_D + 4 * par + b) % 8
            dve.wait_ge(exp_done, s + 1)
            dve.reciprocal(inv_sum[:, c:c + 1], row_sum[:, c:c + 1]).then_inc(recip_done, 1)
            dve.wait_ge(recip_done, n + 1)
            dve.tensor_scalar(pn[:, b % 2, :], sc[:, b, :], inv_sum[:, c:c + 1], None, ALU.mult).then_inc(p_ready, 1)

        def dve_head_d(dve, h, par):
            first, last = isinstance(h, int) and h == 0, is_last(h)
            for b in range(TB):
                s = h * 4 + (S_D + b)
                c = (S_D + 4 * par + b) % 8
                if b >= 1:
                    dve_norm_d(dve, h, par, b - 1)
                elif not first:
                    dve_norm_d(dve, h - 1, 1 - par, 3)
                dve.wait_ge(s_ready, s + 1)
                dve.tensor_reduce(neg_max[:, c:c + 1], s_bank[(S_D + b) % 2][:, :], AX.X, ALU.max,
                                  negate=True).then_inc(scored, 1)
                if b == 0 and not first:
                    dve.wait_ge(pt_hi, set_d(h - 1, -1) + 1)
                    dve.tensor_tensor(v_d[:, par, 1, :, :], bank3(m_bank, TB)[:, :, HD:P], v_d[:, par, 0, :, :].bitcast(F32),
                                      ALU.subtract).then_inc(t_free, 1)
                if b < 2 and not first:
                    dve_pt_d(dve, h - 1, 1 - par, 2 + b)
                if b >= 2:
                    dve_pt_d(dve, h, par, b - 2)
                if b == 1 and not last:
                    dve_q_d(dve, h + 1)
                if b == 2 and not last:
                    dve_kv_d(dve, h + 1)

        @block.sync
        def _(sp):
            sync_program(sp)

        @block.gpsimd
        def _(pool):
            gpsimd_program(pool)

        @block.scalar
        def _(act):
            scalar_program(act)

        @block.vector
        def _(dve):
            vector_program(dve)

        @block.tensor
        def _(pe):
            tensor_program(pe)

def t5_bucket(rel):
    nb = NB // 2
    max_exact = nb // 2
    n = np.abs(rel)
    nf = np.maximum(n, 1).astype(np.float32)
    large = max_exact + (np.log(nf / np.float32(max_exact)) / np.float32(math.log(MAX_DISTANCE / max_exact))
                         * np.float32(nb - max_exact)).astype(np.int32)
    large = np.minimum(large, nb - 1)
    return np.where(rel > 0, nb, 0) + np.where(n < max_exact, n, large)

def one_hot_table():
    table = np.zeros((NB + 1, VEC_LEN), np.float32)
    for (length, dilation, widest, _, _), at, centre in zip(VECS, VEC_AT, VEC_CENTRE):
        rel = np.arange(length) - centre
        row = np.where(np.abs(rel) <= widest, t5_bucket(rel * dilation), NB)
        if at == VEC_AT[4]:
            row = np.where(rel % 4 == 0, row, NB)
        table[row, at + np.arange(length)] = 1.0
    return table

def rotary_tables():
    half = D_ROPE // 2
    inv = np.float32(10000.0) ** (-np.arange(half, dtype=np.float32) / np.float32(half))
    angle = np.arange(T, dtype=np.float32)[:, None] * inv[None, :]
    cos, sin = np.cos(angle).T, np.sin(angle).T
    cos2, sin2 = np.concatenate([cos, cos]), np.concatenate([-sin, sin])
    scale = np.float32((D_NOPE + D_ROPE) ** -0.5)
    q_mult = np.concatenate([np.ones((D_NOPE, T), np.float32), cos2, sin2]) * scale
    k_cos = np.concatenate([cos2] * 4)
    k_sin = np.concatenate([sin2] * 4)
    return np.ascontiguousarray(np.stack([q_mult, k_cos, k_sin], axis=1).astype(np.float32))

def comb_select():
    select = np.zeros((P, TB, P), np.float32)
    masks = np.zeros((P, TB), np.float32)
    p = np.arange(P)
    for b in range(TB):
        select[(P * b + p) // 4, b, p] = 1.0
    masks[p, p % 4] = 1.0
    return select.reshape(P, TB * P), masks

def panels(w, cols=None):
    if cols is not None:
        w = w[:, cols]
    k, m = w.shape
    return np.ascontiguousarray(w.reshape(k // P, P, m // P, P).transpose(2, 1, 0, 3).reshape(m // P, P, k))

def kernel(x, bias_table, attn_norm, ffn_norm, final_norm, ab_w_in, ab_lambda_q1, ab_lambda_k1,
           ab_lambda_q2, ab_lambda_k2, ab_subln, ab_sink, ab_w_o, cd_w_in, cd_q_norm, cd_w_q_b,
           cd_kv_norm, cd_w_kv_b, cd_w_o, ffn_w_gate, ffn_w_up, ffn_w_down):
    import concourse.bacc as bacc
    from concourse.bass_utils import run_bass_kernel_spmd

    (x, bias_table, attn_norm, ffn_norm, final_norm, ab_w_in, ab_subln, ab_sink, ab_w_o, cd_w_in, cd_q_norm, cd_w_q_b,
     cd_kv_norm, cd_w_kv_b, cd_w_o, ffn_w_gate, ffn_w_up, ffn_w_down) = map(np.asarray, (
         x, bias_table, attn_norm, ffn_norm, final_norm, ab_w_in, ab_subln, ab_sink, ab_w_o, cd_w_in, cd_q_norm,
         cd_w_q_b, cd_kv_norm, cd_w_kv_b, cd_w_o, ffn_w_gate, ffn_w_up, ffn_w_down))

    ar = np.arange
    o1, o2, o3 = 512, 1024, 1536
    o4, o5 = o3 + 512, o3 + 512 + 128
    cols = [o + h * P + ar(P) for h in range(A_HEADS) for o in (0, o1, o2)]
    cols += [o4 + ar(P), o5 + ar(P)]
    cols += [o3 + np.concatenate([j * HD + ar(HD), (j + 4) * HD + ar(HD)]) for j in range(4)]
    w_ab = panels(ab_w_in[0], np.concatenate(cols))
    rows = np.concatenate([ar(512)] + [512 + np.concatenate([j * HD + ar(HD), (j + 4) * HD + ar(HD)]) for j in range(4)])
    w_o0 = panels(ab_w_o[0][rows])

    cols = [o + (2 * g + p) * P + ar(P) for p in range(2) for g in range(3) for o in (0, 768, 1536)]
    cols += [2304 + c * P + ar(P) for c in range(QC + KVC)]
    kr = 2304 + (QC + KVC) * P + ar(D_ROPE)
    kr_swapped = np.roll(kr, D_ROPE // 2)
    cols += [np.tile(kr, 4), np.tile(kr_swapped, 4)]
    w_c = panels(cd_w_in[0], np.concatenate(cols))
    per = D_NOPE + D_ROPE
    qcols = np.concatenate([h * per + np.concatenate([ar(per), D_NOPE + np.roll(ar(D_ROPE), D_ROPE // 2)])
                            for h in range(D_HEADS)])
    w_d = np.ascontiguousarray(np.concatenate([panels(cd_w_q_b[0], qcols), panels(cd_w_kv_b[0])], axis=2))
    w_o1 = panels(cd_w_o[0])

    arrays = {
        "x_t": np.ascontiguousarray(x[0].T.reshape(KC, P, T).transpose(1, 0, 2)),
        "bias_table": bias_table,
        "one_hot": one_hot_table(),
        "rotary": rotary_tables(),
        "comb_select": comb_select()[0],
        "comb_masks": comb_select()[1],
        "gains": np.ascontiguousarray(np.concatenate(
            [g.reshape(-1, P).T for g in (attn_norm[0], ffn_norm[0], attn_norm[1], ffn_norm[1], final_norm,
                                          cd_q_norm[0], cd_kv_norm[0], ab_subln[0])], axis=1)),
        "sink": ab_sink[0],
        "lambdas": np.concatenate([np.asarray(a)[0] for a in (ab_lambda_q1, ab_lambda_k1, ab_lambda_q2, ab_lambda_k2)]),
        "w_ab": w_ab, "w_o0": w_o0, "w_c": w_c, "w_d": w_d, "w_o1": w_o1,
    }
    for layer in range(2):
        gate, up = panels(ffn_w_gate[layer]), panels(ffn_w_up[layer])
        arrays[f"w_gu{layer}"] = np.ascontiguousarray(np.stack([gate, up], axis=1).reshape(2 * FC, P, DM))
        down = panels(ffn_w_down[layer])
        arrays[f"w_dn{layer}"] = np.ascontiguousarray(
            down.reshape(KC, P, 2, DOWN_HALF * P).transpose(0, 2, 1, 3).reshape(2 * KC, P, DOWN_HALF * P))

    nc = bacc.Bacc("TRN2", target_bir_lowering=False, num_devices=1)
    arrays = {f"in_{n}": a for n, a in arrays.items()}
    io = {n[3:]: nc.dram_tensor(n, a.shape, mybir.dt.from_np(a.dtype), kind="ExternalInput").ap() for n, a in arrays.items()}
    io["out"] = nc.dram_tensor("out", (P, KC, T), F32, kind="ExternalOutput").ap()
    build_program(nc, io)
    r = run_bass_kernel_spmd(nc, [arrays], core_ids=[0])
    out = np.asarray(r.results[0]["out"])
    return np.ascontiguousarray(out.transpose(1, 0, 2).reshape(DM, T).T)[None]
```
